# Optimizing a Trainium2 kernel written in Bass

```python
import math
import jax, jax.numpy as jnp
from jax import lax
import numpy as np

D_MODEL = 1024
BATCH = 1
SEQ = 256
DEPTH = 2

N_MIXERS = 2
N_A_LAYERS = (DEPTH + 1) // 2
N_B_LAYERS = DEPTH // 2

CHUNK = 128
GATE_WIDTH = D_MODEL
GATE_GROUPS = 8
GATE_GROUP_DIM = GATE_WIDTH // GATE_GROUPS

WINDOW_DILATIONS = ((128, 1), (512, 4), (2048, 16))
N_DIL_GROUPS = len(WINDOW_DILATIONS)
ATT_HEADS = 8
HEAD_DIM = 64
ATT_WIDTH = ATT_HEADS * HEAD_DIM

N_BUCKETS = 32
MAX_EXACT = N_BUCKETS // 2
REL_MAX_DISTANCE = max(w for w, _ in WINDOW_DILATIONS)

D_FF = 4 * D_MODEL

EPS = 1e-6
NEG_INF = -1e30


def _rms_norm(x, g):
    xf = x.astype(jnp.float32)
    y = xf * lax.rsqrt(jnp.mean(xf * xf, axis=-1, keepdims=True) + EPS)
    return (y * g.astype(jnp.float32)).astype(x.dtype)

def _layer_norm(x, g, b):
    xf = x.astype(jnp.float32)
    mu = jnp.mean(xf, axis=-1, keepdims=True)
    xc = xf - mu
    y = xc * lax.rsqrt(jnp.mean(xc * xc, axis=-1, keepdims=True) + EPS)
    return (y * g.astype(jnp.float32) + b.astype(jnp.float32)).astype(x.dtype)

def _t5_bucket(distance):
    small = distance < MAX_EXACT
    nf = jnp.maximum(distance, 1).astype(jnp.float32)
    large = MAX_EXACT + (jnp.log(nf / MAX_EXACT) / math.log(REL_MAX_DISTANCE / MAX_EXACT)
                         * (N_BUCKETS - MAX_EXACT)).astype(jnp.int32)
    large = jnp.minimum(large, N_BUCKETS - 1)
    return jnp.where(small, distance, large)

def _chunk_gating_mixer(h, w_in, ln_g, ln_b, w_s, b_s, w_out):
    B_, S_, _ = h.shape
    uv = jax.nn.gelu(h @ w_in, approximate=False)
    u, v = jnp.split(uv, 2, axis=-1)
    v = _layer_norm(v, ln_g, ln_b)
    nc = S_ // CHUNK
    v = v.reshape(B_, nc, CHUNK, GATE_GROUPS, GATE_GROUP_DIM)
    causal = jnp.tril(jnp.ones((CHUNK, CHUNK), dtype=bool))
    w = jnp.where(causal[None], w_s, 0.0)
    mixed = jnp.einsum('gts,bnsgc->bntgc', w, v) + b_s.T[None, None, :, :, None]
    gate = mixed.reshape(B_, S_, GATE_WIDTH)
    return (u * gate) @ w_out

def _dilated_group(q, k, v, bias_table, window, dilation):
    B_, S_, H, hd = q.shape
    blk = window // dilation
    span = blk * dilation
    Sp = -(-S_ // span) * span
    nb = Sp // span

    def split(t):
        t = jnp.pad(t, ((0, 0), (0, Sp - S_), (0, 0), (0, 0)))
        return t.reshape(B_, nb, blk, dilation, H, hd)

    def with_prev(t):
        prev = jnp.pad(t, ((0, 0), (1, 0), (0, 0), (0, 0), (0, 0), (0, 0)))[:, :-1]
        return jnp.concatenate([prev, t], axis=2)

    qb = split(q)
    kc = with_prev(split(k))
    vc = with_prev(split(v))

    s = jnp.einsum('bnqrhc,bnkrhc->bnrhqk', qb, kc) * (HEAD_DIM ** -0.5)
    rel = blk + jnp.arange(blk)[:, None] - jnp.arange(2 * blk)[None, :]
    band = (rel >= 0) & (rel <= blk)
    bucket = _t5_bucket(jnp.clip(rel, 0, blk) * dilation)
    bias = jnp.transpose(bias_table[bucket], (2, 0, 1))
    first = (jnp.arange(nb)[:, None, None] == 0) & (jnp.arange(2 * blk)[None, None, :] < blk)
    valid = band[None] & ~first
    logits = jnp.where(valid[None, :, None, None], s + bias[None, None, None], NEG_INF)

    m = jnp.max(logits, axis=-1)
    p = jnp.exp(logits - m[..., None])
    den = jnp.sum(p, axis=-1)
    num = jnp.einsum('bnrhqk,bnkrhc->bnqrhc', p, vc)

    num = num.reshape(B_, Sp, H, hd)[:, :S_]
    den = jnp.transpose(den, (0, 1, 4, 2, 3)).reshape(B_, Sp, H)[:, :S_]
    m = jnp.transpose(m, (0, 1, 4, 2, 3)).reshape(B_, Sp, H)[:, :S_]
    return num, den, m

def _dilated_attention_mixer(h, w_qkv, w_out, rel_bias):
    B_, S_, _ = h.shape
    qkv = (h @ w_qkv).astype(jnp.float32).reshape(B_, S_, 3, N_DIL_GROUPS, ATT_HEADS, HEAD_DIM)
    rb = rel_bias.astype(jnp.float32)
    nums, dens, maxs = [], [], []
    for g, (window, dil) in enumerate(WINDOW_DILATIONS):
        n_, d_, m_ = _dilated_group(qkv[:, :, 0, g], qkv[:, :, 1, g], qkv[:, :, 2, g],
                                    rb[:, g * ATT_HEADS:(g + 1) * ATT_HEADS], window, dil)
        nums.append(n_)
        dens.append(d_)
        maxs.append(m_)
    m_all = jnp.max(jnp.stack(maxs), axis=0)
    scales = [jnp.exp(m_ - m_all) for m_ in maxs]
    num_sum = sum(n_ * c[..., None] for n_, c in zip(nums, scales))
    den_sum = sum(d_ * c for d_, c in zip(dens, scales))
    o = (num_sum / den_sum[..., None]).astype(h.dtype).reshape(B_, S_, ATT_WIDTH)
    return o @ w_out

def first_inputs(seed: int = 0) -> dict:
    key = jax.random.key(seed)
    ks = jax.random.split(key, 16)
    f32 = jnp.float32
    nrm = lambda k, shape, s: jax.random.normal(k, shape, f32) * s
    qkv_cols = 3 * N_DIL_GROUPS * ATT_HEADS * HEAD_DIM
    return {
        "x": jax.random.normal(ks[0], (BATCH, SEQ, D_MODEL), f32),
        "mix_norm_g": 1.0 + nrm(ks[1], (DEPTH, D_MODEL), 0.05),
        "mlp_norm_g": 1.0 + nrm(ks[2], (DEPTH, D_MODEL), 0.05),
        "final_norm_g": 1.0 + nrm(ks[3], (D_MODEL,), 0.05),
        "a_w_in": nrm(ks[4], (N_A_LAYERS, D_MODEL, 2 * GATE_WIDTH), D_MODEL ** -0.5),
        "a_ln_g": 1.0 + nrm(ks[5], (N_A_LAYERS, GATE_WIDTH), 0.05),
        "a_ln_b": nrm(ks[6], (N_A_LAYERS, GATE_WIDTH), 0.02),
        "a_w_s": nrm(ks[7], (N_A_LAYERS, GATE_GROUPS, CHUNK, CHUNK), CHUNK ** -0.5),
        "a_b_s": 1.0 + nrm(ks[8], (N_A_LAYERS, GATE_GROUPS, CHUNK), 0.1),
        "a_w_out": nrm(ks[9], (N_A_LAYERS, GATE_WIDTH, D_MODEL), GATE_WIDTH ** -0.5),
        "b_w_qkv": nrm(ks[10], (N_B_LAYERS, D_MODEL, qkv_cols), D_MODEL ** -0.5),
        "b_w_out": nrm(ks[11], (N_B_LAYERS, ATT_WIDTH, D_MODEL), ATT_WIDTH ** -0.5),
        "rel_bias": nrm(ks[12], (N_BUCKETS, N_DIL_GROUPS * ATT_HEADS), 0.5),
        "w_up": nrm(ks[13], (DEPTH, D_MODEL, D_FF), D_MODEL ** -0.5),
        "w_down": nrm(ks[14], (DEPTH, D_FF, D_MODEL), D_FF ** -0.5),
    }

def first_block(x, mix_norm_g, mlp_norm_g, final_norm_g, a_w_in, a_ln_g, a_ln_b, a_w_s, a_b_s,
              a_w_out, b_w_qkv, b_w_out, rel_bias, w_up, w_down):
    h = x
    for layer in range(DEPTH):
        y = _rms_norm(h, mix_norm_g[layer])
        j = layer // N_MIXERS
        if layer % N_MIXERS == 0:
            y = _chunk_gating_mixer(y, a_w_in[j], a_ln_g[j], a_ln_b[j], a_w_s[j], a_b_s[j], a_w_out[j])
        else:
            y = _dilated_attention_mixer(y, b_w_qkv[j], b_w_out[j], rel_bias)
        h = h + y
        y = _rms_norm(h, mlp_norm_g[layer])
        h = h + jnp.square(jax.nn.relu(y @ w_up[layer])) @ w_down[layer]
    return _rms_norm(h, final_norm_g)


CHUNK_2 = 64
POOL_WINDOWS = (2, 4, 8, 16)
N_POOL_GROUPS = len(POOL_WINDOWS)
POOL_GROUP_DIM = D_MODEL // N_POOL_GROUPS
CONV_WIDTH = 3
D_FF_2 = ((8 * D_MODEL // 3 + 255) // 256) * 256
N_SUB = 3
N_MOD = 3
RMS_EPS = 1e-6
N_POOL_LAYERS = (DEPTH + 1) // 2
N_CONV_LAYERS = DEPTH // 2


def rms_norm(x, g):
    xf = x.astype(jnp.float32)
    y = xf * lax.rsqrt(jnp.mean(xf * xf, axis=-1, keepdims=True) + RMS_EPS)
    return (y * g.astype(jnp.float32)).astype(x.dtype)

def modulate(h, shift, scale):
    return h * (1 + scale[:, None, :]) + shift[:, None, :]

def swiglu(h, w_in, w_out):
    a, b = jnp.split(h @ w_in, 2, axis=-1)
    return (jax.nn.silu(a) * b) @ w_out

def pool_mixer(h, w_grp, scale):
    B, T, D = h.shape
    hg = h.reshape(B, T, N_POOL_GROUPS, POOL_GROUP_DIM)
    cs = jnp.cumsum(hg.astype(jnp.float32), axis=1)
    pos = jnp.arange(1, T + 1, dtype=jnp.float32)
    pooled = []
    for g, w in enumerate(POOL_WINDOWS):
        csg = cs[:, :, g]
        lag = jnp.pad(csg, ((0, 0), (w, 0), (0, 0)))[:, :T]
        cnt = jnp.minimum(pos, float(w))[None, :, None]
        pooled.append((csg - lag) / cnt)
    pooled = jnp.stack(pooled, axis=2).astype(h.dtype)
    mixed = pooled - hg
    y = jnp.einsum('btgc,gcd->btgd', mixed, w_grp).reshape(B, T, D)
    return y * scale

def conv_mixer(h, w_in, w_conv, w_out):
    D = h.shape[-1]
    b_gate, c_gate, v = jnp.split(h @ w_in, 3, axis=-1)
    u = c_gate * v
    conv = lax.conv_general_dilated(
        u, w_conv[:, None, :].astype(u.dtype),
        window_strides=(1,),
        padding=[(CONV_WIDTH - 1, 0)],
        dimension_numbers=('NWC', 'WIO', 'NWC'),
        feature_group_count=D)
    return (b_gate * conv) @ w_out

def second_inputs(seed: int = 0) -> dict:
    key = jax.random.key(seed)
    ks = jax.random.split(key, 14)
    f32 = jnp.float32
    x = jax.random.normal(ks[0], (BATCH, SEQ, D_MODEL), f32)
    c = jax.random.normal(ks[1], (BATCH, D_MODEL), f32)
    ada_w = jax.random.normal(ks[2], (DEPTH, D_MODEL, N_SUB * N_MOD * D_MODEL), f32) * D_MODEL ** -0.5
    ada_b = 0.01 * jax.random.normal(ks[3], (DEPTH, N_SUB * N_MOD * D_MODEL), f32)
    norm_g = 1.0 + 0.1 * jax.random.normal(ks[4], (DEPTH, N_SUB, D_MODEL), f32)
    ffn_w_in = jax.random.normal(ks[5], (DEPTH, 2, D_MODEL, 2 * D_FF_2), f32) * D_MODEL ** -0.5
    ffn_w_out = jax.random.normal(ks[6], (DEPTH, 2, D_FF_2, D_MODEL), f32) * D_FF_2 ** -0.5
    pool_w = jax.random.normal(ks[7], (N_POOL_LAYERS, N_POOL_GROUPS, POOL_GROUP_DIM, POOL_GROUP_DIM), f32) * POOL_GROUP_DIM ** -0.5
    pool_scale = 1.0 + 0.1 * jax.random.normal(ks[8], (N_POOL_LAYERS, D_MODEL), f32)
    conv_w_in = jax.random.normal(ks[9], (N_CONV_LAYERS, D_MODEL, 3 * D_MODEL), f32) * D_MODEL ** -0.5
    conv_w = jax.random.normal(ks[10], (N_CONV_LAYERS, CONV_WIDTH, D_MODEL), f32) * CONV_WIDTH ** -0.5
    conv_w_out = jax.random.normal(ks[11], (N_CONV_LAYERS, D_MODEL, D_MODEL), f32) * D_MODEL ** -0.5
    final_g = 1.0 + 0.1 * jax.random.normal(ks[12], (D_MODEL,), f32)
    return {"x": x, "c": c, "ada_w": ada_w, "ada_b": ada_b, "norm_g": norm_g,
            "ffn_w_in": ffn_w_in, "ffn_w_out": ffn_w_out,
            "pool_w": pool_w, "pool_scale": pool_scale,
            "conv_w_in": conv_w_in, "conv_w": conv_w, "conv_w_out": conv_w_out,
            "final_g": final_g}

def second_block(x, c, ada_w, ada_b, norm_g, ffn_w_in, ffn_w_out, pool_w, pool_scale,
              conv_w_in, conv_w, conv_w_out, final_g):
    B = x.shape[0]
    cond = jax.nn.silu(c)
    for i in range(DEPTH):
        mod = (cond @ ada_w[i] + ada_b[i]).reshape(B, N_SUB, N_MOD, D_MODEL)
        shift, scale, gate = mod[:, :, 0], mod[:, :, 1], mod[:, :, 2]

        h = modulate(rms_norm(x, norm_g[i, 0]), shift[:, 0], scale[:, 0])
        x = x + 0.5 * gate[:, 0, None, :] * swiglu(h, ffn_w_in[i, 0], ffn_w_out[i, 0])

        h = modulate(rms_norm(x, norm_g[i, 1]), shift[:, 1], scale[:, 1])
        j = i // N_MIXERS
        if i % N_MIXERS == 0:
            y = pool_mixer(h, pool_w[j], pool_scale[j])
        else:
            y = conv_mixer(h, conv_w_in[j], conv_w[j], conv_w_out[j])
        x = x + gate[:, 1, None, :] * y

        h = modulate(rms_norm(x, norm_g[i, 2]), shift[:, 2], scale[:, 2])
        x = x + 0.5 * gate[:, 2, None, :] * swiglu(h, ffn_w_in[i, 1], ffn_w_out[i, 1])
    return rms_norm(x, final_g)


def setup_inputs(seed=0):
    out = dict(first_inputs(seed))
    for name, value in second_inputs(seed + 1).items():
        if name != "x":
            out[name + "_2"] = value
    return out


def reference(
    x, mix_norm_g, mlp_norm_g, final_norm_g, a_w_in, a_ln_g, a_ln_b, a_w_s, a_b_s, a_w_out,
    b_w_qkv, b_w_out, rel_bias, w_up, w_down, c_2, ada_w_2, ada_b_2, norm_g_2, ffn_w_in_2,
    ffn_w_out_2, pool_w_2, pool_scale_2, conv_w_in_2, conv_w_2, conv_w_out_2, final_g_2,
):
    x = first_block(
        x, mix_norm_g, mlp_norm_g, final_norm_g, a_w_in, a_ln_g, a_ln_b, a_w_s, a_b_s, a_w_out,
        b_w_qkv, b_w_out, rel_bias, w_up, w_down,
    )
    return second_block(
        x, c_2, ada_w_2, ada_b_2, norm_g_2, ffn_w_in_2, ffn_w_out_2, pool_w_2, pool_scale_2,
        conv_w_in_2, conv_w_2, conv_w_out_2, final_g_2,
    )


_drawn_inputs = setup_inputs


def setup_inputs(seed=0):
    import zlib

    import numpy as np

    out = dict(_drawn_inputs(seed))
    spreads = {}
    factors = {'a_ln_b': 4.474}
    for name, (base, spread) in spreads.items():
        noise = np.random.default_rng([zlib.crc32(name.encode()), seed]).standard_normal(out[name].shape)
        drawn = base * np.exp(spread * noise) if base else spread * noise
        out[name] = __import__('jax').numpy.asarray(drawn.astype(out[name].dtype))
    for name, factor in factors.items():
        out[name] = (out[name] * factor).astype(out[name].dtype)
    return out
```

```python
from contextlib import ExitStack
import math

import numpy as np
import concourse.bass as bass
from concourse import mybir

ALU = mybir.AluOpType
ACT = mybir.ActivationFunctionType
AX_X = mybir.AxisListType.X
F32 = mybir.dt.float32
F32R = mybir.dt.float32r

P = 128
D = 1024
KT = D // P
TOKENS = 256
TT = TOKENS // P
SLAB = 2048
UPK = 4
UPN = SLAB // UPK
DOWNK = SLAB // D
RING = 3
EPS = 1e-6

D_FF = 4 * D
D_FF_2 = ((8 * D // 3 + 255) // 256) * 256
HALF = UPN // 2
MLP_CHUNKS = D_FF // UPN
FFN_CHUNKS = D_FF_2 // HALF
MLP_BODY = 3

HEADS = 8
HD = 64
WINDOWS = ((128, 1), (512, 4), (2048, 16))
NG = len(WINDOWS)
N_BUCKETS = 32
VLEN = 3 * P
NEG_INF = -1e30

GROUPS = 8
ADA_COLS = 9 * D
ADA_UNITS = ADA_COLS // UPN
POOL_WINDOWS = (2, 4, 8, 16)
PAD = 16
CONV_W = 3

ROWS = {}
for _name, _n in (("mix", 2 * KT), ("mlp", 2 * KT), ("norm", 6 * KT), ("convw", CONV_W * KT), ("bs", GROUPS), ("c", KT)):
    ROWS[_name] = (sum(n for _, n in ROWS.values()), _n)
N_ROWS = sum(n for _, n in ROWS.values())


MLP_BODIES = (MLP_CHUNKS - 2) // MLP_BODY
ADA_AT = {"mlp0": 0, "qkv": MLP_CHUNKS, "mlp1": MLP_CHUNKS + 2, "ffn0": ADA_UNITS, "ffn1": ADA_UNITS + FFN_CHUNKS - 2}
FFN_AT = {"ffn0": 0, "ffn1": 1, "ffn2": 2, "ffn3": 3}


def tr_of(u):
    return 3 * (u // 2) + u % 2


def bucket_masks():
    m = np.zeros((N_BUCKETS + 1, NG, VLEN), np.float32)
    exact = N_BUCKETS // 2
    longest = max(w for w, _ in WINDOWS)
    for g, (window, dil) in enumerate(WINDOWS):
        for i in range(VLEN):
            d = TOKENS - 1 - i
            if d < 0 or d % dil or d // dil > window // dil:
                m[N_BUCKETS, g, i] = NEG_INF
                continue
            b = d if d < exact else min(
                exact + int(math.log(d / exact) / math.log(longest / exact) * (N_BUCKETS - exact)), N_BUCKETS - 1)
            m[b, g, i] = 1.0
    return m


class Phase:

    def __init__(self, slab, up, tr, split, norm):
        self.slab, self.up, self.tr, self.split, self.norm = slab, up, tr, split, norm


def plan():
    mlp = (4 * MLP_CHUNKS, MLP_CHUNKS, 4 * MLP_CHUNKS)
    ffn = (3 * FFN_CHUNKS, FFN_CHUNKS, 2 * FFN_CHUNKS)
    parts = [
        ("setup", 0, 0, 3 + GROUPS, 0, 0),
        ("gate_in", 8, 4, KT, KT, 1),
        ("gate_out", 4, 0, KT, KT, 0),
        ("mlp0", mlp[0], mlp[1], KT + mlp[2], KT + mlp[2], 1),
        ("qkv", 18, 9, KT + 24, KT, 1),
        ("attn", 0, 0, 3 * HEADS, 0, 0),
        ("attn_out", 2, 0, 4, 4, 0),
        ("mlp1", mlp[0], mlp[1], KT + mlp[2], KT + mlp[2], 1),
        ("final1", 0, 0, 0, 0, 1),
        ("ffn0", ffn[0], ffn[1], KT + ffn[2], KT + ffn[2], 1),
        ("pool", 1, 0, KT, 0, 1),
        ("ffn1", ffn[0], ffn[1], KT + ffn[2], KT + ffn[2], 1),
        ("ffn2", ffn[0], ffn[1], KT + ffn[2], KT + ffn[2], 1),
        ("conv_in", 12, 6, KT, KT, 1),
        ("conv_out", 4, 0, 2 * KT, 0, 0),
        ("ffn3", ffn[0], ffn[1], KT + ffn[2], KT + ffn[2], 1),
        ("final2", 0, 0, 0, 0, 1),
    ]
    at, c = {}, [0, 0, 0, 0, 0]
    for name, *n in parts:
        at[name] = Phase(*c)
        c = [a + b for a, b in zip(c, n)]
    at["end"] = Phase(*c)
    return at


def build(nc, x, mix_norm_g, mlp_norm_g, final_norm_g, a_w_in, a_ln_g, a_ln_b, a_w_s, a_b_s, a_w_out,
          b_w_qkv, b_w_out, rel_bias, w_up, w_down, c_2, ada_w_2, ada_b_2, norm_g_2, ffn_w_in_2,
          ffn_w_out_2, pool_w_2, pool_scale_2, conv_w_in_2, conv_w_2, conv_w_out_2, final_g_2,
          masks, bias_rows, out):
    at = plan()
    N_SLABS = at["end"].slab

    ctx = ExitStack()
    with ctx:
        def sb(name, shape, dt=F32):
            return ctx.enter_context(nc.sbuf_tensor(name, shape, dt))

        def sem(name):
            return ctx.enter_context(nc.semaphore(name))

        raw = sb("raw", [P, RING, SLAB])
        w_hi = sb("w_hi", [P, RING, SLAB], F32R)
        w_lo = sb("w_lo", [P, RING, SLAB], F32R)
        ada_raw = sb("ada_raw", [P, 2, SLAB])
        ada_acc = sb("ada_acc", [P, ADA_COLS])
        res = sb("res", [P, TT, D])
        xn = sb("xn", [P, TT, D])
        xT_hi = sb("xT_hi", [P, KT, TOKENS], F32R)
        xT_lo = sb("xT_lo", [P, KT, TOKENS], F32R)
        mid = sb("mid", [P, TT, UPN])
        pre = sb("pre", [P, TT, UPN])
        hT_hi = sb("hT_hi", [P, 4, TOKENS], F32R)
        hT_lo = sb("hT_lo", [P, 4, TOKENS], F32R)
        flip = sb("flip", [P, 2, P])
        ident = flip[:, 1, :]
        ones = sb("ones", [P, P])
        vecT = sb("vecT", [P, N_ROWS])
        adabT = sb("adabT", [P, 2, 72])
        cond = sb("cond", [P, KT])
        sumsq = sb("sumsq", [P, TT])
        msq = sb("msq", [P, TT])
        rstd = sb("rstd", [P, TT])
        neg_half = sb("neg_half", [P, 1])
        mod = sb("mod", [P, 3, 24])
        gain = sb("gain", [P, 3, KT])
        y_tmp = sb("y_tmp", [P, 2, TOKENS])
        den = sb("den", [P, 2 * HEADS])
        rden = sb("rden", [P, 2 * HEADS])
        mx = sb("mx", [P, 2 * HEADS])
        nmx = sb("nmx", [P, 2 * HEADS])
        stats = sb("stats", [P, TT, 2, 6])
        mv = sb("mv", [P, TT, 2])
        region = sb("region", [P, 10752])

        g_u = region[:, 0:2048].rearrange("p (t n) -> p t n", t=TT)
        g_v = region[:, 2048:4096].rearrange("p (t n) -> p t n", t=TT)
        ln_g = region[:, 4096:5120]
        ln_b = region[:, 5120:6144]
        ws_raw = region[:, 6144:7168].rearrange("p (g n) -> p g n", g=GROUPS)
        ws_T = region[:, 7168:8192].rearrange("p (g n) -> p g n", g=GROUPS)
        rows = region[0:N_ROWS, 8192:8320]
        rows_b = region[0:72, 8320:8576].rearrange("p (l n) -> p l n", l=2)
        rel = region[0:N_BUCKETS + 1, 8576:8600]
        mask_sb = region[0:N_BUCKETS + 1, 8600:8600 + NG * VLEN].rearrange("p (g n) -> p g n", g=NG)
        bias_v = region[0:HEADS, 8600:8600 + NG * VLEN]
        qkT = region[:, 0:6144].rearrange("p (f n) -> p f n", f=24)
        v_tok = region[:, 6144:9216].rearrange("p (t n) -> p t n", t=TT)
        bias_t = region[:, 9216:10752].rearrange("p (b g n) -> p b g n", b=2, g=NG)
        gate_B = region[:, 0:3072].rearrange("p (s n) -> p s n", s=3)
        gF = region[:, 4096:5120]
        hp = region[:, 4096:4096 + KT * (PAD + TOKENS)].rearrange("p (k n) -> p k n", k=KT)
        pool_a = region[:, 6272:6272 + 2 * (PAD + TOKENS)].rearrange("p (k n) -> p k n", k=2)
        pool_b = region[:, 6816:6816 + 2 * (PAD + TOKENS)].rearrange("p (k n) -> p k n", k=2)
        ps_B = region[:, 7424:8448]
        b_tok = region[:, 4096:6144].rearrange("p (t n) -> p t n", t=TT)
        uT = region[:, 6144:6144 + KT * (TOKENS + 2)].rearrange("p (k n) -> p k n", k=KT)
        conv = region[:, 8208:8208 + KT * TOKENS].rearrange("p (k n) -> p k n", k=KT)
        rcp = sb("rcp", [P, PAD])
        o_tok = sb("o_tok", [P, TT, HEADS * HD])

        up_ps = ctx.enter_context(nc.psum_tensor("up_ps", [P, TT, UPN], F32))
        acc = ctx.enter_context(nc.psum_tensor("acc", [P, TT, D], F32))
        tr_ps = ctx.enter_context(nc.psum_tensor("tr_ps", [P, 2, 512], F32))

        raw_landed = [sem(f"raw_landed{i}") for i in range(RING)]
        ada_landed = [sem(f"ada_landed{i}") for i in range(2)]
        x_landed, small_landed = sem("x_landed"), sem("small_landed")
        ln_landed, mask_landed = sem("ln_landed"), sem("mask_landed")
        bias_stored = sem("bias_stored")
        bias_landed = [sem(f"bias_landed{i}") for i in range(2)]
        row_landed, gF_landed, ps_landed = sem("row_landed"), sem("gF_landed"), sem("ps_landed")
        ws_landed, o_ready = sem("ws_landed"), sem("o_ready")
        out_stored = sem("out_stored")
        hi_ready, lo_ready, slab_used = sem("hi_ready"), sem("lo_ready"), sem("slab_used")
        ada_step = sem("ada_step")
        consts_ready, ws_masked = sem("consts_ready"), sem("ws_masked")
        up0_ready, acc0_ready = sem("up0_ready"), sem("acc0_ready")
        tr_ready, tr_hi, tr_read = sem("tr_ready"), sem("tr_hi"), sem("tr_read")
        res_ready, sumsq_ready, rstd_ready, xn_ready = (sem("res_ready"), sem("sumsq_ready"), sem("rstd_ready"),
                                                        sem("xn_ready"))
        msq_ready = sem("msq_ready")
        gelu_done, relu_done, mlp_mid = sem("gelu_done"), sem("relu_done"), sem("mlp_mid")
        var_ready, ln_rstd, vn_ready, mix_ready, gated = (sem("var_ready"), sem("ln_rstd"), sem("vn_ready"),
                                                          sem("mix_ready"), sem("gated"))
        cond_ready = sem("cond_ready")
        bias_ps_ready, bias_sb_ready = sem("bias_ps_ready"), sem("bias_sb_ready")
        qkv_copied = sem("qkv_copied")
        score_ready, logit_ready, max_ready, prob_ready = (sem("score_ready"), sem("logit_ready"), sem("max_ready"),
                                                           sem("prob_ready"))
        pv_ready = sem("pv_ready")
        silu_done, ffn_mid = sem("silu_done"), sem("ffn_mid")
        mod_ps_ready, mod_ready = sem("mod_ps_ready"), sem("mod_ready")
        gate_ps_ready, gate_ready = sem("gate_ps_ready"), sem("gate_ready")
        pooled, pool_hi, pool_lo = sem("pooled"), sem("pool_hi"), sem("pool_lo")
        conv_copied, u_ready, conv_y, conv_hi, conv_lo = (sem("conv_copied"), sem("u_ready"), sem("conv_y"),
                                                          sem("conv_hi"), sem("conv_lo"))
        dve_step = sem("dve_step")

        block = ctx.enter_context(nc.Block())

        NORM = {n: at[n].norm for n in ("gate_in", "mlp0", "qkv", "mlp1", "final1", "ffn0", "pool", "ffn1", "ffn2",
                                        "conv_in", "ffn3", "final2")}
        XN = {n: i for i, n in enumerate(n for n in NORM if n != "final1")}
        SUBS = ["ffn0", "pool", "ffn1", "ffn2", "conv_in", "ffn3"]

        up_view = lambda r: r.rearrange("p (k n) -> p k n", k=UPK)
        down_view = lambda r: r.rearrange("p (k n) -> p k n", k=DOWNK)
        ffn_view = lambda r: r.rearrange("p (k h n) -> p k h n", k=UPK, h=2)

        def up_src(w, s, col):
            return w[s * 512:(s + 1) * 512, bass.ds(col, UPN)].rearrange("(k p) n -> p k n", p=P)

        def load_bias(eng, h):
            skew = bass.AP(tensor=bias_rows.tensor, offset=h * NG * VLEN, ap=[[1, P], [VLEN, NG], [1, TOKENS]])
            eng.dma_start(bias_t[:, h % 2], skew).then_inc(bias_landed[h % 2], 16)

        @block.sync
        def _(sp):
            sp.dma_start(res[:, :, :], x.rearrange("b (t p) n -> p (b t) n", p=P)).then_inc(x_landed, 16)
            srcs = {"mix": mix_norm_g.rearrange("l (k p) -> (l k) p", p=P),
                    "mlp": mlp_norm_g.rearrange("l (k p) -> (l k) p", p=P),
                    "norm": norm_g_2.rearrange("l s (k p) -> (l s k) p", p=P),
                    "convw": conv_w_2.rearrange("j w (k p) -> (j w k) p", p=P),
                    "bs": a_b_s[0],
                    "c": c_2.rearrange("b (k p) -> (b k) p", p=P)}
            for name, (r0, n) in ROWS.items():
                sp.dma_start(rows[r0:r0 + n, :], srcs[name]).then_inc(small_landed, 16)
            sp.dma_start(rows_b, ada_b_2.rearrange("l (k p) -> k l p", p=P)).then_inc(small_landed, 16)
            sp.dma_start(ws_raw, a_w_s[0].rearrange("g t s -> t g s")).then_inc(ws_landed, 16)

            def load(g, src, view):
                n = g if isinstance(g, int) else None
                slot = (g if n is not None else g[0]) % RING
                if n is not None:
                    if n >= RING:
                        sp.wait_ge(hi_ready, n - RING + 1)
                        sp.wait_ge(lo_ready, n - RING + 1)
                else:
                    sp.wait_ge(hi_ready, g[1] + (g[0] - RING + 1))
                    sp.wait_ge(lo_ready, g[1] + (g[0] - RING + 1))
                dst = view(raw[:, slot, :])
                for h in range(2):
                    if len(src.shape) == 4:
                        part = (slice(None), slice(None), h)
                    else:
                        k = src.shape[1] // 2
                        part = (slice(None), slice(h * k, (h + 1) * k))
                    sp.dma_start(dst[part], src[part]).then_inc(raw_landed[slot], 16)

            def down_src(w, row):
                return w[bass.ds(row, DOWNK * P), :].rearrange("(k p) n -> p k n", p=P)

            def ffn_src(w, s, col):
                v = w[s * 512:(s + 1) * 512, :].rearrange("(k p) (h n) -> p k h n", p=P, h=2)
                return v[:, :, :, bass.ds(col, HALF)]

            g = at["gate_in"].slab
            for n, chunk in enumerate((2, 3, 0, 1)):
                for s in range(2):
                    load(g, up_src(a_w_in[0], s, chunk * UPN), up_view)
                    g += 1
                if n == 0:
                    sp.dma_start(ln_g, a_ln_g.to_broadcast([P, D])).then_inc(ln_landed, 16)
                    sp.dma_start(ln_b, a_ln_b.to_broadcast([P, D])).then_inc(ln_landed, 16)
                    sp.dma_start(rel[0:N_BUCKETS, :], rel_bias).then_inc(mask_landed, 16)
                    sp.dma_start(mask_sb, masks).then_inc(mask_landed, 16)
            for k in range(4):
                load(g, down_src(a_w_out[0], k * DOWNK * P), down_view)
                g += 1

            def mlp(name, layer):
                g0 = at[name].slab

                def up(g, j):
                    for s in range(2):
                        load(g(s), up_src(w_up[layer], s, j * UPN), up_view)

                def down(g, j):
                    for s in range(2):
                        load(g(s), down_src(w_down[layer], j * UPN + s * DOWNK * P), down_view)

                up(lambda s: g0 + s, 0)
                up(lambda s: g0 + 2 + s, 1)
                down(lambda s: g0 + 4 + s, 0)
                with sp.Fori(0, MLP_BODIES) as i:
                    for b in range(MLP_BODY):
                        j = i * MLP_BODY + (b + 2)
                        up(lambda s: (g0 + 6 + 4 * b + s, i * (4 * MLP_BODY)), j)
                        down(lambda s: (g0 + 8 + 4 * b + s, i * (4 * MLP_BODY)), j - 1)
                down(lambda s: g0 + 4 * MLP_CHUNKS - 2 + s, MLP_CHUNKS - 1)

            sp.wait_ge(bias_sb_ready, 1)
            sp.dma_start(bias_rows.rearrange("(h n) -> h n", h=HEADS), bias_v).then_inc(bias_stored, 16)
            mlp("mlp0", 0)

            g0 = at["qkv"].slab
            with sp.Fori(0, 3) as i:
                for b in range(3):
                    for s in range(2):
                        load((g0 + 2 * b + s, i * 6), up_src(b_w_qkv[0], s, (i * 3 + b) * UPN), up_view)
            sp.wait_ge(bias_stored, 16)
            g = at["attn_out"].slab
            load(g, down_src(b_w_out[0], 0), down_view)
            sp.wait_ge(xn_ready, 2 * XN["qkv"] + 2)
            for h in range(2):
                load_bias(sp, h)
            load(g + 1, down_src(b_w_out[0], DOWNK * P), down_view)

            mlp("mlp1", 1)

            sp.wait_ge(xn_ready, 2 * XN["mlp1"] + 2)
            sp.dma_start(gF, final_norm_g.rearrange("(a n) -> a n", a=1).to_broadcast([P, D])).then_inc(gF_landed, 16)

            def gate_rows(layer):
                if layer:
                    sp.wait_ge(res_ready, 2 * NORM["ffn2"])
                for s in range(3):
                    sp.dma_start(gate_B[:, s, :], ada_b_2[layer:layer + 1, (3 * s + 2) * D:(3 * s + 3) * D]
                                 .to_broadcast([P, D])).then_inc(row_landed, 16)

            def ffn(name, idx, rows_of=None):
                g0 = at[name].slab
                layer, which = divmod(idx, 2)
                w_in, w_out = ffn_w_in_2[layer, which], ffn_w_out_2[layer, which]
                for j in range(2):
                    for s in range(2):
                        load(g0 + 2 * j + s, ffn_src(w_in, s, j * HALF), ffn_view)
                load(g0 + 4, down_src(w_out, 0), down_view)
                if rows_of is not None:
                    gate_rows(rows_of)
                with sp.Fori(0, FFN_CHUNKS - 2) as i:
                    for s in range(2):
                        load((g0 + 5 + s, i * 3), ffn_src(w_in, s, (i + 2) * HALF), ffn_view)
                    load((g0 + 7, i * 3), down_src(w_out, (i + 1) * HALF), down_view)
                load(g0 + 3 * FFN_CHUNKS - 1, down_src(w_out, (FFN_CHUNKS - 1) * HALF), down_view)

            sp.dma_start(ps_B, pool_scale_2.to_broadcast([P, D])).then_inc(ps_landed, 16)
            ffn("ffn0", 0, 0)
            load(at["pool"].slab, pool_w_2[0].rearrange("g (k p) n -> p (g k) n", p=P),
                 lambda r: r.rearrange("p (k n) -> p k n", k=KT))
            ffn("ffn1", 1)
            ffn("ffn2", 2, 1)
            g = at["conv_in"].slab
            for chunk in (2, 3, 4, 5, 0, 1):
                for s in range(2):
                    load(g, up_src(conv_w_in_2[0], s, chunk * UPN), up_view)
                    g += 1
            for k in range(4):
                load(g, down_src(conv_w_out_2[0], k * DOWNK * P), down_view)
                g += 1
            ffn("ffn3", 3)
            sp.dma_start(gF, final_g_2.rearrange("(a n) -> a n", a=1).to_broadcast([P, D])).then_inc(gF_landed, 16)
            for t in range(TT):
                sp.wait_ge(xn_ready, 2 * XN["final2"] + t + 1)
                sp.dma_start(out[0, t * P:(t + 1) * P, :], xn[:, t, :]).then_inc(out_stored, 16)
            sp.wait_ge(out_stored, 16 * TT)

        @block.gpsimd
        def _(pool):
            nc.gpsimd.memset(flip[:, :, :], 0.0).then_inc(consts_ready, 1)
            nc.gpsimd.memset(ones[:, :], 1.0).then_inc(consts_ready, 1)
            nc.gpsimd.memset(neg_half[:, :], -0.5).then_inc(consts_ready, 1)
            for t in range(PAD):
                m = nc.gpsimd.memset(rcp[:, t:t + 1], 1.0 / (t + 1))
            m.then_inc(consts_ready, 1)
            pool.wait_ge(consts_ready, 4)
            nc.gpsimd.memset(rel[N_BUCKETS:N_BUCKETS + 1, :], 1.0).then_inc(consts_ready, 1)
            pool.wait_ge(consts_ready, 5)
            nc.gpsimd.affine_select(out=ident, in_=ident, compare_op=ALU.not_equal, fill=1.0, base=0,
                                    pattern=[[-1, P]], channel_multiplier=1).then_inc(consts_ready, 1)
            nc.gpsimd.affine_select(out=flip[:, 0, :], in_=flip[:, 0, :], compare_op=ALU.not_equal, fill=1.0,
                                    base=1 - P, pattern=[[1, P]], channel_multiplier=1).then_inc(consts_ready, 1)
            pool.wait_ge(ws_landed, 16)
            nc.gpsimd.affine_select(out=ws_raw, in_=ws_raw, compare_op=ALU.is_ge, fill=0.0, base=0,
                                    pattern=[[0, GROUPS], [-1, P]], channel_multiplier=1).then_inc(ws_masked, 1)

            def inverse_root(src, dst, ready):
                nc.gpsimd.tensor_tensor(dst, src, neg_half[:, 0:1], ALU.pow).then_inc(ready, 1)

            def norm(n):
                for t in range(TT):
                    pool.wait_ge(sumsq_ready, 2 * n + t + 1)
                    nc.gpsimd.tensor_scalar(msq[:, t:t + 1], sumsq[:, t:t + 1], 1.0 / D, EPS, ALU.mult, ALU.add)\
                        .then_inc(msq_ready, 1)
                    pool.wait_ge(msq_ready, 2 * n + t + 1 + (TT if n > 0 else 0))
                    inverse_root(msq[:, t:t + 1], rstd[:, t:t + 1], rstd_ready)

            norm(0)
            for t in range(TT):
                pool.wait_ge(var_ready, t + 1)
                nc.gpsimd.tensor_scalar(msq[:, t:t + 1], mv[:, t, 1:2], 1.0, EPS, ALU.mult, ALU.add)\
                    .then_inc(msq_ready, 1)
                pool.wait_ge(msq_ready, TT + t + 1)
                inverse_root(msq[:, t:t + 1], rstd[:, t:t + 1], ln_rstd)
            for n in range(1, len(NORM)):
                norm(n)

        @block.scalar
        def _(act):
            def split_hi(slot, n):
                if isinstance(n, int):
                    if n >= N_SLABS:
                        return
                    act.wait_ge(raw_landed[slot], 32 * (n // RING + 1))
                    if n >= RING:
                        act.wait_ge(slab_used, n - RING + 1)
                else:
                    first, i, per = n
                    act.wait_ge(raw_landed[slot], i * (32 * per // RING) + 32 * (first // RING + 1))
                    act.wait_ge(slab_used, i * per + (first - RING + 1))
                nc.scalar.activation(w_hi[:, slot, :], raw[:, slot, :], ACT.Copy).then_inc(hi_ready, 1)

            def ahead(g, i=None, per=0):
                n = g + RING
                split_hi(n % RING, n if i is None else (n, i, per))

            def plus(i, k, per=1):
                return k if i is None else i * per + k

            def hi_part(dst, tr, i=None, per=0, scale=None, bias=None):
                act.wait_ge(tr_ready, plus(i, tr + 1, per))
                src = tr_ps[:, tr % 2, 0:TOKENS]
                if bias is not None:
                    a = nc.scalar.activation(dst, src, ACT.Identity, bias=bias, scale=scale)
                elif scale is not None:
                    a = nc.scalar.activation(dst, src, ACT.Copy, scale=scale)
                else:
                    a = nc.scalar.activation(dst, src, ACT.Copy)
                a.then_inc(tr_hi, 1)

            def squares(n):
                for t in range(TT):
                    if n == 0:
                        if t == 0:
                            act.wait_ge(x_landed, 16)
                    else:
                        act.wait_ge(res_ready, 2 * (n - 1) + t + 1)
                    nc.scalar.activation(xn[:, t, :], res[:, t, :], ACT.Square,
                                         accum_out=sumsq[:, t:t + 1]).then_inc(sumsq_ready, 1)

            def norm_hi(name, gain_of):
                for k in range(KT):
                    scale, bias = gain_of(k)
                    hi_part(xT_hi[:, k, :], at[name].tr + k, scale=scale, bias=bias)

            def vec(name, k):
                r0 = ROWS[name][0]
                return vecT[:, r0 + k:r0 + k + 1], None

            def load_ada(u, i=None, per=0):
                col = plus(i, (u % ADA_UNITS) * UPN, per * UPN)
                for s in range(2):
                    if u:
                        act.wait_ge(ada_step, plus(i, 8 * u - 4 + 4 * s, 8 * per))
                    act.dma_start(up_view(ada_raw[:, s, :]), up_src(ada_w_2[u // ADA_UNITS], s, col))\
                        .then_inc(ada_landed[s], 16)

            squares(0)
            for n in range(RING):
                split_hi(n, n)
            act.wait_ge(tr_read, 1)
            c0 = ROWS["c"][0]
            nc.scalar.activation(cond[:, :], vecT[:, c0:c0 + KT], ACT.Silu).then_inc(cond_ready, 1)
            norm_hi("gate_in", lambda k: vec("mix", k))
            g = at["gate_in"].slab
            for c in range(4):
                ahead(g)
                dst = (g_v, g_u)[c // 2]
                for t in range(TT):
                    if t == 0:
                        act.wait_ge(up0_ready, c + 1)
                    else:
                        act.wait_ge(slab_used, g + 2)
                    nc.scalar.activation(dst[:, t, (c % 2) * UPN:(c % 2 + 1) * UPN], up_ps[:, t, :], ACT.Gelu)\
                        .then_inc(gelu_done, 1)
                ahead(g + 1)
                g += 2
            for k in range(KT):
                hi_part(xT_hi[:, k, :], at["gate_out"].tr + k)
            for k in range(4):
                if k == 3:
                    squares(NORM["mlp0"])
                ahead(g)
                g += 1

            def mlp(name, vecs):
                p = at[name]
                m0 = 0 if name == "mlp0" else MLP_CHUNKS
                norm_hi(name, vecs)
                tr0 = p.tr + KT
                unit0 = ADA_AT[name]

                def hidden(c, g, i=None, cper=0):
                    for t in range(TT):
                        if t == 0:
                            act.wait_ge(up0_ready, plus(i, p.up + c + 1, cper))
                        else:
                            act.wait_ge(slab_used, plus(i, g + 2, 4 * cper))
                        nc.scalar.activation(pre[:, t, :], up_ps[:, t, :], ACT.Relu).then_inc(relu_done, 1)
                        act.wait_ge(relu_done, plus(i, 2 * (m0 + c) + t + 1, 2 * cper))
                        nc.scalar.activation(mid[:, t, :], pre[:, t, :], ACT.Square).then_inc(mlp_mid, 1)

                def transposed(c, i=None, cper=0):
                    for f in range(4):
                        hi_part(hT_hi[:, f, :], tr0 + 4 * c + f, i, 4 * cper)

                def step(c, g, i=None, cper=0):
                    per = 4 * cper
                    load_ada(unit0 + c, i, cper)
                    ahead(g, i, per)
                    hidden(c, g, i, cper)
                    ahead(g + 1, i, per)
                    ahead(g + 2, i, per)
                    ahead(g + 3, i, per)
                    transposed(c, i, cper)

                g = p.slab
                load_ada(unit0)
                ahead(g)
                hidden(0, g)
                ahead(g + 1)
                transposed(0)
                step(1, g + 2)
                with act.Fori(0, MLP_BODIES) as i:
                    for b in range(MLP_BODY):
                        step(2 + b, g + 6 + 4 * b, i, MLP_BODY)
                g += 4 * MLP_CHUNKS - 2
                ahead(g)
                squares(p.norm + 1)
                ahead(g + 1)

            mlp("mlp0", lambda k: vec("mlp", k))

            p = at["qkv"]
            norm_hi("qkv", lambda k: vec("mix", KT + k))
            stage = [mid, pre, xn]
            with act.Fori(0, 2) as i:
                for b in range(3):
                    g = p.slab + 2 * b
                    ahead(g, i, 6)
                    for t in range(TT):
                        if t == 0:
                            act.wait_ge(up0_ready, i * 3 + (p.up + b + 1))
                        else:
                            act.wait_ge(slab_used, i * 6 + (g + 2))
                        nc.scalar.activation(stage[b][:, t, 0:UPN], up_ps[:, t, :], ACT.Copy).then_inc(qkv_copied, 1)
                    ahead(g + 1, i, 6)
            for b in range(3):
                g = p.slab + 12 + 2 * b
                if b < 2:
                    load_ada(ADA_AT["qkv"] + b)
                ahead(g)
                for t in range(TT):
                    if t == 0:
                        act.wait_ge(up0_ready, p.up + 6 + b + 1)
                    else:
                        act.wait_ge(slab_used, g + 2)
                    act.wait_ge(bias_stored, 16)
                    nc.scalar.activation(v_tok[:, t, b * UPN:(b + 1) * UPN], up_ps[:, t, :], ACT.Copy)\
                        .then_inc(qkv_copied, 1)
                ahead(g + 1)

            p = at["attn"]

            def probs(u):
                t = u % 2
                act.wait_ge(max_ready, 2 * (u + 1))
                pt = xn[:, t, 0:NG * P * (t + 1)]
                nc.scalar.activation(pt, pt, ACT.Exp, bias=nmx[:, u:u + 1], accum_out=den[:, u:u + 1])\
                    .then_inc(prob_ready, 1)
                if t == 1 and u // 2 + 2 < HEADS:
                    load_bias(act, u // 2 + 2)

            def copy_probs(u):
                for a in range(1 + u % 2):
                    tr = p.tr + tr_of(u) + a
                    act.wait_ge(tr_ready, tr + 1)
                    if a == 0 and u >= 2:
                        act.wait_ge(pv_ready, u - 1)
                    nc.scalar.activation((mid, pre)[u % 2][:, :, :].rearrange("p t n -> p (t n)")[:, a * 384:(a + 1) * 384],
                                         tr_ps[:, tr % 2, 0:384], ACT.Copy).then_inc(tr_read, 1)

            for u in range(2 * HEADS):
                probs(u)
                if u >= 1:
                    copy_probs(u - 1)
            copy_probs(2 * HEADS - 1)
            p = at["attn_out"]
            for f in range(4):
                hi_part(hT_hi[:, f, :], p.tr + f)
            ahead(p.slab)
            squares(NORM["mlp1"])
            ahead(p.slab + 1)

            mlp("mlp1", lambda k: vec("mlp", KT + k))
            squares(NORM["ffn0"])

            def affine(sub):
                s = sub % 3
                return lambda k: (gain[:, s, k:k + 1], mod[:, s, k:k + 1])

            def ffn(name, sub):
                p = at[name]
                if sub % 3 == 0:
                    act.wait_ge(mod_ready, sub // 3 + 1)
                norm_hi(name, affine(sub))
                tr0 = p.tr + KT

                def gates(c, g, i=None):
                    for t in range(TT):
                        if t == 0:
                            act.wait_ge(up0_ready, plus(i, p.up + c + 1))
                        else:
                            act.wait_ge(slab_used, plus(i, g + 2, 3))
                        nc.scalar.activation(pre[:, t, 0:HALF], up_ps[:, t, 0:HALF], ACT.Silu).then_inc(silu_done, 1)

                def transposed(c, i=None):
                    for f in range(2):
                        hi_part(hT_hi[:, f, :], tr0 + 2 * c + f, i, 2)

                def step(c, g, i=None):
                    if unit0 is not None and i is not None:
                        load_ada(unit0, i, 1)
                    ahead(g, i, 3)
                    gates(c, g, i)
                    ahead(g + 1, i, 3)
                    ahead(g + 2, i, 3)
                    transposed(c, i)

                unit0 = ADA_AT.get(name)
                g = p.slab
                ahead(g)
                gates(0, g)
                ahead(g + 1)
                transposed(0)
                step(1, g + 2)
                with act.Fori(0, FFN_CHUNKS - 2 - (name == "ffn3")) as i:
                    step(2, g + 5, i)
                if name == "ffn3":
                    step(FFN_CHUNKS - 1, g + 3 * FFN_CHUNKS - 4)
                squares(p.norm + 1)
                ahead(g + 3 * FFN_CHUNKS - 1)

            ffn("ffn0", 0)
            p = at["pool"]
            for q in range(len(POOL_WINDOWS)):
                act.wait_ge(pooled, q + 1)
                nc.scalar.activation(xT_hi[:, 2 * q:2 * q + 2, :], pool_a[:, :, 0:TOKENS], ACT.Copy)\
                    .then_inc(pool_hi, 1)
            squares(p.norm + 1)
            ahead(p.slab)
            ffn("ffn1", 2)
            ffn("ffn2", 3)
            p = at["conv_in"]
            norm_hi("conv_in", affine(4))
            g = p.slab
            for c in range(6):
                ahead(g)
                if c // 2 != 1:
                    dst = xn if c < 2 else b_tok
                    for t in range(TT):
                        if t == 0:
                            act.wait_ge(up0_ready, p.up + c + 1)
                        else:
                            act.wait_ge(slab_used, g + 2)
                        nc.scalar.activation(dst[:, t, (c % 2) * UPN:(c % 2 + 1) * UPN], up_ps[:, t, :], ACT.Copy)\
                            .then_inc(conv_copied, 1)
                ahead(g + 1)
                g += 2
            for k in range(KT):
                act.wait_ge(conv_y, k + 1)
                nc.scalar.activation(xT_hi[:, k, :], conv[:, k, :], ACT.Copy).then_inc(conv_hi, 1)
            for k in range(4):
                if k == 3:
                    squares(NORM["ffn3"])
                ahead(g)
                g += 1
            ffn("ffn3", 5)

        @block.vector
        def _(dve):
            steps = [0]

            def own(ins):
                ins.then_inc(dve_step, 1)
                steps[0] += 1
                dve.wait_ge(dve_step, steps[0])

            def plus(i, k, per=1):
                return k if i is None else i * per + k

            def split_lo(slot, n):
                if isinstance(n, int):
                    if n >= N_SLABS:
                        return
                    dve.wait_ge(hi_ready, n + 1)
                    if n >= RING:
                        dve.wait_ge(slab_used, n - RING + 1)
                else:
                    first, i, per = n
                    dve.wait_ge(hi_ready, i * per + (first + 1))
                    dve.wait_ge(slab_used, i * per + (first - RING + 1))
                nc.vector.tensor_tensor(w_lo[:, slot, :], raw[:, slot, :], w_hi[:, slot, :].bitcast(F32),
                                        ALU.subtract).then_inc(lo_ready, 1)

            def ahead(g, i=None, per=0):
                n = g + RING
                split_lo(n % RING, n if i is None else (n, i, per))

            def lo_part(hi, lo, tr, h, i=None, per=0, scale=None, bias=None):
                dve.wait_ge(tr_hi, plus(i, h + 1, per))
                src = tr_ps[:, tr % 2, 0:TOKENS]
                hi = hi.bitcast(F32)
                if bias is not None:
                    y = y_tmp[:, tr % 2, :]
                    own(nc.vector.tensor_scalar(y, src, scale, bias, ALU.mult, ALU.add))
                    a = nc.vector.tensor_tensor(lo, y, hi, ALU.subtract)
                elif scale is not None:
                    a = nc.vector.scalar_tensor_tensor(out=lo, in0=src, scalar=scale, in1=hi, op0=ALU.mult,
                                                       op1=ALU.subtract)
                else:
                    a = nc.vector.tensor_tensor(lo, src, hi, ALU.subtract)
                a.then_inc(tr_read, 1)

            def norm_lo(name, gain_of):
                p = at[name]
                for k in range(KT):
                    scale, bias = gain_of(k)
                    lo_part(xT_hi[:, k, :], xT_lo[:, k, :], p.tr + k, p.split + k, scale=scale, bias=bias)

            def vec(name, k):
                r0 = ROWS[name][0]
                return vecT[:, r0 + k:r0 + k + 1], None

            def scale_tokens(n):
                for t in range(TT):
                    dve.wait_ge(rstd_ready, 2 * n + t + 1)
                    nc.vector.tensor_scalar(xn[:, t, :], res[:, t, :], rstd[:, t:t + 1], None, ALU.mult)\
                        .then_inc(xn_ready, 1)

            def ada(u, i=None, per=0, first=False):
                col = plus(i, (u % ADA_UNITS) * UPN, per * UPN)
                dst = ada_acc[:, bass.ds(col, UPN)]
                for k in range(KT):
                    s, q = divmod(k, UPK)
                    if q == 0:
                        dve.wait_ge(ada_landed[s], plus(i, 16 * (u + 1), 16 * per))
                    src = ada_raw[:, s, q * UPN:(q + 1) * UPN]
                    if k == 0:
                        a = nc.vector.tensor_scalar(dst, src, cond[:, k:k + 1], None, ALU.mult)
                    else:
                        dve.wait_ge(ada_step, plus(i, 8 * u + k, 8 * per))
                        a = nc.vector.scalar_tensor_tensor(out=dst, in0=src, scalar=cond[:, k:k + 1], in1=dst,
                                                           op0=ALU.mult, op1=ALU.add)
                    a.then_inc(ada_step, 1)

            def residual(g, product, gate=None, sub=None):
                if sub is not None:
                    dve.wait_ge(gate_ready, 3 * (sub // 3 + 1))
                for t in range(TT):
                    if t == 0:
                        dve.wait_ge(acc0_ready, product + 1)
                    else:
                        dve.wait_ge(slab_used, g + 1)
                    src = acc[:, t, :]
                    if gate is not None:
                        own(nc.vector.scalar_tensor_tensor(out=xn[:, t, :], in0=src, scalar=gate, in1=gate_B[:, sub % 3, :],
                                                           op0=ALU.mult, op1=ALU.mult))
                        src = xn[:, t, :]
                    nc.vector.tensor_tensor(res[:, t, :], res[:, t, :], src, ALU.add).then_inc(res_ready, 1)

            for n, dst in ((0, vecT[:, :]), (1, adabT[:, 0, :]), (2, adabT[:, 1, :])):
                dve.wait_ge(tr_ready, n + 1)
                nc.vector.tensor_copy(dst, tr_ps[:, n % 2, 0:dst.shape[1]]).then_inc(tr_read, 1)
            dve.wait_ge(tr_read, 3)
            for n in range(RING):
                split_lo(n, n)
            scale_tokens(0)
            for g in range(GROUPS):
                dve.wait_ge(tr_ready, 3 + g + 1)
                nc.vector.tensor_copy(ws_T[:, g, :], tr_ps[:, (3 + g) % 2, 0:P]).then_inc(tr_read, 1)
            norm_lo("gate_in", lambda k: vec("mix", k))
            g = at["gate_in"].slab
            for c in range(4):
                ahead(g)
                ahead(g + 1)
                if c < 2:
                    for t in range(TT):
                        dve.wait_ge(gelu_done, 2 * c + t + 1)
                        a = nc.vector.bn_stats(out=stats[:, t, c, :], in_=g_v[:, t, c * UPN:(c + 1) * UPN])
                        own(a)
                if c == 1:
                    for t in range(TT):
                        a = nc.vector.bn_aggr(out=mv[:, t, :], in_=stats[:, t, :, :])
                        a.then_inc(var_ready, 1)
                if c == 2:
                    dve.wait_ge(ln_landed, 32)
                    for t in range(TT):
                        dve.wait_ge(ln_rstd, t + 1)
                        own(nc.vector.tensor_scalar(g_v[:, t, :], g_v[:, t, :], mv[:, t, 0:1], rstd[:, t:t + 1],
                                                    ALU.subtract, ALU.mult))
                        own(nc.vector.tensor_tensor(g_v[:, t, :], g_v[:, t, :], ln_g, ALU.mult))
                        nc.vector.tensor_tensor(g_v[:, t, :], g_v[:, t, :], ln_b, ALU.add).then_inc(vn_ready, 1)
                g += 2
            dve.wait_ge(bias_ps_ready, 1)
            nc.vector.tensor_copy(bias_v[:, 0:D], acc[0:HEADS, 0, :])
            nc.vector.tensor_copy(bias_v[:, D:NG * VLEN], acc[0:HEADS, 1, 0:NG * VLEN - D]).then_inc(bias_sb_ready, 1)
            dve.wait_ge(gelu_done, 8)
            b0 = ROWS["bs"][0]
            for t in range(TT):
                dve.wait_ge(mix_ready, t + 1)
                for q in range(GROUPS):
                    cols = slice(q * P, (q + 1) * P)
                    a = nc.vector.scalar_tensor_tensor(out=xn[:, t, cols], in0=acc[:, t, cols],
                                                       scalar=vecT[:, b0 + q:b0 + q + 1], in1=g_u[:, t, cols],
                                                       op0=ALU.add, op1=ALU.mult)
                a.then_inc(gated, 1)
            p = at["gate_out"]
            for k in range(KT):
                lo_part(xT_hi[:, k, :], xT_lo[:, k, :], p.tr + k, p.split + k)
            for k in range(4):
                if k == 3:
                    residual(g, 0)
                ahead(g)
                g += 1
            dve.wait_ge(cond_ready, 1)

            def mlp(name, vecs, product):
                p = at[name]
                unit0 = ADA_AT[name]
                scale_tokens(p.norm)
                norm_lo(name, vecs)
                tr0, h0 = p.tr + KT, p.split + KT

                def transposed(c, i=None, cper=0):
                    for f in range(4):
                        lo_part(hT_hi[:, f, :], hT_lo[:, f, :], tr0 + 4 * c + f, h0 + 4 * c + f, i, 4 * cper)

                g = p.slab
                ahead(g)
                ahead(g + 1)
                transposed(0)
                ada(unit0)

                def step(c, g, i=None, per=0):
                    ahead(g, i, 4 * per)
                    ahead(g + 1, i, 4 * per)
                    ada(unit0 + c, i, per)
                    ahead(g + 2, i, 4 * per)
                    ahead(g + 3, i, 4 * per)
                    transposed(c, i, per)

                step(1, g + 2)
                with dve.Fori(0, MLP_BODIES) as i:
                    for b in range(MLP_BODY):
                        step(2 + b, g + 6 + 4 * b, i, MLP_BODY)
                g += 4 * MLP_CHUNKS - 2
                ahead(g)
                residual(g + 1, product)
                ahead(g + 1)

            mlp("mlp0", lambda k: vec("mlp", k), 1)

            p = at["qkv"]
            scale_tokens(p.norm)
            norm_lo("qkv", lambda k: vec("mix", KT + k))
            tr0 = p.tr + KT
            with dve.Fori(0, 2) as i:
                for b in range(3):
                    g = p.slab + 2 * b
                    ahead(g, i, 6)
                    ahead(g + 1, i, 6)
                    for f in range((0, 4, 8)[b]):
                        tr = tr0 + 4 * (b - 1) + f
                        dve.wait_ge(tr_ready, i * 12 + (tr + 1))
                        nc.vector.tensor_copy(qkT[:, bass.ds(i * 12 + (4 * (b - 1) + f), 1), :],
                                              tr_ps[:, tr % 2:tr % 2 + 1, 0:TOKENS]).then_inc(tr_read, 1)
            for b in range(3):
                g = p.slab + 12 + 2 * b
                ahead(g)
                ahead(g + 1)
                if b < 2:
                    ada(ADA_AT["qkv"] + b)

            def logits(u):
                h, t = divmod(u, 2)
                nk = P * (t + 1)
                dve.wait_ge(score_ready, u + 1)
                if t == 0:
                    dve.wait_ge(bias_landed[h % 2], 16 * (h // 2 + 1))
                if u >= 2:
                    dve.wait_ge(tr_ready, at["attn"].tr + tr_of(u - 1))
                dst = xn[:, t, 0:NG * nk].rearrange("p (g n) -> p g n", g=NG)
                nc.vector.scalar_tensor_tensor(
                    out=dst, in0=acc[:, t, 0:NG * TOKENS].rearrange("p (g n) -> p g n", g=NG)[:, :, 0:nk],
                    scalar=HD ** -0.5, in1=bias_t[:, h % 2, :, TOKENS - nk:TOKENS], op0=ALU.mult,
                    op1=ALU.add).then_inc(logit_ready, 1)
                dve.wait_ge(logit_ready, u + 1)
                nc.vector.tensor_reduce(mx[:, u:u + 1], xn[:, t, 0:NG * nk], AX_X, ALU.max).then_inc(max_ready, 1)
                dve.wait_ge(max_ready, 2 * u + 1)
                nc.vector.tensor_scalar(nmx[:, u:u + 1], mx[:, u:u + 1], -1.0, None, ALU.mult).then_inc(max_ready, 1)

            def attended(u):
                h, t = divmod(u, 2)
                dve.wait_ge(prob_ready, u + 1)
                own(nc.vector.reciprocal(rden[:, u:u + 1], den[:, u:u + 1]))
                dve.wait_ge(pv_ready, u + 1)
                nc.vector.tensor_scalar(o_tok[:, t, h * HD:(h + 1) * HD], up_ps[:, t, h * HD:(h + 1) * HD],
                                        rden[:, u:u + 1], None, ALU.mult).then_inc(o_ready, 1)

            for u in range(2 * HEADS):
                logits(u)
                if u >= 2:
                    attended(u - 2)
            attended(2 * HEADS - 2)
            attended(2 * HEADS - 1)
            p = at["attn_out"]
            for f in range(4):
                lo_part(hT_hi[:, f, :], hT_lo[:, f, :], p.tr + f, p.split + f)
            ahead(p.slab)
            residual(p.slab + 1, 2)
            ahead(p.slab + 1)

            mlp("mlp1", lambda k: vec("mlp", KT + k), 3)

            def final(n, dst, ready):
                for t in range(TT):
                    dve.wait_ge(rstd_ready, 2 * n + t + 1)
                    nc.vector.scalar_tensor_tensor(out=dst[:, t, :], in0=res[:, t, :], scalar=rstd[:, t:t + 1],
                                                   in1=gF, op0=ALU.mult, op1=ALU.mult).then_inc(ready, 1)

            dve.wait_ge(gF_landed, 16)
            final(NORM["final1"], res, res_ready)

            def modulation(layer):
                dve.wait_ge(mod_ps_ready, layer + 1)
                b = adabT[:, layer, :].rearrange("p (s m) -> p s m", s=3)
                own(nc.vector.tensor_tensor(mod[:, :, 0:2 * KT], up_ps[:, 0, 0:72].rearrange("p (s m) -> p s m", s=3)
                                            [:, :, 0:2 * KT], b[:, :, 0:2 * KT], ALU.add))
                r0 = ROWS["norm"][0] + 3 * KT * layer
                nc.vector.scalar_tensor_tensor(out=gain[:, :, :], in0=mod[:, :, KT:2 * KT], scalar=1.0,
                                               in1=vecT[:, r0:r0 + 3 * KT].rearrange("p (s k) -> p s k", s=3),
                                               op0=ALU.add, op1=ALU.mult).then_inc(mod_ready, 1)
                dve.wait_ge(mod_ready, layer + 1)

            def affine(sub):
                s = sub % 3
                return lambda k: (gain[:, s, k:k + 1], mod[:, s, k:k + 1])

            def gate(sub):
                s = sub % 3
                dve.wait_ge(gate_ps_ready, sub + 1)
                dve.wait_ge(row_landed, 48 * (sub // 3 + 1))
                a = nc.vector.tensor_tensor(gate_B[:, s, :], acc[:, s % 2, :], gate_B[:, s, :], ALU.add)
                if SUBS[sub] == "pool":
                    own(a)
                    dve.wait_ge(ps_landed, 16)
                    a = nc.vector.tensor_tensor(gate_B[:, s, :], gate_B[:, s, :], ps_B, ALU.mult)
                a.then_inc(gate_ready, 1)

            def ffn(name, sub, product):
                p = at[name]
                f0 = FFN_AT[name] * FFN_CHUNKS
                unit0 = ADA_AT.get(name)
                scale_tokens(p.norm)
                if sub % 3 == 0:
                    modulation(sub // 3)
                norm_lo(name, affine(sub))
                if sub % 3 == 0:
                    gate(sub)
                    gate(sub + 1)
                tr0, h0 = p.tr + KT, p.split + KT

                def gated_mid(c, i=None):
                    for t in range(TT):
                        dve.wait_ge(silu_done, plus(i, 2 * (f0 + c) + t + 1, 2))
                        nc.vector.tensor_tensor(mid[:, t, 0:HALF], pre[:, t, 0:HALF], up_ps[:, t, HALF:UPN],
                                                ALU.mult).then_inc(ffn_mid, 1)

                def transposed(c, i=None):
                    for f in range(2):
                        lo_part(hT_hi[:, f, :], hT_lo[:, f, :], tr0 + 2 * c + f, h0 + 2 * c + f, i, 2)

                def step(c, g, i=None):
                    ahead(g, i, 3)
                    gated_mid(c, i)
                    ahead(g + 1, i, 3)
                    if unit0 is not None and i is not None:
                        ada(unit0, i, 1)
                    ahead(g + 2, i, 3)
                    transposed(c, i)

                g = p.slab
                ahead(g)
                gated_mid(0)
                ahead(g + 1)
                transposed(0)
                if sub % 3 == 0:
                    gate(sub + 2)
                step(1, g + 2)
                with dve.Fori(0, FFN_CHUNKS - 2 - (name == "ffn3")) as i:
                    step(2, g + 5, i)
                if name == "ffn3":
                    step(FFN_CHUNKS - 1, g + 3 * FFN_CHUNKS - 4)
                g = p.slab + 3 * FFN_CHUNKS - 1
                residual(g, product, 0.5, sub)
                ahead(g)

            ffn("ffn0", 0, 4)

            p = at["pool"]
            scale_tokens(p.norm)
            for k in range(KT):
                scale, bias = affine(1)(k)
                if k == 0:
                    nc.vector.memset(hp[:, :, 0:PAD], 0.0)
                    nc.vector.memset(pool_a[:, :, 0:PAD], 0.0)
                    own(nc.vector.memset(pool_b[:, :, 0:PAD], 0.0))
                dve.wait_ge(tr_ready, p.tr + k + 1)
                nc.vector.tensor_scalar(hp[:, k, PAD:], tr_ps[:, (p.tr + k) % 2, 0:TOKENS], scale, bias, ALU.mult,
                                        ALU.add).then_inc(tr_read, 1)
            dve.wait_ge(tr_read, p.tr + KT)
            W = PAD + TOKENS
            for q, window in enumerate(POOL_WINDOWS):
                h = hp[:, 2 * q:2 * q + 2, :]
                if q:
                    dve.wait_ge(pool_lo, q)
                    own(nc.vector.memset(pool_a[:, :, 0:PAD], 0.0))
                cur, lag = h, 1
                nxt = [pool_a, pool_b]
                if (q + 1) % 2 == 1:
                    nxt = [pool_b, pool_a]
                n = 0
                while lag < window:
                    dst = nxt[n % 2]
                    own(nc.vector.tensor_tensor(dst[:, :, lag:W], cur[:, :, lag:W], cur[:, :, 0:W - lag], ALU.add))
                    cur, lag, n = dst, 2 * lag, n + 1
                assert cur is pool_b
                own(nc.vector.scalar_tensor_tensor(out=pool_a[:, :, 0:TOKENS], in0=cur[:, :, PAD:W],
                                                   scalar=1.0 / window, in1=h[:, :, PAD:W], op0=ALU.mult,
                                                   op1=ALU.subtract))
                for kk in range(2):
                    own(nc.vector.tensor_tensor(pool_a[:, kk, 0:window - 1], cur[:, kk, PAD:PAD + window - 1],
                                                rcp[:, 0:window - 1], ALU.mult))
                nc.vector.tensor_tensor(pool_a[:, :, 0:window - 1], pool_a[:, :, 0:window - 1],
                                        h[:, :, PAD:PAD + window - 1], ALU.subtract).then_inc(pooled, 1)
                dve.wait_ge(pool_hi, q + 1)
                nc.vector.tensor_tensor(xT_lo[:, 2 * q:2 * q + 2, :], pool_a[:, :, 0:TOKENS],
                                        xT_hi[:, 2 * q:2 * q + 2, :].bitcast(F32), ALU.subtract).then_inc(pool_lo, 1)
            residual(p.slab, 5, 1.0, 1)
            ahead(p.slab)

            ffn("ffn1", 2, 6)
            ffn("ffn2", 3, 7)

            p = at["conv_in"]
            scale_tokens(p.norm)
            norm_lo("conv_in", affine(4))
            own(nc.vector.memset(uT[:, :, 0:CONV_W - 1], 0.0))
            g = p.slab
            q = at["conv_out"]
            for c in range(6):
                ahead(g)
                if c // 2 == 1:
                    for t in range(TT):
                        cols = slice((c % 2) * UPN, (c % 2 + 1) * UPN)
                        dve.wait_ge(conv_copied, 4)
                        if t == 0:
                            dve.wait_ge(up0_ready, p.up + c + 1)
                        else:
                            dve.wait_ge(slab_used, g + 2)
                        nc.vector.tensor_tensor(xn[:, t, cols], xn[:, t, cols], up_ps[:, t, :], ALU.mult)\
                            .then_inc(u_ready, 1)
                ahead(g + 1)
                if c == 4:
                    w0 = ROWS["convw"][0]
                    tap = lambda j, k: vecT[:, w0 + KT * j + k:w0 + KT * j + k + 1]
                    for k in range(KT):
                        dve.wait_ge(tr_ready, q.tr + k + 1)
                        own(nc.vector.tensor_copy(uT[:, k, 2:2 + TOKENS], tr_ps[:, (q.tr + k) % 2, 0:TOKENS]))
                        nc.vector.tensor_scalar(conv[:, k, :], uT[:, k, 2:2 + TOKENS], tap(2, k), None, ALU.mult)\
                            .then_inc(tr_read, 1)
                        dve.wait_ge(tr_read, q.tr + k + 1)
                        own(nc.vector.scalar_tensor_tensor(out=conv[:, k, :], in0=uT[:, k, 1:1 + TOKENS],
                                                           scalar=tap(1, k), in1=conv[:, k, :], op0=ALU.mult,
                                                           op1=ALU.add))
                        own(nc.vector.scalar_tensor_tensor(out=conv[:, k, :], in0=uT[:, k, 0:TOKENS],
                                                           scalar=tap(0, k), in1=conv[:, k, :], op0=ALU.mult,
                                                           op1=ALU.add))
                g += 2
            for k in range(KT):
                tr = q.tr + KT + k
                dve.wait_ge(tr_ready, tr + 1)
                nc.vector.tensor_tensor(conv[:, k, :], conv[:, k, :], tr_ps[:, tr % 2, 0:TOKENS], ALU.mult)\
                    .then_inc(conv_y, 1)
                dve.wait_ge(conv_hi, k + 1)
                nc.vector.tensor_tensor(xT_lo[:, k, :], conv[:, k, :], xT_hi[:, k, :].bitcast(F32), ALU.subtract)\
                    .then_inc(tr_read, 1)
            for k in range(4):
                if k == 3:
                    residual(g, 8, 1.0, 4)
                ahead(g)
                g += 1
            ffn("ffn3", 5, 9)
            dve.wait_ge(gF_landed, 32)
            final(NORM["final2"], xn, xn_ready)

        @block.tensor
        def _(pe):
            def plus(i, k, per=1):
                return k if i is None else i * per + k

            def mm(dst, a, b, start=False, stop=False):
                return nc.tensor.matmul(dst, a, b, start=start, stop=stop, skip_group_check=True)

            def up_slab(g, s, i=None, per=0, free=None, xT_first=None, cuses=None):
                slot = g % RING
                pe.wait_ge(lo_ready, plus(i, g + 1, per))
                for t in range(TT):
                    if s == 0 and free is not None:
                        pe.wait_ge(free[0], plus(i, free[1] + t, free[2]))
                    for q in range(UPK):
                        k = s * UPK + q
                        if xT_first is not None and t == 0:
                            pe.wait_ge(tr_read, xT_first + k + 1)
                        a = slice(t * P, (t + 1) * P)
                        b = slice(q * UPN, (q + 1) * UPN)
                        mm(up_ps[:, t, :], xT_hi[:, k, a], w_hi[:, slot, b], start=(k == 0))
                        mm(up_ps[:, t, :], xT_hi[:, k, a], w_lo[:, slot, b])
                        last = mm(up_ps[:, t, :], xT_lo[:, k, a], w_hi[:, slot, b], stop=(k == KT - 1))
                    if s == 1 and t == 0:
                        last.then_inc(up0_ready, 1)
                last.then_inc(slab_used, 1)

            def up_chunk(g, i=None, per=0, free=None, xT_first=None):
                up_slab(g, 0, i, per, free, xT_first)
                up_slab(g + 1, 1, i, per, None, xT_first)

            def down_slab(g, hi, lo, k0, start, stop, i=None, per=0):
                slot = g % RING
                pe.wait_ge(lo_ready, plus(i, g + 1, per))
                for t in range(TT):
                    a = slice(t * P, (t + 1) * P)
                    for q in range(DOWNK):
                        for x_part, w_part in ((hi, w_hi), (hi, w_lo), (lo, w_hi)):
                            for c in range(2):
                                cols = slice(c * 512, (c + 1) * 512)
                                last = mm(acc[:, t, cols], x_part[:, k0 + q, a],
                                          w_part[:, slot, q * D + c * 512:q * D + (c + 1) * 512],
                                          start=start and q == 0 and x_part is hi and w_part is w_hi,
                                          stop=stop and q == DOWNK - 1 and x_part is lo)
                    if stop and t == 0:
                        last.then_inc(acc0_ready, 1)
                last.then_inc(slab_used, 1)

            def transposes(src, f, tr, i=None, per=0, order=None):
                if tr >= 2:
                    pe.wait_ge(tr_read, plus(i, tr - 1, per))
                for t in range(TT):
                    dst, tile = tr_ps[:, tr % 2, t * P:(t + 1) * P], src[:, t, f * P:(f + 1) * P]
                    if order is None:
                        last = nc.tensor.transpose(dst, tile, ident)
                    else:
                        last = mm(dst, tile, order, start=True, stop=True)
                last.then_inc(tr_ready, 1)

            def norm_T(name):
                pe.wait_ge(xn_ready, 2 * XN[name] + 2)
                for k in range(KT):
                    transposes(xn, k, at[name].tr + k)

            pe.wait_ge(consts_ready, 7)
            pe.wait_ge(small_landed, 16 * (len(ROWS) + 1))
            for n, src in ((0, rows), (1, rows_b[:, 0, :]), (2, rows_b[:, 1, :])):
                if n >= 2:
                    pe.wait_ge(tr_read, n - 1)
                w = src.shape[0]
                nc.tensor.transpose(tr_ps[:, n % 2, 0:w], src, ident[0:w, 0:w]).then_inc(tr_ready, 1)
            pe.wait_ge(ws_masked, 1)
            for g in range(GROUPS):
                tr = 3 + g
                pe.wait_ge(tr_read, tr - 1)
                nc.tensor.transpose(tr_ps[:, tr % 2, 0:P], ws_raw[:, g, :], ident).then_inc(tr_ready, 1)

            norm_T("gate_in")
            g = at["gate_in"].slab
            for c in range(4):
                up_chunk(g, free=(gelu_done, 2 * (c - 1) + 1, 0) if c else None,
                         xT_first=at["gate_in"].tr if c == 0 else None)
                g += 2
            pe.wait_ge(mask_landed, 32)
            for n in range(NG):
                for part, (c0, c1) in enumerate(((n * VLEN, (n + 1) * VLEN),)):
                    for b0 in range(0, 3):
                        lo_c, hi_c = max(c0, 512 * b0), min(c1, 512 * (b0 + 1))
                        if lo_c < hi_c:
                            dst = acc[0:HEADS, b0 // 2, (b0 % 2) * 512 + lo_c - 512 * b0:
                                      (b0 % 2) * 512 + hi_c - 512 * b0]
                            last = mm(dst, rel[:, n * HEADS:(n + 1) * HEADS], mask_sb[:, n, lo_c - c0:hi_c - c0],
                                      start=True, stop=True)
            last.then_inc(bias_ps_ready, 1)
            pe.wait_ge(bias_sb_ready, 1)
            for t in range(TT):
                pe.wait_ge(vn_ready, t + 1)
                for q in range(GROUPS):
                    last = mm(acc[:, t, q * P:(q + 1) * P], ws_T[:, q, :], g_v[:, t, q * P:(q + 1) * P],
                              start=True, stop=True)
                last.then_inc(mix_ready, 1)
            pe.wait_ge(gated, 2)
            for k in range(KT):
                transposes(xn, k, at["gate_out"].tr + k)
            for k in range(4):
                pe.wait_ge(tr_read, at["gate_out"].tr + 2 * k + 2)
                down_slab(g, xT_hi, xT_lo, 2 * k, k == 0, k == 3)
                g += 1

            def mlp(name):
                p = at[name]
                m0 = 0 if name == "mlp0" else MLP_CHUNKS
                tr0 = p.tr + KT
                g = p.slab
                norm_T(name)

                def turn(c, i=None, cper=0):
                    for f in range(4):
                        if f == 0:
                            pe.wait_ge(mlp_mid, plus(i, 2 * (m0 + c) + 2, 2 * cper))
                        transposes(mid, f, tr0 + 4 * c + f, i, 4 * cper)

                def down(c, g, start, stop, i=None, cper=0):
                    pe.wait_ge(tr_read, plus(i, tr0 + 4 * c + 4, 4 * cper))
                    for s in range(2):
                        down_slab(g + s, hT_hi, hT_lo, 2 * s, start and s == 0, stop and s == 1, i, 4 * cper)

                def step(c, start, i=None, cper=0):
                    gb = g + 4 * c - 2
                    up_chunk(gb, i, 4 * cper, free=(relu_done, 2 * (m0 + c - 1) + 1, 2 * cper))
                    down(c - 1, gb + 2, start, False, i, cper)
                    turn(c, i, cper)

                up_chunk(g, xT_first=p.tr)
                turn(0)
                step(1, True)
                with pe.Fori(0, MLP_BODIES) as i:
                    for b in range(MLP_BODY):
                        step(2 + b, False, i, MLP_BODY)
                down(MLP_CHUNKS - 1, g + 4 * MLP_CHUNKS - 2, False, True)

            mlp("mlp0")

            p = at["qkv"]
            norm_T("qkv")
            stage = [mid, pre, xn]
            tr0 = p.tr + KT

            def qk_turn(n, c, i=None):
                pe.wait_ge(qkv_copied, plus(i, 2 * n + 2, 6))
                for f in range(4):
                    transposes(stage[c], f, tr0 + 4 * n + f, i, 12, flip[:, bass.ds(i, 1), :])

            pe.wait_ge(tr_read, p.tr + KT)
            with pe.Fori(0, 2) as i:
                for b in range(3):
                    up_chunk(p.slab + 2 * b, i, 6, free=(qkv_copied, 2 * b - 1, 6) if b else None)
                    if b:
                        qk_turn(b - 1, b - 1, i)
                qk_turn(2, 2, i)
            for b in range(3):
                up_chunk(p.slab + 12 + 2 * b, free=(qkv_copied, 2 * (6 + b - 1) + 1, 0))

            p = at["attn"]
            pe.wait_ge(tr_read, p.tr)
            pe.wait_ge(qkv_copied, 18)

            def scores(u):
                h, t = divmod(u, 2)
                rows_h = slice((h % 2) * HD, (h % 2 + 1) * HD)
                if u >= 2:
                    pe.wait_ge(logit_ready, u - 1)
                for n in range(NG):
                    last = mm(acc[:, t, n * TOKENS:n * TOKENS + P * (t + 1)],
                              qkT[rows_h, 4 * n + h // 2, t * P:(t + 1) * P],
                              qkT[rows_h, 12 + 4 * n + h // 2, 0:P * (t + 1)], start=True, stop=True)
                last.then_inc(score_ready, 1)

            def turn_probs(u):
                t = u % 2
                pe.wait_ge(prob_ready, u + 1)
                for a in range(1 + t):
                    tr = p.tr + tr_of(u) + a
                    pe.wait_ge(tr_read, tr - 1)
                    for q in range(3):
                        m = 3 * a + q
                        last = nc.tensor.transpose(tr_ps[:, tr % 2, q * P:(q + 1) * P],
                                                   xn[:, t, m * P:(m + 1) * P], ident)
                    last.then_inc(tr_ready, 1)

            def attend(u):
                h, t = divmod(u, 2)
                pe.wait_ge(tr_read, p.tr + tr_of(u + 1))
                if u >= 2:
                    pe.wait_ge(o_ready, u - 1)
                blocks = [(n, k) for n in range(NG) for k in range(t + 1)]
                src = (mid, pre)[u % 2][:, :, :].rearrange("p t n -> p (t n)")
                for m, (n, k) in enumerate(blocks):
                    last = mm(up_ps[:, t, h * HD:(h + 1) * HD], src[:, m * P:(m + 1) * P],
                              v_tok[:, k, n * UPN + h * HD:n * UPN + (h + 1) * HD],
                              start=(m == 0), stop=(m == len(blocks) - 1))
                last.then_inc(pv_ready, 1)

            scores(0)
            scores(1)
            turn_probs(0)
            for u in range(2 * HEADS):
                if u + 2 < 2 * HEADS:
                    scores(u + 2)
                if u + 1 < 2 * HEADS:
                    turn_probs(u + 1)
                attend(u)
            p = at["attn_out"]
            pe.wait_ge(o_ready, 2 * HEADS)
            for f in range(4):
                transposes(o_tok, f, p.tr + f, order=flip[:, 0, :])
            for s in range(2):
                pe.wait_ge(tr_read, p.tr + 2 * s + 2)
                down_slab(p.slab + s, hT_hi, hT_lo, 2 * s, s == 0, s == 1)

            mlp("mlp1")

            def modulation(layer):
                pe.wait_ge(ada_step, 8 * ADA_UNITS * (layer + 1))
                pe.wait_ge(res_ready, 2 * at[("ffn0", "ffn2")[layer]].norm)
                for s in range(3):
                    for m in range(2 * KT):
                        n = s * 3 * KT + m
                        last = mm(up_ps[:, 0, n:n + 1], ada_acc[:, n * P:(n + 1) * P], ones[:, 0:1],
                                  start=True, stop=True)
                last.then_inc(mod_ps_ready, 1)

            def gate(sub):
                s = sub % 3
                for c in range(2):
                    n = (3 * s + 2) * D + c * 512
                    last = mm(acc[:, s % 2, c * 512:(c + 1) * 512], ones[:, :], ada_acc[:, n:n + 512],
                              start=True, stop=True)
                last.then_inc(gate_ps_ready, 1)

            def ffn(name, sub):
                p = at[name]
                f0 = FFN_AT[name] * FFN_CHUNKS
                tr0 = p.tr + KT
                g = p.slab
                if sub % 3 == 0:
                    modulation(sub // 3)
                    gate(sub)
                    gate(sub + 1)
                norm_T(name)

                def turn(c, i=None):
                    pe.wait_ge(ffn_mid, plus(i, 2 * (f0 + c) + 2, 2))
                    for f in range(2):
                        transposes(mid, f, tr0 + 2 * c + f, i, 2)

                def down(c, g, start, stop, i=None):
                    pe.wait_ge(tr_read, plus(i, tr0 + 2 * c + 2, 2))
                    down_slab(g, hT_hi, hT_lo, 0, start, stop, i, 3)

                up_chunk(g, xT_first=p.tr)
                turn(0)
                if sub % 3 == 0:
                    pe.wait_ge(gate_ready, sub + 1)
                    gate(sub + 2)

                def step(c, g, start, i=None):
                    up_chunk(g, i, 3, free=(ffn_mid, 2 * (f0 + c - 1) + 1, 2))
                    if start and sub % 3 == 0:
                        pe.wait_ge(gate_ready, sub + 3)
                    down(c - 1, g + 2, start, False, i)
                    turn(c, i)

                step(1, g + 2, True)
                with pe.Fori(0, FFN_CHUNKS - 2) as i:
                    step(2, g + 5, False, i)
                down(FFN_CHUNKS - 1, g + 3 * FFN_CHUNKS - 1, False, True)

            ffn("ffn0", 0)
            p = at["pool"]
            norm_T("pool")
            pe.wait_ge(lo_ready, p.slab + 1)
            slot = p.slab % RING
            for t in range(TT):
                for q in range(len(POOL_WINDOWS)):
                    pe.wait_ge(pool_lo, q + 1)
                    for kk in range(2):
                        k = 2 * q + kk
                        for n, (x_part, w_part) in enumerate(((xT_hi, w_hi), (xT_hi, w_lo), (xT_lo, w_hi))):
                            last = mm(acc[:, t, q * 256:(q + 1) * 256], x_part[:, k, t * P:(t + 1) * P],
                                      w_part[:, slot, k * 256:(k + 1) * 256], start=(kk == 0 and n == 0),
                                      stop=(kk == 1 and n == 2))
                if t == 0:
                    last.then_inc(acc0_ready, 1)
            last.then_inc(slab_used, 1)
            ffn("ffn1", 2)
            ffn("ffn2", 3)

            p = at["conv_in"]
            q = at["conv_out"]
            norm_T("conv_in")
            g = p.slab
            free = [None, (conv_copied, 1, 0), (conv_copied, 3, 0), (u_ready, 1, 0), (u_ready, 3, 0), (conv_copied, 5, 0)]
            for c in range(6):
                up_chunk(g, free=free[c], xT_first=p.tr if c == 0 else None)
                g += 2
                if c == 4:
                    for k in range(KT):
                        transposes(xn, k, q.tr + k)
            pe.wait_ge(conv_copied, 8)
            for k in range(KT):
                transposes(b_tok, k, q.tr + KT + k)
            for k in range(4):
                pe.wait_ge(tr_read, q.tr + KT + 2 * k + 2)
                down_slab(g, xT_hi, xT_lo, 2 * k, k == 0, k == 3)
                g += 1
            ffn("ffn3", 5)


_INS = ["x", "mix_norm_g", "mlp_norm_g", "final_norm_g", "a_w_in", "a_ln_g", "a_ln_b", "a_w_s", "a_b_s", "a_w_out",
        "b_w_qkv", "b_w_out", "rel_bias", "w_up", "w_down", "c_2", "ada_w_2", "ada_b_2", "norm_g_2", "ffn_w_in_2",
        "ffn_w_out_2", "pool_w_2", "pool_scale_2", "conv_w_in_2", "conv_w_2", "conv_w_out_2", "final_g_2"]


def kernel(**inputs):
    import concourse.bacc as bacc
    from concourse.bass_utils import run_bass_kernel_spmd

    nc = bacc.Bacc("TRN2", target_bir_lowering=False, num_devices=1, dynamic_dma_scratch_size=64)
    arrays, args = {}, []
    for name in _INS:
        a = np.ascontiguousarray(inputs[name])
        arrays[f"in_{name}"] = a
        args.append(nc.dram_tensor(f"in_{name}", a.shape, mybir.dt.from_np(a.dtype), kind="ExternalInput").ap())
    masks = nc.inline_tensor(bucket_masks(), "bucket_masks").ap()
    bias_rows = nc.dram_tensor("bias_rows", (HEADS * NG * VLEN,), F32).ap()
    out = nc.dram_tensor("out", (1, TOKENS, D), F32, kind="ExternalOutput").ap()
    build(nc, *args, masks, bias_rows, out)
    r = run_bass_kernel_spmd(nc, [arrays], core_ids=[0])
    return r.results[0]["out"]
```

```python
from contextlib import ExitStack
import math

import numpy as np
import concourse.bass as bass
from concourse import mybir

ALU = mybir.AluOpType
ACT = mybir.ActivationFunctionType
AX_X = mybir.AxisListType.X
F32 = mybir.dt.float32
F32R = mybir.dt.float32r

P = 128
D = 1024
KT = D // P
TOKENS = 256
TT = TOKENS // P
SLAB = 2048
UPK = 4
UPN = SLAB // UPK
DOWNK = SLAB // D
RING = 3
FILL = 4
NORM_FILLS = TT * KT // FILL
EPS = 1e-6

D_FF = 4 * D
D_FF_2 = ((8 * D // 3 + 255) // 256) * 256
HALF = UPN // 2
MLP_CHUNKS = D_FF // UPN
FFN_CHUNKS = D_FF_2 // HALF
MLP_BODY = 3

HEADS = 8
HD = 64
WINDOWS = ((128, 1), (512, 4), (2048, 16))
NG = len(WINDOWS)
N_BUCKETS = 32
VLEN = 3 * P
NEG_INF = -1e30

GROUPS = 8
ADA_COLS = 9 * D
ADA_UNITS = ADA_COLS // UPN
POOL_WINDOWS = (2, 4, 8, 16)
PAD = 16
CONV_W = 3

ROWS = {}
for _name, _n in (("mix", 2 * KT), ("mlp", 2 * KT), ("norm", 6 * KT), ("convw", CONV_W * KT), ("bs", GROUPS), ("c", KT)):
    ROWS[_name] = (sum(n for _, n in ROWS.values()), _n)
N_ROWS = sum(n for _, n in ROWS.values())


MLP_BODIES = (MLP_CHUNKS - 2) // MLP_BODY
ADA_AT = {"mlp0": 0, "qkv": MLP_CHUNKS, "mlp1": MLP_CHUNKS + 2, "ffn0": ADA_UNITS, "ffn1": ADA_UNITS + FFN_CHUNKS - 2}
FFN_AT = {"ffn0": 0, "ffn1": 1, "ffn2": 2, "ffn3": 3}


def tr_of(u):
    return 3 * (u // 2) + u % 2


def bucket_masks():
    m = np.zeros((N_BUCKETS + 1, NG, VLEN), np.float32)
    exact = N_BUCKETS // 2
    longest = max(w for w, _ in WINDOWS)
    for g, (window, dil) in enumerate(WINDOWS):
        for i in range(VLEN):
            d = TOKENS - 1 - i
            if d < 0 or d % dil or d // dil > window // dil:
                m[N_BUCKETS, g, i] = NEG_INF
                continue
            b = d if d < exact else min(
                exact + int(math.log(d / exact) / math.log(longest / exact) * (N_BUCKETS - exact)), N_BUCKETS - 1)
            m[b, g, i] = 1.0
    return m


class Phase:

    def __init__(self, slab, up, tr, split, norm):
        self.slab, self.up, self.tr, self.split, self.norm = slab, up, tr, split, norm


def plan():
    mlp = (4 * MLP_CHUNKS, MLP_CHUNKS, NORM_FILLS + TT * MLP_CHUNKS, TT * MLP_CHUNKS, 1)
    ffn = (3 * FFN_CHUNKS, FFN_CHUNKS, NORM_FILLS + TT * FFN_CHUNKS, TT * FFN_CHUNKS, 1)
    parts = [
        ("setup", 0, 0, 3 + GROUPS, 0, 0),
        ("gate_in", 8, 4, NORM_FILLS, 0, 1),
        ("gate_out", 4, 0, NORM_FILLS, NORM_FILLS, 0),
        ("mlp0", *mlp),
        ("qkv", 18, 9, NORM_FILLS + 24, 0, 1),
        ("attn", 0, 0, 3 * HEADS, 0, 0),
        ("attn_out", 2, 0, TT, TT, 0),
        ("mlp1", *mlp),
        ("final1", 0, 0, 0, 0, 1),
        ("ffn0", *ffn),
        ("pool", 1, 0, KT, 0, 1),
        ("ffn1", *ffn),
        ("ffn2", *ffn),
        ("conv_in", 12, 6, NORM_FILLS, 0, 1),
        ("conv_out", 4, 0, 2 * KT, 0, 0),
        ("ffn3", *ffn),
        ("final2", 0, 0, 0, 0, 1),
    ]
    at, c = {}, [0, 0, 0, 0, 0]
    for name, *n in parts:
        at[name] = Phase(*c)
        c = [a + b for a, b in zip(c, n)]
    at["end"] = Phase(*c)
    return at


def build(nc, x, mix_norm_g, mlp_norm_g, final_norm_g, a_w_in, a_ln_g, a_ln_b, a_w_s, a_b_s, a_w_out,
          b_w_qkv, b_w_out, rel_bias, w_up, w_down, c_2, ada_w_2, ada_b_2, norm_g_2, ffn_w_in_2,
          ffn_w_out_2, pool_w_2, pool_scale_2, conv_w_in_2, conv_w_2, conv_w_out_2, final_g_2,
          masks, bias_rows, out):
    at = plan()
    N_SLABS = at["end"].slab

    ctx = ExitStack()
    with ctx:
        def sb(name, shape, dt=F32):
            return ctx.enter_context(nc.sbuf_tensor(name, shape, dt))

        def sem(name):
            return ctx.enter_context(nc.semaphore(name))

        raw = sb("raw", [P, RING, SLAB])
        w_hi = sb("w_hi", [P, RING, SLAB], F32R)
        w_lo = sb("w_lo", [P, RING, SLAB], F32R)
        ada_raw = sb("ada_raw", [P, 2, SLAB])
        ada_acc = sb("ada_acc", [P, ADA_COLS])
        res = sb("res", [P, TT, D])
        xn = sb("xn", [P, TT, D])
        xT_hi = sb("xT_hi", [P, KT, TOKENS], F32R)
        xT_lo = sb("xT_lo", [P, KT, TOKENS], F32R)
        mid = sb("mid", [P, TT, UPN])
        pre = sb("pre", [P, TT, UPN])
        hT_hi = sb("hT_hi", [P, 4, TOKENS], F32R)
        hT_lo = sb("hT_lo", [P, 4, TOKENS], F32R)
        flip = sb("flip", [P, 2, P])
        ident = flip[:, 1, :]
        ones = sb("ones", [P, P])
        vecT = sb("vecT", [P, N_ROWS])
        adabT = sb("adabT", [P, 2, 72])
        cond = sb("cond", [P, KT])
        sumsq = sb("sumsq", [P, TT])
        msq = sb("msq", [P, TT])
        rstd = sb("rstd", [P, TT])
        neg_half = sb("neg_half", [P, 1])
        mod = sb("mod", [P, 3, 24])
        gain = sb("gain", [P, 3, KT])
        den = sb("den", [P, 2 * HEADS])
        rden = sb("rden", [P, 2 * HEADS])
        mx = sb("mx", [P, 2 * HEADS])
        nmx = sb("nmx", [P, 2 * HEADS])
        stats = sb("stats", [P, TT, 2, 6])
        mv = sb("mv", [P, TT, 2])
        region = sb("region", [P, 10752])

        g_u = region[:, 0:2048].rearrange("p (t n) -> p t n", t=TT)
        g_v = region[:, 2048:4096].rearrange("p (t n) -> p t n", t=TT)
        ln_g = region[:, 4096:5120]
        ln_b = region[:, 5120:6144]
        ws_raw = region[:, 6144:7168].rearrange("p (g n) -> p g n", g=GROUPS)
        ws_T = region[:, 7168:8192].rearrange("p (g n) -> p g n", g=GROUPS)
        rows = region[0:N_ROWS, 8192:8320]
        rows_b = region[0:72, 8320:8576].rearrange("p (l n) -> p l n", l=2)
        rel = region[0:N_BUCKETS + 1, 8576:8600]
        mask_sb = region[0:N_BUCKETS + 1, 8600:8600 + NG * VLEN].rearrange("p (g n) -> p g n", g=NG)
        bias_v = region[0:HEADS, 8600:8600 + NG * VLEN]
        qkT = region[:, 0:6144].rearrange("p (f n) -> p f n", f=24)
        v_tok = region[:, 6144:9216].rearrange("p (t n) -> p t n", t=TT)
        bias_t = region[:, 9216:10752].rearrange("p (b g n) -> p b g n", b=2, g=NG)
        gate_B = region[:, 0:3072].rearrange("p (s n) -> p s n", s=3)
        gF = region[:, 4096:5120]
        hp = region[:, 4096:4096 + KT * (PAD + TOKENS)].rearrange("p (k n) -> p k n", k=KT)
        pool_a = region[:, 6272:6272 + 2 * (PAD + TOKENS)].rearrange("p (k n) -> p k n", k=2)
        pool_b = region[:, 6816:6816 + 2 * (PAD + TOKENS)].rearrange("p (k n) -> p k n", k=2)
        ps_B = region[:, 7424:8448]
        b_tok = region[:, 4096:6144].rearrange("p (t n) -> p t n", t=TT)
        uT = region[:, 6144:6144 + KT * (TOKENS + 2)].rearrange("p (k n) -> p k n", k=KT)
        conv = region[:, 8208:8208 + KT * TOKENS].rearrange("p (k n) -> p k n", k=KT)
        rcp = sb("rcp", [P, PAD])
        o_tok = sb("o_tok", [P, TT, HEADS * HD])

        up_ps = ctx.enter_context(nc.psum_tensor("up_ps", [P, TT, UPN], F32))
        acc = ctx.enter_context(nc.psum_tensor("acc", [P, TT, D], F32))
        tr_ps = ctx.enter_context(nc.psum_tensor("tr_ps", [P, 2, 512], F32))

        raw_landed = [sem(f"raw_landed{i}") for i in range(RING)]
        ada_landed = [sem(f"ada_landed{i}") for i in range(2)]
        x_landed, small_landed = sem("x_landed"), sem("small_landed")
        ln_landed, mask_landed = sem("ln_landed"), sem("mask_landed")
        bias_stored = sem("bias_stored")
        bias_landed = [sem(f"bias_landed{i}") for i in range(2)]
        row_landed, gF_landed, ps_landed = sem("row_landed"), sem("gF_landed"), sem("ps_landed")
        ws_landed, o_ready = sem("ws_landed"), sem("o_ready")
        out_stored = sem("out_stored")
        hi_ready, lo_ready, slab_used = sem("hi_ready"), sem("lo_ready"), sem("slab_used")
        ada_step = sem("ada_step")
        consts_ready, ws_masked = sem("consts_ready"), sem("ws_masked")
        up0_ready, acc0_ready = sem("up0_ready"), sem("acc0_ready")
        tr_ready, tr_hi, tr_read = sem("tr_ready"), sem("tr_hi"), sem("tr_read")
        xT_ready = sem("xT_ready")
        res_ready, sumsq_ready, rstd_ready, xn_ready = (sem("res_ready"), sem("sumsq_ready"), sem("rstd_ready"),
                                                        sem("xn_ready"))
        msq_ready = sem("msq_ready")
        gelu_done, relu_done, mlp_mid = sem("gelu_done"), sem("relu_done"), sem("mlp_mid")
        var_ready, ln_rstd, vn_ready, mix_ready, gated = (sem("var_ready"), sem("ln_rstd"), sem("vn_ready"),
                                                          sem("mix_ready"), sem("gated"))
        cond_ready = sem("cond_ready")
        bias_ps_ready, bias_sb_ready = sem("bias_ps_ready"), sem("bias_sb_ready")
        qkv_copied = sem("qkv_copied")
        score_ready, logit_ready, max_ready, prob_ready = (sem("score_ready"), sem("logit_ready"), sem("max_ready"),
                                                           sem("prob_ready"))
        pv_ready = sem("pv_ready")
        silu_done, ffn_mid = sem("silu_done"), sem("ffn_mid")
        mod_ps_ready, mod_ready = sem("mod_ps_ready"), sem("mod_ready")
        gate_ps_ready, gate_ready = sem("gate_ps_ready"), sem("gate_ready")
        pooled, pool_hi, pool_lo = sem("pooled"), sem("pool_hi"), sem("pool_lo")
        conv_copied, u_ready, conv_y, conv_hi, conv_lo = (sem("conv_copied"), sem("u_ready"), sem("conv_y"),
                                                          sem("conv_hi"), sem("conv_lo"))
        dve_step = sem("dve_step")

        block = ctx.enter_context(nc.Block())

        NORM = {n: at[n].norm for n in ("gate_in", "mlp0", "qkv", "mlp1", "final1", "ffn0", "pool", "ffn1", "ffn2",
                                        "conv_in", "ffn3", "final2")}
        XN = {n: i for i, n in enumerate(n for n in NORM if n != "final1")}
        XT = {n: i for i, n in enumerate(n for n in XN if n not in ("pool", "final2"))}
        SUBS = ["ffn0", "pool", "ffn1", "ffn2", "conv_in", "ffn3"]

        up_view = lambda r: r.rearrange("p (k n) -> p k n", k=UPK)
        down_view = lambda r: r.rearrange("p (k n) -> p k n", k=DOWNK)
        ffn_view = lambda r: r.rearrange("p (k h n) -> p k h n", k=UPK, h=2)

        def up_src(w, s, col):
            return w[s * 512:(s + 1) * 512, bass.ds(col, UPN)].rearrange("(k p) n -> p k n", p=P)

        def load_bias(eng, h):
            skew = bass.AP(tensor=bias_rows.tensor, offset=h * NG * VLEN, ap=[[1, P], [VLEN, NG], [1, TOKENS]])
            eng.dma_start(bias_t[:, h % 2], skew).then_inc(bias_landed[h % 2], 16)

        @block.sync
        def _(sp):
            sp.dma_start(res[:, :, :], x.rearrange("b (t p) n -> p (b t) n", p=P)).then_inc(x_landed, 16)
            srcs = {"mix": mix_norm_g.rearrange("l (k p) -> (l k) p", p=P),
                    "mlp": mlp_norm_g.rearrange("l (k p) -> (l k) p", p=P),
                    "norm": norm_g_2.rearrange("l s (k p) -> (l s k) p", p=P),
                    "convw": conv_w_2.rearrange("j w (k p) -> (j w k) p", p=P),
                    "bs": a_b_s[0],
                    "c": c_2.rearrange("b (k p) -> (b k) p", p=P)}
            for name, (r0, n) in ROWS.items():
                sp.dma_start(rows[r0:r0 + n, :], srcs[name]).then_inc(small_landed, 16)
            sp.dma_start(rows_b, ada_b_2.rearrange("l (k p) -> k l p", p=P)).then_inc(small_landed, 16)
            sp.dma_start(ws_raw, a_w_s[0].rearrange("g t s -> t g s")).then_inc(ws_landed, 16)

            def load(g, src, view):
                n = g if isinstance(g, int) else None
                slot = (g if n is not None else g[0]) % RING
                if n is not None:
                    if n >= RING:
                        sp.wait_ge(hi_ready, n - RING + 1)
                        sp.wait_ge(lo_ready, n - RING + 1)
                else:
                    sp.wait_ge(hi_ready, g[1] + (g[0] - RING + 1))
                    sp.wait_ge(lo_ready, g[1] + (g[0] - RING + 1))
                dst = view(raw[:, slot, :])
                for h in range(2):
                    if len(src.shape) == 4:
                        part = (slice(None), slice(None), h)
                    else:
                        k = src.shape[1] // 2
                        part = (slice(None), slice(h * k, (h + 1) * k))
                    sp.dma_start(dst[part], src[part]).then_inc(raw_landed[slot], 16)

            def down_src(w, row):
                return w[bass.ds(row, DOWNK * P), :].rearrange("(k p) n -> p k n", p=P)

            def ffn_src(w, s, col):
                v = w[s * 512:(s + 1) * 512, :].rearrange("(k p) (h n) -> p k h n", p=P, h=2)
                return v[:, :, :, bass.ds(col, HALF)]

            g = at["gate_in"].slab
            for n, chunk in enumerate((2, 3, 0, 1)):
                for s in range(2):
                    load(g, up_src(a_w_in[0], s, chunk * UPN), up_view)
                    g += 1
                if n == 0:
                    sp.dma_start(ln_g, a_ln_g.to_broadcast([P, D])).then_inc(ln_landed, 16)
                    sp.dma_start(ln_b, a_ln_b.to_broadcast([P, D])).then_inc(ln_landed, 16)
                    sp.dma_start(rel[0:N_BUCKETS, :], rel_bias).then_inc(mask_landed, 16)
                    sp.dma_start(mask_sb, masks).then_inc(mask_landed, 16)
            for k in range(4):
                load(g, down_src(a_w_out[0], k * DOWNK * P), down_view)
                g += 1

            def mlp(name, layer):
                g0 = at[name].slab

                def up(g, j):
                    for s in range(2):
                        load(g(s), up_src(w_up[layer], s, j * UPN), up_view)

                def down(g, j):
                    for s in range(2):
                        load(g(s), down_src(w_down[layer], j * UPN + s * DOWNK * P), down_view)

                up(lambda s: g0 + s, 0)
                up(lambda s: g0 + 2 + s, 1)
                down(lambda s: g0 + 4 + s, 0)
                with sp.Fori(0, MLP_BODIES) as i:
                    for b in range(MLP_BODY):
                        j = i * MLP_BODY + (b + 2)
                        up(lambda s: (g0 + 6 + 4 * b + s, i * (4 * MLP_BODY)), j)
                        down(lambda s: (g0 + 8 + 4 * b + s, i * (4 * MLP_BODY)), j - 1)
                down(lambda s: g0 + 4 * MLP_CHUNKS - 2 + s, MLP_CHUNKS - 1)

            sp.wait_ge(bias_sb_ready, 1)
            sp.dma_start(bias_rows.rearrange("(h n) -> h n", h=HEADS), bias_v).then_inc(bias_stored, 16)
            mlp("mlp0", 0)

            g0 = at["qkv"].slab
            with sp.Fori(0, 3) as i:
                for b in range(3):
                    for s in range(2):
                        load((g0 + 2 * b + s, i * 6), up_src(b_w_qkv[0], s, (i * 3 + b) * UPN), up_view)
            sp.wait_ge(bias_stored, 16)
            g = at["attn_out"].slab
            load(g, down_src(b_w_out[0], 0), down_view)
            sp.wait_ge(xn_ready, 2 * XN["qkv"] + 2)
            for h in range(2):
                load_bias(sp, h)
            load(g + 1, down_src(b_w_out[0], DOWNK * P), down_view)

            mlp("mlp1", 1)

            sp.wait_ge(xn_ready, 2 * XN["mlp1"] + 2)
            sp.dma_start(gF, final_norm_g.rearrange("(a n) -> a n", a=1).to_broadcast([P, D])).then_inc(gF_landed, 16)

            def gate_rows(layer):
                if layer:
                    sp.wait_ge(res_ready, 2 * NORM["ffn2"])
                for s in range(3):
                    sp.dma_start(gate_B[:, s, :], ada_b_2[layer:layer + 1, (3 * s + 2) * D:(3 * s + 3) * D]
                                 .to_broadcast([P, D])).then_inc(row_landed, 16)

            def ffn(name, idx, rows_of=None):
                g0 = at[name].slab
                layer, which = divmod(idx, 2)
                w_in, w_out = ffn_w_in_2[layer, which], ffn_w_out_2[layer, which]
                for j in range(2):
                    for s in range(2):
                        load(g0 + 2 * j + s, ffn_src(w_in, s, j * HALF), ffn_view)
                load(g0 + 4, down_src(w_out, 0), down_view)
                if rows_of is not None:
                    gate_rows(rows_of)
                with sp.Fori(0, FFN_CHUNKS - 2) as i:
                    for s in range(2):
                        load((g0 + 5 + s, i * 3), ffn_src(w_in, s, (i + 2) * HALF), ffn_view)
                    load((g0 + 7, i * 3), down_src(w_out, (i + 1) * HALF), down_view)
                load(g0 + 3 * FFN_CHUNKS - 1, down_src(w_out, (FFN_CHUNKS - 1) * HALF), down_view)

            sp.dma_start(ps_B, pool_scale_2.to_broadcast([P, D])).then_inc(ps_landed, 16)
            ffn("ffn0", 0, 0)
            load(at["pool"].slab, pool_w_2[0].rearrange("g (k p) n -> p (g k) n", p=P),
                 lambda r: r.rearrange("p (k n) -> p k n", k=KT))
            ffn("ffn1", 1)
            ffn("ffn2", 2, 1)
            g = at["conv_in"].slab
            for chunk in (2, 3, 4, 5, 0, 1):
                for s in range(2):
                    load(g, up_src(conv_w_in_2[0], s, chunk * UPN), up_view)
                    g += 1
            for k in range(4):
                load(g, down_src(conv_w_out_2[0], k * DOWNK * P), down_view)
                g += 1
            ffn("ffn3", 3)
            sp.dma_start(gF, final_g_2.rearrange("(a n) -> a n", a=1).to_broadcast([P, D])).then_inc(gF_landed, 16)
            for t in range(TT):
                sp.wait_ge(xn_ready, 2 * XN["final2"] + t + 1)
                sp.dma_start(out[0, t * P:(t + 1) * P, :], xn[:, t, :]).then_inc(out_stored, 16)
            sp.wait_ge(out_stored, 16 * TT)

        @block.gpsimd
        def _(pool):
            nc.gpsimd.memset(flip[:, :, :], 0.0).then_inc(consts_ready, 1)
            nc.gpsimd.memset(ones[:, :], 1.0).then_inc(consts_ready, 1)
            nc.gpsimd.memset(neg_half[:, :], -0.5).then_inc(consts_ready, 1)
            for t in range(PAD):
                m = nc.gpsimd.memset(rcp[:, t:t + 1], 1.0 / (t + 1))
            m.then_inc(consts_ready, 1)
            pool.wait_ge(consts_ready, 4)
            nc.gpsimd.memset(rel[N_BUCKETS:N_BUCKETS + 1, :], 1.0).then_inc(consts_ready, 1)
            pool.wait_ge(consts_ready, 5)
            nc.gpsimd.affine_select(out=ident, in_=ident, compare_op=ALU.not_equal, fill=1.0, base=0,
                                    pattern=[[-1, P]], channel_multiplier=1).then_inc(consts_ready, 1)
            nc.gpsimd.affine_select(out=flip[:, 0, :], in_=flip[:, 0, :], compare_op=ALU.not_equal, fill=1.0,
                                    base=1 - P, pattern=[[1, P]], channel_multiplier=1).then_inc(consts_ready, 1)
            pool.wait_ge(ws_landed, 16)
            nc.gpsimd.affine_select(out=ws_raw, in_=ws_raw, compare_op=ALU.is_ge, fill=0.0, base=0,
                                    pattern=[[0, GROUPS], [-1, P]], channel_multiplier=1).then_inc(ws_masked, 1)

            def inverse_root(src, dst, ready):
                nc.gpsimd.tensor_tensor(dst, src, neg_half[:, 0:1], ALU.pow).then_inc(ready, 1)

            def norm(n):
                for t in range(TT):
                    pool.wait_ge(sumsq_ready, 2 * n + t + 1)
                    nc.gpsimd.tensor_scalar(msq[:, t:t + 1], sumsq[:, t:t + 1], 1.0 / D, EPS, ALU.mult, ALU.add)\
                        .then_inc(msq_ready, 1)
                    pool.wait_ge(msq_ready, 2 * n + t + 1 + (TT if n > 0 else 0))
                    inverse_root(msq[:, t:t + 1], rstd[:, t:t + 1], rstd_ready)

            norm(0)
            for t in range(TT):
                pool.wait_ge(var_ready, t + 1)
                nc.gpsimd.tensor_scalar(msq[:, t:t + 1], mv[:, t, 1:2], 1.0, EPS, ALU.mult, ALU.add)\
                    .then_inc(msq_ready, 1)
                pool.wait_ge(msq_ready, TT + t + 1)
                inverse_root(msq[:, t:t + 1], rstd[:, t:t + 1], ln_rstd)
            for n in range(1, len(NORM)):
                norm(n)

        @block.scalar
        def _(act):
            def split_hi(slot, n):
                if isinstance(n, int):
                    if n >= N_SLABS:
                        return
                    act.wait_ge(raw_landed[slot], 32 * (n // RING + 1))
                    if n >= RING:
                        act.wait_ge(slab_used, n - RING + 1)
                else:
                    first, i, per = n
                    act.wait_ge(raw_landed[slot], i * (32 * per // RING) + 32 * (first // RING + 1))
                    act.wait_ge(slab_used, i * per + (first - RING + 1))
                nc.scalar.activation(w_hi[:, slot, :], raw[:, slot, :], ACT.Copy).then_inc(hi_ready, 1)

            def ahead(g, i=None, per=0):
                n = g + RING
                split_hi(n % RING, n if i is None else (n, i, per))

            def plus(i, k, per=1):
                return k if i is None else i * per + k

            def hi_part(dst, tr, i=None, per=0):
                act.wait_ge(tr_ready, plus(i, tr + 1, per))
                src = tr_ps[:, tr % 2, 0:dst.shape[1] * P].rearrange("p (f n) -> p f n", n=P)
                nc.scalar.activation(dst, src, ACT.Copy).then_inc(tr_hi, 1)

            def square(n, t):
                if n:
                    act.wait_ge(res_ready, 2 * (n - 1) + t + 1)
                elif t == 0:
                    act.wait_ge(x_landed, 16)
                nc.scalar.activation(xn[:, t, :], res[:, t, :], ACT.Square,
                                     accum_out=sumsq[:, t:t + 1]).then_inc(sumsq_ready, 1)

            def norm_out(name, t, gain_of):
                for b in range(KT // FILL):
                    fill = at[name].tr + (KT // FILL) * t + b
                    act.wait_ge(tr_ready, fill + 1)
                    for q in range(FILL):
                        k = b * FILL + q
                        scale, bias = gain_of(k)
                        dst, src = xn[:, t, k * P:(k + 1) * P], tr_ps[:, fill % 2, q * P:(q + 1) * P]
                        if bias is None:
                            a = nc.scalar.activation(dst, src, ACT.Copy, scale=scale)
                        else:
                            a = nc.scalar.activation(dst, src, ACT.Identity, bias=bias, scale=scale)
                    a.then_inc(tr_read, 1)

            def enter(name, gain_of, before=(), after=(), layer=None):
                n = NORM[name]
                square(n, 0)
                for g in before:
                    ahead(g)
                if layer is not None:
                    act.wait_ge(mod_ready, layer + 1)
                if gain_of is not None:
                    norm_out(name, 0, gain_of)
                square(n, 1)
                if gain_of is not None:
                    norm_out(name, 1, gain_of)
                for g in after:
                    ahead(g)

            def vec(name, k):
                r0 = ROWS[name][0]
                return vecT[:, r0 + k:r0 + k + 1], None

            def load_ada(u, s, i=None, per=0):
                col = plus(i, (u % ADA_UNITS) * UPN, per * UPN)
                if u:
                    act.wait_ge(ada_step, plus(i, 8 * u - 4 + 4 * s, 8 * per))
                act.dma_start(up_view(ada_raw[:, s, :]), up_src(ada_w_2[u // ADA_UNITS], s, col))\
                    .then_inc(ada_landed[s], 16)

            square(0, 0)
            square(0, 1)
            for n in range(RING):
                split_hi(n, n)
            act.wait_ge(tr_read, 1)
            c0 = ROWS["c"][0]
            nc.scalar.activation(cond[:, :], vecT[:, c0:c0 + KT], ACT.Silu).then_inc(cond_ready, 1)
            for t in range(TT):
                norm_out("gate_in", t, lambda k: vec("mix", k))
            g = at["gate_in"].slab
            for c in range(4):
                ahead(g)
                dst = (g_v, g_u)[c // 2]
                for t in range(TT):
                    if t == 0:
                        act.wait_ge(up0_ready, c + 1)
                    else:
                        act.wait_ge(slab_used, g + 2)
                    nc.scalar.activation(dst[:, t, (c % 2) * UPN:(c % 2 + 1) * UPN], up_ps[:, t, :], ACT.Gelu)\
                        .then_inc(gelu_done, 1)
                ahead(g + 1)
                g += 2
            p = at["gate_out"]
            for n in range(NORM_FILLS):
                t, b = divmod(n, KT // FILL)
                hi_part(xT_hi[:, b * FILL:(b + 1) * FILL, t * P:(t + 1) * P], p.tr + n)
            for k in range(2):
                ahead(p.slab + k)

            def mlp(name):
                p = at[name]
                m0 = 0 if name == "mlp0" else MLP_CHUNKS
                tr0 = p.tr + NORM_FILLS
                unit0 = ADA_AT[name]

                def hidden(c, t, g, i=None, cper=0):
                    if t == 0:
                        act.wait_ge(up0_ready, plus(i, p.up + c + 1, cper))
                    else:
                        act.wait_ge(slab_used, plus(i, g + 2, 4 * cper))
                    nc.scalar.activation(pre[:, t, :], up_ps[:, t, :], ACT.Relu).then_inc(relu_done, 1)
                    act.wait_ge(relu_done, plus(i, 2 * (m0 + c) + t + 1, 2 * cper))
                    nc.scalar.activation(mid[:, t, :], pre[:, t, :], ACT.Square).then_inc(mlp_mid, 1)

                def transposed(c, i=None, cper=0):
                    for t in range(TT):
                        hi_part(hT_hi[:, :, t * P:(t + 1) * P], tr0 + 2 * c + t, i, 2 * cper)

                def step(c, g, i=None, cper=0):
                    per = 4 * cper
                    load_ada(unit0 + c, 0, i, cper)
                    ahead(g, i, per)
                    load_ada(unit0 + c, 1, i, cper)
                    for t in range(TT):
                        hidden(c, t, g, i, cper)
                    ahead(g + 1, i, per)
                    ahead(g + 2, i, per)
                    transposed(c, i, cper)
                    ahead(g + 3, i, per)

                g = p.slab
                for s in range(2):
                    load_ada(unit0, s)
                hidden(0, 0, g)
                ahead(g)
                hidden(0, 1, g)
                ahead(g + 1)
                transposed(0)
                step(1, g + 2)
                with act.Fori(0, MLP_BODIES) as i:
                    for b in range(MLP_BODY):
                        step(2 + b, g + 6 + 4 * b, i, MLP_BODY)

            last = lambda name: at[name].slab - 1
            enter("mlp0", lambda k: vec("mlp", k), [last("mlp0") - 1], [last("mlp0")])
            mlp("mlp0")

            enter("qkv", lambda k: vec("mix", KT + k), [last("qkv") - 1], [last("qkv")])
            p = at["qkv"]
            stage = [mid, pre, xn]
            with act.Fori(0, 2) as i:
                for b in range(3):
                    g = p.slab + 2 * b
                    ahead(g, i, 6)
                    for t in range(TT):
                        if t == 0:
                            act.wait_ge(up0_ready, i * 3 + (p.up + b + 1))
                        else:
                            act.wait_ge(slab_used, i * 6 + (g + 2))
                        nc.scalar.activation(stage[b][:, t, 0:UPN], up_ps[:, t, :], ACT.Copy).then_inc(qkv_copied, 1)
                    ahead(g + 1, i, 6)
            for b in range(3):
                g = p.slab + 12 + 2 * b
                if b < 2:
                    for s in range(2):
                        load_ada(ADA_AT["qkv"] + b, s)
                ahead(g)
                for t in range(TT):
                    if t == 0:
                        act.wait_ge(up0_ready, p.up + 6 + b + 1)
                    else:
                        act.wait_ge(slab_used, g + 2)
                    act.wait_ge(bias_stored, 16)
                    nc.scalar.activation(v_tok[:, t, b * UPN:(b + 1) * UPN], up_ps[:, t, :], ACT.Copy)\
                        .then_inc(qkv_copied, 1)
                ahead(g + 1)

            p = at["attn"]

            def probs(u):
                t = u % 2
                act.wait_ge(max_ready, 2 * (u + 1))
                pt = xn[:, t, 0:NG * P * (t + 1)]
                nc.scalar.activation(pt, pt, ACT.Exp, bias=nmx[:, u:u + 1], accum_out=den[:, u:u + 1])\
                    .then_inc(prob_ready, 1)
                if t == 1 and u // 2 + 2 < HEADS:
                    load_bias(act, u // 2 + 2)

            def copy_probs(u):
                for a in range(1 + u % 2):
                    tr = p.tr + tr_of(u) + a
                    act.wait_ge(tr_ready, tr + 1)
                    if a == 0 and u >= 2:
                        act.wait_ge(pv_ready, u - 1)
                    nc.scalar.activation((mid, pre)[u % 2][:, :, :].rearrange("p t n -> p (t n)")[:, a * 384:(a + 1) * 384],
                                         tr_ps[:, tr % 2, 0:384], ACT.Copy).then_inc(tr_read, 1)

            for u in range(2 * HEADS):
                probs(u)
                if u >= 1:
                    copy_probs(u - 1)
            copy_probs(2 * HEADS - 1)
            p = at["attn_out"]
            for t in range(TT):
                hi_part(hT_hi[:, :, t * P:(t + 1) * P], p.tr + t)
            enter("mlp1", lambda k: vec("mlp", KT + k), [last("mlp1") - 1], [last("mlp1")])
            mlp("mlp1")
            enter("final1", None, [last("ffn0") - 1])

            def affine(sub):
                s = sub % 3
                return lambda k: (gain[:, s, k:k + 1], mod[:, s, k:k + 1])

            def ffn(name):
                p = at[name]
                tr0 = p.tr + NORM_FILLS
                unit0 = ADA_AT.get(name)

                def gates(c, t, g, i=None):
                    if t == 0:
                        act.wait_ge(up0_ready, plus(i, p.up + c + 1))
                    else:
                        act.wait_ge(slab_used, plus(i, g + 2, 3))
                    nc.scalar.activation(pre[:, t, 0:HALF], up_ps[:, t, 0:HALF], ACT.Silu).then_inc(silu_done, 1)

                def transposed(c, i=None, f0=0):
                    for t in range(TT):
                        hi_part(hT_hi[:, f0:f0 + 2, t * P:(t + 1) * P], tr0 + 2 * c + t, i, 2)

                def begin(c, g, i=None):
                    unit = None if unit0 is None or c < 2 else unit0 + c - 2
                    if unit is not None:
                        load_ada(unit, 0, i, 1)
                    ahead(g, i, 3)
                    if unit is not None:
                        load_ada(unit, 1, i, 1)
                    for t in range(TT):
                        gates(c, t, g, i)
                    ahead(g + 1, i, 3)

                def step(c, g, i=None):
                    begin(c, g, i)
                    transposed(c, i)
                    ahead(g + 2, i, 3)

                g = p.slab
                gates(0, 0, g)
                ahead(g)
                gates(0, 1, g)
                ahead(g + 1)
                transposed(0)
                step(1, g + 2)
                with act.Fori(0, FFN_CHUNKS - 3) as i:
                    step(2, g + 5, i)
                begin(FFN_CHUNKS - 1, g + 3 * FFN_CHUNKS - 4)
                transposed(FFN_CHUNKS - 1, f0=2)

            enter("ffn0", affine(0), (), [last("ffn0")], 0)
            ffn("ffn0")
            enter("pool", None, [last("pool") - 1], [last("pool")])
            for q in range(len(POOL_WINDOWS)):
                act.wait_ge(pooled, q + 1)
                nc.scalar.activation(xT_hi[:, 2 * q:2 * q + 2, :], pool_a[:, :, 0:TOKENS], ACT.Copy)\
                    .then_inc(pool_hi, 1)
            enter("ffn1", affine(2), (), [last("ffn1")])
            ffn("ffn1")
            enter("ffn2", affine(3), [last("ffn2") - 1], [last("ffn2")], 1)
            ffn("ffn2")
            enter("conv_in", affine(4), [last("conv_in") - 1], [last("conv_in")])
            p = at["conv_in"]
            g = p.slab
            for c in range(6):
                ahead(g)
                if c // 2 != 1:
                    dst = xn if c < 2 else b_tok
                    for t in range(TT):
                        if t == 0:
                            act.wait_ge(up0_ready, p.up + c + 1)
                        else:
                            act.wait_ge(slab_used, g + 2)
                        nc.scalar.activation(dst[:, t, (c % 2) * UPN:(c % 2 + 1) * UPN], up_ps[:, t, :], ACT.Copy)\
                            .then_inc(conv_copied, 1)
                ahead(g + 1)
                g += 2
            for k in range(KT):
                act.wait_ge(conv_y, k + 1)
                nc.scalar.activation(xT_hi[:, k, :], conv[:, k, :], ACT.Copy).then_inc(conv_hi, 1)
            for k in range(2):
                ahead(g + k)
            enter("ffn3", affine(5), [last("ffn3") - 1], [last("ffn3")])
            ffn("ffn3")
            enter("final2", None)

        @block.vector
        def _(dve):
            steps = [0]

            def own(ins):
                ins.then_inc(dve_step, 1)
                steps[0] += 1
                dve.wait_ge(dve_step, steps[0])

            def plus(i, k, per=1):
                return k if i is None else i * per + k

            def split_lo(slot, n):
                if isinstance(n, int):
                    if n >= N_SLABS:
                        return
                    dve.wait_ge(hi_ready, n + 1)
                    if n >= RING:
                        dve.wait_ge(slab_used, n - RING + 1)
                else:
                    first, i, per = n
                    dve.wait_ge(hi_ready, i * per + (first + 1))
                    dve.wait_ge(slab_used, i * per + (first - RING + 1))
                nc.vector.tensor_tensor(w_lo[:, slot, :], raw[:, slot, :], w_hi[:, slot, :].bitcast(F32),
                                        ALU.subtract).then_inc(lo_ready, 1)

            def ahead(g, i=None, per=0):
                n = g + RING
                split_lo(n % RING, n if i is None else (n, i, per))

            def lo_part(hi, lo, tr, h, i=None, per=0):
                dve.wait_ge(tr_hi, plus(i, h + 1, per))
                src = tr_ps[:, tr % 2, 0:lo.shape[1] * P].rearrange("p (f n) -> p f n", n=P)
                nc.vector.tensor_tensor(lo, src, hi.bitcast(F32), ALU.subtract).then_inc(tr_read, 1)

            def scale_tokens(n, t):
                dve.wait_ge(rstd_ready, 2 * n + t + 1)
                nc.vector.tensor_scalar(xn[:, t, :], res[:, t, :], rstd[:, t:t + 1], None, ALU.mult)\
                    .then_inc(xn_ready, 1)

            def norm_split(name, t):
                for b in range(KT // FILL):
                    dve.wait_ge(tr_read, at[name].tr + (KT // FILL) * t + b + 1)
                    k = slice(b * FILL, (b + 1) * FILL)
                    src = xn[:, t, b * FILL * P:(b + 1) * FILL * P].rearrange("p (k n) -> p k n", n=P)
                    hi, lo = xT_hi[:, k, t * P:(t + 1) * P], xT_lo[:, k, t * P:(t + 1) * P]
                    own(nc.vector.tensor_copy(hi, src))
                    nc.vector.tensor_tensor(lo, src, hi.bitcast(F32), ALU.subtract).then_inc(xT_ready, 1)

            def enter(name, products, before=(), after=(), extra=None):
                for t in range(TT):
                    products(t)
                    if t == 0:
                        scale_tokens(NORM[name], 0)
                if extra is not None:
                    extra()
                if name in XT:
                    norm_split(name, 0)
                for g in before:
                    ahead(g)
                scale_tokens(NORM[name], 1)
                if name in XT:
                    norm_split(name, 1)
                for g in after:
                    ahead(g)

            def ada(u, s, i=None, per=0):
                col = plus(i, (u % ADA_UNITS) * UPN, per * UPN)
                dst = ada_acc[:, bass.ds(col, UPN)]
                dve.wait_ge(ada_landed[s], plus(i, 16 * (u + 1), 16 * per))
                for q in range(UPK):
                    k = s * UPK + q
                    src = ada_raw[:, s, q * UPN:(q + 1) * UPN]
                    if k == 0:
                        a = nc.vector.tensor_scalar(dst, src, cond[:, k:k + 1], None, ALU.mult)
                    else:
                        dve.wait_ge(ada_step, plus(i, 8 * u + k, 8 * per))
                        a = nc.vector.scalar_tensor_tensor(out=dst, in0=src, scalar=cond[:, k:k + 1], in1=dst,
                                                           op0=ALU.mult, op1=ALU.add)
                    a.then_inc(ada_step, 1)

            def residual(g, product, gate=None, sub=None):
                def products(t):
                    if sub is not None and t == 0:
                        dve.wait_ge(gate_ready, 3 * (sub // 3 + 1))
                    if t == 0:
                        dve.wait_ge(acc0_ready, product + 1)
                    else:
                        dve.wait_ge(slab_used, g + 1)
                    src = acc[:, t, :]
                    if gate is not None:
                        own(nc.vector.scalar_tensor_tensor(out=xn[:, t, :], in0=src, scalar=gate,
                                                           in1=gate_B[:, sub % 3, :], op0=ALU.mult, op1=ALU.mult))
                        src = xn[:, t, :]
                    nc.vector.tensor_tensor(res[:, t, :], res[:, t, :], src, ALU.add).then_inc(res_ready, 1)
                return products

            last = lambda name: at[name].slab - 1

            for n, dst in ((0, vecT[:, :]), (1, adabT[:, 0, :]), (2, adabT[:, 1, :])):
                dve.wait_ge(tr_ready, n + 1)
                nc.vector.tensor_copy(dst, tr_ps[:, n % 2, 0:dst.shape[1]]).then_inc(tr_read, 1)
            dve.wait_ge(tr_read, 3)
            for n in range(RING):
                split_lo(n, n)
            for t in range(TT):
                scale_tokens(0, t)
            for g in range(GROUPS):
                dve.wait_ge(tr_ready, 3 + g + 1)
                nc.vector.tensor_copy(ws_T[:, g, :], tr_ps[:, (3 + g) % 2, 0:P]).then_inc(tr_read, 1)
            for t in range(TT):
                norm_split("gate_in", t)
            g = at["gate_in"].slab
            for c in range(4):
                ahead(g)
                ahead(g + 1)
                if c < 2:
                    for t in range(TT):
                        dve.wait_ge(gelu_done, 2 * c + t + 1)
                        a = nc.vector.bn_stats(out=stats[:, t, c, :], in_=g_v[:, t, c * UPN:(c + 1) * UPN])
                        own(a)
                if c == 1:
                    for t in range(TT):
                        a = nc.vector.bn_aggr(out=mv[:, t, :], in_=stats[:, t, :, :])
                        a.then_inc(var_ready, 1)
                if c == 2:
                    dve.wait_ge(ln_landed, 32)
                    for t in range(TT):
                        dve.wait_ge(ln_rstd, t + 1)
                        own(nc.vector.tensor_scalar(g_v[:, t, :], g_v[:, t, :], mv[:, t, 0:1], rstd[:, t:t + 1],
                                                    ALU.subtract, ALU.mult))
                        own(nc.vector.tensor_tensor(g_v[:, t, :], g_v[:, t, :], ln_g, ALU.mult))
                        nc.vector.tensor_tensor(g_v[:, t, :], g_v[:, t, :], ln_b, ALU.add).then_inc(vn_ready, 1)
                g += 2
            dve.wait_ge(bias_ps_ready, 1)
            nc.vector.tensor_copy(bias_v[:, 0:D], acc[0:HEADS, 0, :])
            nc.vector.tensor_copy(bias_v[:, D:NG * VLEN], acc[0:HEADS, 1, 0:NG * VLEN - D]).then_inc(bias_sb_ready, 1)
            dve.wait_ge(gelu_done, 8)
            b0 = ROWS["bs"][0]
            for t in range(TT):
                dve.wait_ge(mix_ready, t + 1)
                for q in range(GROUPS):
                    cols = slice(q * P, (q + 1) * P)
                    a = nc.vector.scalar_tensor_tensor(out=xn[:, t, cols], in0=acc[:, t, cols],
                                                       scalar=vecT[:, b0 + q:b0 + q + 1], in1=g_u[:, t, cols],
                                                       op0=ALU.add, op1=ALU.mult)
                a.then_inc(gated, 1)
            p = at["gate_out"]
            for n in range(NORM_FILLS):
                t, b = divmod(n, KT // FILL)
                tiles = (slice(None), slice(b * FILL, (b + 1) * FILL), slice(t * P, (t + 1) * P))
                lo_part(xT_hi[tiles], xT_lo[tiles], p.tr + n, p.split + n)
            for k in range(2):
                ahead(p.slab + k)
            dve.wait_ge(cond_ready, 1)

            def mlp(name):
                p = at[name]
                unit0 = ADA_AT[name]
                tr0, h0 = p.tr + NORM_FILLS, p.split

                def transposed(c, i=None, cper=0):
                    for t in range(TT):
                        tiles = (slice(None), slice(None), slice(t * P, (t + 1) * P))
                        lo_part(hT_hi[tiles], hT_lo[tiles], tr0 + 2 * c + t, h0 + 2 * c + t, i, 2 * cper)

                g = p.slab
                ahead(g)
                ahead(g + 1)
                transposed(0)
                for s in range(2):
                    ada(unit0, s)

                def step(c, g, i=None, per=0):
                    for s in range(2):
                        ahead(g + s, i, 4 * per)
                        ada(unit0 + c, s, i, per)
                    ahead(g + 2, i, 4 * per)
                    transposed(c, i, per)
                    ahead(g + 3, i, 4 * per)

                step(1, g + 2)
                with dve.Fori(0, MLP_BODIES) as i:
                    for b in range(MLP_BODY):
                        step(2 + b, g + 6 + 4 * b, i, MLP_BODY)

            enter("mlp0", residual(last("mlp0"), 0), [last("mlp0") - 1], [last("mlp0")])
            mlp("mlp0")

            enter("qkv", residual(last("qkv"), 1), [last("qkv") - 1], [last("qkv")])
            p = at["qkv"]
            tr0 = p.tr + NORM_FILLS
            with dve.Fori(0, 2) as i:
                for b in range(3):
                    g = p.slab + 2 * b
                    ahead(g, i, 6)
                    ahead(g + 1, i, 6)
                    for f in range((0, 4, 8)[b]):
                        tr = tr0 + 4 * (b - 1) + f
                        dve.wait_ge(tr_ready, i * 12 + (tr + 1))
                        nc.vector.tensor_copy(qkT[:, bass.ds(i * 12 + (4 * (b - 1) + f), 1), :],
                                              tr_ps[:, tr % 2:tr % 2 + 1, 0:TOKENS]).then_inc(tr_read, 1)
            for b in range(3):
                g = p.slab + 12 + 2 * b
                ahead(g)
                ahead(g + 1)
                if b < 2:
                    for s in range(2):
                        ada(ADA_AT["qkv"] + b, s)

            def logits(u):
                h, t = divmod(u, 2)
                nk = P * (t + 1)
                dve.wait_ge(score_ready, u + 1)
                if t == 0:
                    dve.wait_ge(bias_landed[h % 2], 16 * (h // 2 + 1))
                if u >= 2:
                    dve.wait_ge(tr_ready, at["attn"].tr + tr_of(u - 1))
                dst = xn[:, t, 0:NG * nk].rearrange("p (g n) -> p g n", g=NG)
                nc.vector.scalar_tensor_tensor(
                    out=dst, in0=acc[:, t, 0:NG * TOKENS].rearrange("p (g n) -> p g n", g=NG)[:, :, 0:nk],
                    scalar=HD ** -0.5, in1=bias_t[:, h % 2, :, TOKENS - nk:TOKENS], op0=ALU.mult,
                    op1=ALU.add).then_inc(logit_ready, 1)
                dve.wait_ge(logit_ready, u + 1)
                nc.vector.tensor_reduce(mx[:, u:u + 1], xn[:, t, 0:NG * nk], AX_X, ALU.max).then_inc(max_ready, 1)
                dve.wait_ge(max_ready, 2 * u + 1)
                nc.vector.tensor_scalar(nmx[:, u:u + 1], mx[:, u:u + 1], -1.0, None, ALU.mult).then_inc(max_ready, 1)

            def attended(u):
                h, t = divmod(u, 2)
                dve.wait_ge(prob_ready, u + 1)
                own(nc.vector.reciprocal(rden[:, u:u + 1], den[:, u:u + 1]))
                dve.wait_ge(pv_ready, u + 1)
                nc.vector.tensor_scalar(o_tok[:, t, h * HD:(h + 1) * HD], up_ps[:, t, h * HD:(h + 1) * HD],
                                        rden[:, u:u + 1], None, ALU.mult).then_inc(o_ready, 1)

            for u in range(2 * HEADS):
                logits(u)
                if u >= 2:
                    attended(u - 2)
            attended(2 * HEADS - 2)
            attended(2 * HEADS - 1)
            p = at["attn_out"]
            for t in range(TT):
                tiles = (slice(None), slice(None), slice(t * P, (t + 1) * P))
                lo_part(hT_hi[tiles], hT_lo[tiles], p.tr + t, p.split + t)
            enter("mlp1", residual(last("mlp1"), 2), [last("mlp1") - 1], [last("mlp1")])
            mlp("mlp1")

            def final(name, dst, t, ready):
                dve.wait_ge(rstd_ready, 2 * NORM[name] + t + 1)
                nc.vector.scalar_tensor_tensor(out=dst[:, t, :], in0=res[:, t, :], scalar=rstd[:, t:t + 1],
                                               in1=gF, op0=ALU.mult, op1=ALU.mult).then_inc(ready, 1)

            products = residual(last("ffn0"), 3)
            for t in range(TT):
                products(t)
            dve.wait_ge(gF_landed, 16)
            ahead(last("ffn0") - 1)

            def modulation(layer):
                dve.wait_ge(mod_ps_ready, layer + 1)
                b = adabT[:, layer, :].rearrange("p (s m) -> p s m", s=3)
                own(nc.vector.tensor_tensor(mod[:, :, 0:2 * KT], up_ps[:, 0, 0:72].rearrange("p (s m) -> p s m", s=3)
                                            [:, :, 0:2 * KT], b[:, :, 0:2 * KT], ALU.add))
                r0 = ROWS["norm"][0] + 3 * KT * layer
                nc.vector.scalar_tensor_tensor(out=gain[:, :, :], in0=mod[:, :, KT:2 * KT], scalar=1.0,
                                               in1=vecT[:, r0:r0 + 3 * KT].rearrange("p (s k) -> p s k", s=3),
                                               op0=ALU.add, op1=ALU.mult).then_inc(mod_ready, 1)
                dve.wait_ge(mod_ready, layer + 1)

            def affine(sub):
                s = sub % 3
                return lambda k: (gain[:, s, k:k + 1], mod[:, s, k:k + 1])

            def gate(sub):
                s = sub % 3
                dve.wait_ge(gate_ps_ready, sub + 1)
                dve.wait_ge(row_landed, 48 * (sub // 3 + 1))
                a = nc.vector.tensor_tensor(gate_B[:, s, :], acc[:, s % 2, :], gate_B[:, s, :], ALU.add)
                if SUBS[sub] == "pool":
                    own(a)
                    dve.wait_ge(ps_landed, 16)
                    a = nc.vector.tensor_tensor(gate_B[:, s, :], gate_B[:, s, :], ps_B, ALU.mult)
                a.then_inc(gate_ready, 1)

            def ffn(name, sub):
                p = at[name]
                f0 = FFN_AT[name] * FFN_CHUNKS
                unit0 = ADA_AT.get(name)
                if sub % 3 == 0:
                    gate(sub)
                    gate(sub + 1)
                tr0, h0 = p.tr + NORM_FILLS, p.split

                def gated_mid(c, i=None):
                    for t in range(TT):
                        dve.wait_ge(silu_done, plus(i, 2 * (f0 + c) + t + 1, 2))
                        nc.vector.tensor_tensor(mid[:, t, 0:HALF], pre[:, t, 0:HALF], up_ps[:, t, HALF:UPN],
                                                ALU.mult).then_inc(ffn_mid, 1)

                def transposed(c, i=None, f=0):
                    for t in range(TT):
                        tiles = (slice(None), slice(f, f + 2), slice(t * P, (t + 1) * P))
                        lo_part(hT_hi[tiles], hT_lo[tiles], tr0 + 2 * c + t, h0 + 2 * c + t, i, 2)

                def begin(c, g, i=None):
                    ahead(g, i, 3)
                    if unit0 is not None and c >= 2:
                        ada(unit0 + c - 2, 0, i, 1)
                    gated_mid(c, i)
                    ahead(g + 1, i, 3)

                def rest(c, i=None):
                    if unit0 is not None and c >= 2:
                        ada(unit0 + c - 2, 1, i, 1)

                def step(c, g, i=None):
                    begin(c, g, i)
                    transposed(c, i)
                    rest(c, i)
                    ahead(g + 2, i, 3)

                g = p.slab
                ahead(g)
                gated_mid(0)
                ahead(g + 1)
                transposed(0)
                if sub % 3 == 0:
                    gate(sub + 2)
                step(1, g + 2)
                with dve.Fori(0, FFN_CHUNKS - 3) as i:
                    step(2, g + 5, i)
                begin(FFN_CHUNKS - 1, g + 3 * FFN_CHUNKS - 4)
                transposed(FFN_CHUNKS - 1, f=2)
                rest(FFN_CHUNKS - 1)

            enter("ffn0", lambda t: final("final1", res, t, res_ready), (), [last("ffn0")], lambda: modulation(0))
            ffn("ffn0", 0)

            enter("pool", residual(last("pool"), 4, 0.5, 0), [last("pool") - 1], [last("pool")])
            p = at["pool"]
            for k in range(KT):
                scale, bias = affine(1)(k)
                if k == 0:
                    nc.vector.memset(hp[:, :, 0:PAD], 0.0)
                    nc.vector.memset(pool_a[:, :, 0:PAD], 0.0)
                    own(nc.vector.memset(pool_b[:, :, 0:PAD], 0.0))
                dve.wait_ge(tr_ready, p.tr + k + 1)
                nc.vector.tensor_scalar(hp[:, k, PAD:], tr_ps[:, (p.tr + k) % 2, 0:TOKENS], scale, bias, ALU.mult,
                                        ALU.add).then_inc(tr_read, 1)
            dve.wait_ge(tr_read, p.tr + KT)
            W = PAD + TOKENS
            for q, window in enumerate(POOL_WINDOWS):
                h = hp[:, 2 * q:2 * q + 2, :]
                if q:
                    dve.wait_ge(pool_lo, q)
                    own(nc.vector.memset(pool_a[:, :, 0:PAD], 0.0))
                cur, lag = h, 1
                nxt = [pool_a, pool_b]
                if (q + 1) % 2 == 1:
                    nxt = [pool_b, pool_a]
                n = 0
                while lag < window:
                    dst = nxt[n % 2]
                    own(nc.vector.tensor_tensor(dst[:, :, lag:W], cur[:, :, lag:W], cur[:, :, 0:W - lag], ALU.add))
                    cur, lag, n = dst, 2 * lag, n + 1
                assert cur is pool_b
                own(nc.vector.scalar_tensor_tensor(out=pool_a[:, :, 0:TOKENS], in0=cur[:, :, PAD:W],
                                                   scalar=1.0 / window, in1=h[:, :, PAD:W], op0=ALU.mult,
                                                   op1=ALU.subtract))
                for kk in range(2):
                    own(nc.vector.tensor_tensor(pool_a[:, kk, 0:window - 1], cur[:, kk, PAD:PAD + window - 1],
                                                rcp[:, 0:window - 1], ALU.mult))
                nc.vector.tensor_tensor(pool_a[:, :, 0:window - 1], pool_a[:, :, 0:window - 1],
                                        h[:, :, PAD:PAD + window - 1], ALU.subtract).then_inc(pooled, 1)
                dve.wait_ge(pool_hi, q + 1)
                nc.vector.tensor_tensor(xT_lo[:, 2 * q:2 * q + 2, :], pool_a[:, :, 0:TOKENS],
                                        xT_hi[:, 2 * q:2 * q + 2, :].bitcast(F32), ALU.subtract).then_inc(pool_lo, 1)
            enter("ffn1", residual(last("ffn1"), 5, 1.0, 1), (), [last("ffn1")])
            ffn("ffn1", 2)
            enter("ffn2", residual(last("ffn2"), 6, 0.5, 2), [last("ffn2") - 1], [last("ffn2")], lambda: modulation(1))
            ffn("ffn2", 3)
            enter("conv_in", residual(last("conv_in"), 7, 0.5, 3), [last("conv_in") - 1], [last("conv_in")])
            p = at["conv_in"]
            own(nc.vector.memset(uT[:, :, 0:CONV_W - 1], 0.0))
            g = p.slab
            q = at["conv_out"]
            for c in range(6):
                ahead(g)
                if c // 2 == 1:
                    for t in range(TT):
                        cols = slice((c % 2) * UPN, (c % 2 + 1) * UPN)
                        dve.wait_ge(conv_copied, 4)
                        if t == 0:
                            dve.wait_ge(up0_ready, p.up + c + 1)
                        else:
                            dve.wait_ge(slab_used, g + 2)
                        nc.vector.tensor_tensor(xn[:, t, cols], xn[:, t, cols], up_ps[:, t, :], ALU.mult)\
                            .then_inc(u_ready, 1)
                ahead(g + 1)
                if c == 4:
                    w0 = ROWS["convw"][0]
                    tap = lambda j, k: vecT[:, w0 + KT * j + k:w0 + KT * j + k + 1]
                    for k in range(KT):
                        dve.wait_ge(tr_ready, q.tr + k + 1)
                        own(nc.vector.tensor_copy(uT[:, k, 2:2 + TOKENS], tr_ps[:, (q.tr + k) % 2, 0:TOKENS]))
                        nc.vector.tensor_scalar(conv[:, k, :], uT[:, k, 2:2 + TOKENS], tap(2, k), None, ALU.mult)\
                            .then_inc(tr_read, 1)
                        dve.wait_ge(tr_read, q.tr + k + 1)
                        own(nc.vector.scalar_tensor_tensor(out=conv[:, k, :], in0=uT[:, k, 1:1 + TOKENS],
                                                           scalar=tap(1, k), in1=conv[:, k, :], op0=ALU.mult,
                                                           op1=ALU.add))
                        own(nc.vector.scalar_tensor_tensor(out=conv[:, k, :], in0=uT[:, k, 0:TOKENS],
                                                           scalar=tap(0, k), in1=conv[:, k, :], op0=ALU.mult,
                                                           op1=ALU.add))
                g += 2
            for k in range(KT):
                tr = q.tr + KT + k
                dve.wait_ge(tr_ready, tr + 1)
                nc.vector.tensor_tensor(conv[:, k, :], conv[:, k, :], tr_ps[:, tr % 2, 0:TOKENS], ALU.mult)\
                    .then_inc(conv_y, 1)
                dve.wait_ge(conv_hi, k + 1)
                nc.vector.tensor_tensor(xT_lo[:, k, :], conv[:, k, :], xT_hi[:, k, :].bitcast(F32), ALU.subtract)\
                    .then_inc(tr_read, 1)
            for k in range(2):
                ahead(g + k)
            enter("ffn3", residual(last("ffn3"), 8, 1.0, 4), [last("ffn3") - 1], [last("ffn3")])
            ffn("ffn3", 5)
            dve.wait_ge(gF_landed, 32)
            products = residual(last("final2"), 9, 0.5, 5)
            for t in range(TT):
                products(t)
            for t in range(TT):
                final("final2", xn, t, xn_ready)

        @block.tensor
        def _(pe):
            def plus(i, k, per=1):
                return k if i is None else i * per + k

            def mm(dst, a, b, start=False, stop=False):
                return nc.tensor.matmul(dst, a, b, start=start, stop=stop, skip_group_check=True)

            def up_tile(g, s, t):
                slot = g % RING
                a = slice(t * P, (t + 1) * P)
                for q in range(UPK):
                    k = s * UPK + q
                    b = slice(q * UPN, (q + 1) * UPN)
                    mm(up_ps[:, t, :], xT_hi[:, k, a], w_hi[:, slot, b], start=(k == 0))
                    mm(up_ps[:, t, :], xT_hi[:, k, a], w_lo[:, slot, b])
                    last = mm(up_ps[:, t, :], xT_lo[:, k, a], w_hi[:, slot, b], stop=(k == KT - 1))
                return last

            def up_chunk(g, i=None, per=0, free=None, between=None):
                for s in range(2):
                    pe.wait_ge(lo_ready, plus(i, g + s + 1, per))
                    for t in range(TT):
                        if s == 0 and free is not None:
                            pe.wait_ge(free[0], plus(i, free[1] + t, free[2]))
                        last = up_tile(g + s, s, t)
                        if (s, t) == (1, 0):
                            last.then_inc(up0_ready, 1)
                        if (s, t) == (0, 0) and between is not None:
                            between()
                    last.then_inc(slab_used, 1)

            def down_tile(g, t, hi, lo, k0, start, stop, qs=range(DOWNK)):
                slot = g % RING
                a = slice(t * P, (t + 1) * P)
                for q in qs:
                    for x_part, w_part in ((hi, w_hi), (hi, w_lo), (lo, w_hi)):
                        for c in range(2):
                            last = mm(acc[:, t, c * 512:(c + 1) * 512], x_part[:, k0 + q, a],
                                      w_part[:, slot, q * D + c * 512:q * D + (c + 1) * 512],
                                      start=start and q == 0 and x_part is hi and w_part is w_hi,
                                      stop=stop and q == DOWNK - 1 and x_part is lo)
                return last

            def down_slab(g, hi, lo, k0, start, i=None, per=0, ready=None):
                pe.wait_ge(lo_ready, plus(i, g + 1, per))
                for t in range(TT):
                    if ready is not None:
                        pe.wait_ge(tr_read, plus(i, ready[0] + (t + 1) * ready[1], ready[2]))
                    last = down_tile(g, t, hi, lo, k0, start, False)
                last.then_inc(slab_used, 1)

            def down_last(g, hi, lo, k0, start, ready):
                for t in range(TT):
                    pe.wait_ge(tr_read, ready[0] + (t + 1) * ready[1])
                    for s in range(2):
                        if t == 0:
                            pe.wait_ge(lo_ready, g + s + 1)
                        last = down_tile(g + s, t, hi, lo, k0 + 2 * s, start and s == 0, s == 1)
                        if t == 1:
                            last.then_inc(slab_used, 1)
                    if t == 0:
                        last.then_inc(acc0_ready, 1)

            def bank(tr, i=None, per=0):
                if tr >= 2:
                    pe.wait_ge(tr_read, plus(i, tr - 1, per))
                return tr_ps[:, tr % 2, :]

            def turn(src, t, f0, n, tr, i=None, per=0, order=ident):
                dst = bank(tr, i, per)
                for q in range(n):
                    tile = src[:, t, (f0 + q) * P:(f0 + q + 1) * P]
                    if order is ident:
                        last = nc.tensor.transpose(dst[:, q * P:(q + 1) * P], tile, ident)
                    else:
                        last = mm(dst[:, q * P:(q + 1) * P], tile, order, start=True, stop=True)
                last.then_inc(tr_ready, 1)

            def turn_tokens(src, f, tr, i=None, per=0, order=None):
                dst = bank(tr, i, per)
                for t in range(TT):
                    tile = src[:, t, f * P:(f + 1) * P]
                    if order is None:
                        last = nc.tensor.transpose(dst[:, t * P:(t + 1) * P], tile, ident)
                    else:
                        last = mm(dst[:, t * P:(t + 1) * P], tile, order, start=True, stop=True)
                last.then_inc(tr_ready, 1)

            def turn_norm(name, t):
                pe.wait_ge(xn_ready, 2 * XN[name] + t + 1)
                if t == 0:
                    pe.wait_ge(tr_read, at[name].tr)
                for b in range(KT // FILL):
                    turn(xn, t, b * FILL, FILL, at[name].tr + (KT // FILL) * t + b)

            def first_chunk(name):
                g = at[name].slab
                x0 = NORM_FILLS * XT[name]
                turn_norm(name, 0)
                for t in range(TT):
                    for s in range(2):
                        if t == 0:
                            pe.wait_ge(lo_ready, g + s + 1)
                        pe.wait_ge(xT_ready, x0 + 2 * t + s + 1)
                        last = up_tile(g + s, s, t)
                        if t == 1:
                            last.then_inc(slab_used, 1)
                        elif s == 0:
                            turn_norm(name, 1)
                        else:
                            last.then_inc(up0_ready, 1)

            pe.wait_ge(consts_ready, 7)
            pe.wait_ge(small_landed, 16 * (len(ROWS) + 1))
            for n, src in ((0, rows), (1, rows_b[:, 0, :]), (2, rows_b[:, 1, :])):
                if n >= 2:
                    pe.wait_ge(tr_read, n - 1)
                w = src.shape[0]
                nc.tensor.transpose(tr_ps[:, n % 2, 0:w], src, ident[0:w, 0:w]).then_inc(tr_ready, 1)
            pe.wait_ge(ws_masked, 1)
            for g in range(GROUPS):
                tr = 3 + g
                pe.wait_ge(tr_read, tr - 1)
                nc.tensor.transpose(tr_ps[:, tr % 2, 0:P], ws_raw[:, g, :], ident).then_inc(tr_ready, 1)

            g = at["gate_in"].slab
            first_chunk("gate_in")
            for c in range(1, 4):
                up_chunk(g + 2 * c, free=(gelu_done, 2 * (c - 1) + 1, 0))
            pe.wait_ge(mask_landed, 32)
            for n in range(NG):
                for part, (c0, c1) in enumerate(((n * VLEN, (n + 1) * VLEN),)):
                    for b0 in range(0, 3):
                        lo_c, hi_c = max(c0, 512 * b0), min(c1, 512 * (b0 + 1))
                        if lo_c < hi_c:
                            dst = acc[0:HEADS, b0 // 2, (b0 % 2) * 512 + lo_c - 512 * b0:
                                      (b0 % 2) * 512 + hi_c - 512 * b0]
                            last = mm(dst, rel[:, n * HEADS:(n + 1) * HEADS], mask_sb[:, n, lo_c - c0:hi_c - c0],
                                      start=True, stop=True)
            last.then_inc(bias_ps_ready, 1)
            pe.wait_ge(bias_sb_ready, 1)
            for t in range(TT):
                pe.wait_ge(vn_ready, t + 1)
                for q in range(GROUPS):
                    last = mm(acc[:, t, q * P:(q + 1) * P], ws_T[:, q, :], g_v[:, t, q * P:(q + 1) * P],
                              start=True, stop=True)
                last.then_inc(mix_ready, 1)
            p = at["gate_out"]
            for n in range(NORM_FILLS):
                t, b = divmod(n, KT // FILL)
                pe.wait_ge(gated, t + 1)
                turn(xn, t, b * FILL, FILL, p.tr + n)
            for k in range(2):
                down_slab(p.slab + k, xT_hi, xT_lo, 2 * k, k == 0, ready=(p.tr, 2, 0))
            down_last(p.slab + 2, xT_hi, xT_lo, 4, False, (p.tr, 2))

            def mlp(name):
                p = at[name]
                m0 = 0 if name == "mlp0" else MLP_CHUNKS
                tr0 = p.tr + NORM_FILLS
                g = p.slab

                def turn_mid(c, i=None, cper=0):
                    for t in range(TT):
                        pe.wait_ge(mlp_mid, plus(i, 2 * (m0 + c) + t + 1, 2 * cper))
                        turn(mid, t, 0, 4, tr0 + 2 * c + t, i, 2 * cper)

                def step(c, start, i=None, cper=0, between=None):
                    gb = g + 4 * c - 2
                    up_chunk(gb, i, 4 * cper, (relu_done, 2 * (m0 + c - 1) + 1, 2 * cper), between)
                    for s in range(2):
                        down_slab(gb + 2 + s, hT_hi, hT_lo, 2 * s, start and s == 0, i, 4 * cper,
                                  (tr0 + 2 * (c - 1), 1, 2 * cper))
                    turn_mid(c, i, cper)

                first_chunk(name)
                step(1, True, between=lambda: turn_mid(0))
                with pe.Fori(0, MLP_BODIES) as i:
                    for b in range(MLP_BODY):
                        step(2 + b, False, i, MLP_BODY)
                down_last(g + 4 * MLP_CHUNKS - 2, hT_hi, hT_lo, 0, False, (tr0 + 2 * (MLP_CHUNKS - 1), 1))

            mlp("mlp0")

            p = at["qkv"]
            stage = [mid, pre, xn]
            tr0 = p.tr + NORM_FILLS

            def qk_turn(n, i):
                pe.wait_ge(qkv_copied, 2 * n + 2 + 6 * i)
                for f in range(4):
                    turn_tokens(stage[n], f, tr0 + 4 * n + f + 12 * i, order=flip[:, i, :])

            for i in range(2):
                for b in range(3):
                    c = 3 * i + b
                    if c == 0:
                        first_chunk("qkv")
                    else:
                        up_chunk(p.slab + 2 * c, free=(qkv_copied, 2 * (c - 1) + 1, 0))
                    if b:
                        qk_turn(b - 1, i)
                qk_turn(2, i)
            for b in range(3):
                up_chunk(p.slab + 12 + 2 * b, free=(qkv_copied, 2 * (6 + b - 1) + 1, 0))

            p = at["attn"]
            pe.wait_ge(tr_read, p.tr)
            pe.wait_ge(qkv_copied, 18)

            def scores(u):
                h, t = divmod(u, 2)
                rows_h = slice((h % 2) * HD, (h % 2 + 1) * HD)
                if u >= 2:
                    pe.wait_ge(logit_ready, u - 1)
                for n in range(NG):
                    last = mm(acc[:, t, n * TOKENS:n * TOKENS + P * (t + 1)],
                              qkT[rows_h, 4 * n + h // 2, t * P:(t + 1) * P],
                              qkT[rows_h, 12 + 4 * n + h // 2, 0:P * (t + 1)], start=True, stop=True)
                last.then_inc(score_ready, 1)

            def turn_probs(u):
                t = u % 2
                pe.wait_ge(prob_ready, u + 1)
                for a in range(1 + t):
                    tr = p.tr + tr_of(u) + a
                    pe.wait_ge(tr_read, tr - 1)
                    for q in range(3):
                        m = 3 * a + q
                        last = nc.tensor.transpose(tr_ps[:, tr % 2, q * P:(q + 1) * P],
                                                   xn[:, t, m * P:(m + 1) * P], ident)
                    last.then_inc(tr_ready, 1)

            def attend(u):
                h, t = divmod(u, 2)
                pe.wait_ge(tr_read, p.tr + tr_of(u + 1))
                if u >= 2:
                    pe.wait_ge(o_ready, u - 1)
                blocks = [(n, k) for n in range(NG) for k in range(t + 1)]
                src = (mid, pre)[u % 2][:, :, :].rearrange("p t n -> p (t n)")
                for m, (n, k) in enumerate(blocks):
                    last = mm(up_ps[:, t, h * HD:(h + 1) * HD], src[:, m * P:(m + 1) * P],
                              v_tok[:, k, n * UPN + h * HD:n * UPN + (h + 1) * HD],
                              start=(m == 0), stop=(m == len(blocks) - 1))
                last.then_inc(pv_ready, 1)

            scores(0)
            scores(1)
            turn_probs(0)
            for u in range(2 * HEADS):
                if u + 2 < 2 * HEADS:
                    scores(u + 2)
                if u + 1 < 2 * HEADS:
                    turn_probs(u + 1)
                attend(u)
            p = at["attn_out"]
            pe.wait_ge(o_ready, 2 * HEADS)
            for t in range(TT):
                turn(o_tok, t, 0, 4, p.tr + t, order=flip[:, 0, :])
            down_last(p.slab, hT_hi, hT_lo, 0, True, (p.tr, 1))

            mlp("mlp1")

            def modulation(layer):
                pe.wait_ge(ada_step, 8 * ADA_UNITS * (layer + 1))
                for s in range(3):
                    for m in range(2 * KT):
                        n = s * 3 * KT + m
                        last = mm(up_ps[:, 0, n:n + 1], ada_acc[:, n * P:(n + 1) * P], ones[:, 0:1],
                                  start=True, stop=True)
                last.then_inc(mod_ps_ready, 1)

            def gate(sub):
                s = sub % 3
                for c in range(2):
                    n = (3 * s + 2) * D + c * 512
                    last = mm(acc[:, s % 2, c * 512:(c + 1) * 512], ones[:, :], ada_acc[:, n:n + 512],
                              start=True, stop=True)
                last.then_inc(gate_ps_ready, 1)

            def ffn(name, sub):
                p = at[name]
                f0 = FFN_AT[name] * FFN_CHUNKS
                tr0 = p.tr + NORM_FILLS
                g = p.slab

                def turn_mid(c, i=None):
                    for t in range(TT):
                        pe.wait_ge(ffn_mid, plus(i, 2 * (f0 + c) + t + 1, 2))
                        turn(mid, t, 0, 2, tr0 + 2 * c + t, i, 2)

                def step(c, start, i=None, between=None):
                    gb = g + 3 * c - 1
                    up_chunk(gb, i, 3, (ffn_mid, 2 * (f0 + c - 1) + 1, 2), between)
                    if start and sub % 3 == 0:
                        pe.wait_ge(gate_ready, sub + 3)
                    down_slab(gb + 2, hT_hi, hT_lo, 0, start, i, 3, (tr0 + 2 * (c - 1), 1, 2))
                    turn_mid(c, i)

                def between():
                    turn_mid(0)
                    if sub % 3 == 0:
                        pe.wait_ge(gate_ready, sub + 1)
                        gate(sub + 2)

                if sub % 3 == 0:
                    modulation(sub // 3)
                first_chunk(name)
                if sub % 3 == 0:
                    pe.wait_ge(res_ready, 2 * p.norm)
                    gate(sub)
                    gate(sub + 1)
                step(1, True, between=between)
                with pe.Fori(0, FFN_CHUNKS - 3) as i:
                    step(2, False, i)
                c = FFN_CHUNKS - 1
                gb = g + 3 * c - 1
                up_chunk(gb, free=(ffn_mid, 2 * (f0 + c - 1) + 1, 0))
                ready = tr0 + 2 * (c - 1)
                pe.wait_ge(lo_ready, gb + 3)
                pe.wait_ge(tr_read, ready + 2)
                down_tile(gb + 2, 0, hT_hi, hT_lo, 0, False, False)
                turn_mid(c)
                down_tile(gb + 2, 1, hT_hi, hT_lo, 0, False, False, [0])
                pe.wait_ge(lo_ready, gb + 4)
                pe.wait_ge(tr_read, ready + 3)
                down_tile(gb + 3, 0, hT_hi, hT_lo, 2, False, True).then_inc(acc0_ready, 1)
                down_tile(gb + 2, 1, hT_hi, hT_lo, 0, False, False, [1]).then_inc(slab_used, 1)
                pe.wait_ge(tr_read, ready + 4)
                down_tile(gb + 3, 1, hT_hi, hT_lo, 2, False, True).then_inc(slab_used, 1)

            ffn("ffn0", 0)
            p = at["pool"]
            pe.wait_ge(xn_ready, 2 * XN["pool"] + 2)
            for k in range(KT):
                turn_tokens(xn, k, p.tr + k)
            pe.wait_ge(lo_ready, p.slab + 1)
            slot = p.slab % RING
            for t in range(TT):
                for q in range(len(POOL_WINDOWS)):
                    pe.wait_ge(pool_lo, q + 1)
                    for kk in range(2):
                        k = 2 * q + kk
                        for n, (x_part, w_part) in enumerate(((xT_hi, w_hi), (xT_hi, w_lo), (xT_lo, w_hi))):
                            last = mm(acc[:, t, q * 256:(q + 1) * 256], x_part[:, k, t * P:(t + 1) * P],
                                      w_part[:, slot, k * 256:(k + 1) * 256], start=(kk == 0 and n == 0),
                                      stop=(kk == 1 and n == 2))
                if t == 0:
                    last.then_inc(acc0_ready, 1)
            last.then_inc(slab_used, 1)
            ffn("ffn1", 2)
            ffn("ffn2", 3)

            p = at["conv_in"]
            q = at["conv_out"]
            g = p.slab
            free = [None, (conv_copied, 1, 0), (conv_copied, 3, 0), (u_ready, 1, 0), (u_ready, 3, 0), (conv_copied, 5, 0)]
            for c in range(6):
                if c == 0:
                    first_chunk("conv_in")
                else:
                    up_chunk(g, free=free[c])
                g += 2
                if c == 4:
                    for k in range(KT):
                        turn_tokens(xn, k, q.tr + k)
            pe.wait_ge(conv_copied, 8)
            for k in range(KT):
                turn_tokens(b_tok, k, q.tr + KT + k)
            for k in range(2):
                pe.wait_ge(tr_read, q.tr + KT + 2 * k + 2)
                down_slab(g + k, xT_hi, xT_lo, 2 * k, k == 0)
            down_last(g + 2, xT_hi, xT_lo, 4, False, (q.tr + 2 * KT, 0))
            ffn("ffn3", 5)


_INS = ["x", "mix_norm_g", "mlp_norm_g", "final_norm_g", "a_w_in", "a_ln_g", "a_ln_b", "a_w_s", "a_b_s", "a_w_out",
        "b_w_qkv", "b_w_out", "rel_bias", "w_up", "w_down", "c_2", "ada_w_2", "ada_b_2", "norm_g_2", "ffn_w_in_2",
        "ffn_w_out_2", "pool_w_2", "pool_scale_2", "conv_w_in_2", "conv_w_2", "conv_w_out_2", "final_g_2"]


def kernel(**inputs):
    import concourse.bacc as bacc
    from concourse.bass_utils import run_bass_kernel_spmd

    nc = bacc.Bacc("TRN2", target_bir_lowering=False, num_devices=1, dynamic_dma_scratch_size=64)
    arrays, args = {}, []
    for name in _INS:
        a = np.ascontiguousarray(inputs[name])
        arrays[f"in_{name}"] = a
        args.append(nc.dram_tensor(f"in_{name}", a.shape, mybir.dt.from_np(a.dtype), kind="ExternalInput").ap())
    masks = nc.inline_tensor(bucket_masks(), "bucket_masks").ap()
    bias_rows = nc.dram_tensor("bias_rows", (HEADS * NG * VLEN,), F32).ap()
    out = nc.dram_tensor("out", (1, TOKENS, D), F32, kind="ExternalOutput").ap()
    build(nc, *args, masks, bias_rows, out)
    r = run_bass_kernel_spmd(nc, [arrays], core_ids=[0])
    return r.results[0]["out"]
```

```python
from contextlib import ExitStack
import math

import numpy as np
import concourse.bass as bass
from concourse import mybir

ALU = mybir.AluOpType
ACT = mybir.ActivationFunctionType
AX_X = mybir.AxisListType.X
F32 = mybir.dt.float32
F32R = mybir.dt.float32r

P = 128
D = 1024
KT = D // P
TOKENS = 256
TT = TOKENS // P
SLAB = 2048
UPK = 4
UPN = SLAB // UPK
DOWNK = SLAB // D
RING = 3
FILL = 4
NORM_FILLS = TT * KT // FILL
EPS = 1e-6

D_FF = 4 * D
D_FF_2 = ((8 * D // 3 + 255) // 256) * 256
HALF = UPN // 2
MLP_CHUNKS = D_FF // UPN
FFN_CHUNKS = D_FF_2 // HALF
MLP_BODY = 3

HEADS = 8
HD = 64
WINDOWS = ((128, 1), (512, 4), (2048, 16))
NG = len(WINDOWS)
N_BUCKETS = 32
VLEN = 3 * P
NEG_INF = -1e30

GROUPS = 8
ADA_COLS = 9 * D
ADA_UNITS = ADA_COLS // UPN
POOL_WINDOWS = (2, 4, 8, 16)
POOLS = len(POOL_WINDOWS)
CONV_W = 3

ROWS = {}
for _name, _n in (("mix", 2 * KT), ("mlp", 2 * KT), ("norm", 6 * KT), ("convw", CONV_W * KT), ("bs", GROUPS), ("c", KT)):
    ROWS[_name] = (sum(n for _, n in ROWS.values()), _n)
N_ROWS = sum(n for _, n in ROWS.values())

MLP_BODIES = (MLP_CHUNKS - 2) // MLP_BODY
ADA_AT = {"mlp0": 0, "qkv": MLP_CHUNKS, "mlp1": MLP_CHUNKS + 2, "ffn0": ADA_UNITS, "ffn1": ADA_UNITS + FFN_CHUNKS - 2}
MODS = {"mlp1": (0,), "ffn0": (1, 2), "ffn1": (3,), "ffn2": (4, 5)}
MOD_FILLS = 2 * KT // FILL
GATES = {"ffn0": (0, 1), "ffn1": (2,), "ffn2": (3, 4), "ffn3": (5,)}
GATE_HALF = {sub: n for subs in GATES.values() for n, sub in enumerate(subs)}
FFN_AT = {"ffn0": 0, "ffn1": 1, "ffn2": 2, "ffn3": 3}


def tr_of(u):
    return 3 * (u // 2) + u % 2


def bucket_masks():
    m = np.zeros((N_BUCKETS + 1, NG, VLEN), np.float32)
    exact = N_BUCKETS // 2
    longest = max(w for w, _ in WINDOWS)
    for g, (window, dil) in enumerate(WINDOWS):
        for i in range(VLEN):
            d = TOKENS - 1 - i
            if d < 0 or d % dil or d // dil > window // dil:
                m[N_BUCKETS, g, i] = NEG_INF
                continue
            b = d if d < exact else min(
                exact + int(math.log(d / exact) / math.log(longest / exact) * (N_BUCKETS - exact)), N_BUCKETS - 1)
            m[b, g, i] = 1.0
    return m


def pool_weights():
    full = np.zeros((len(POOL_WINDOWS), TOKENS, TOKENS), np.float64)
    for n, window in enumerate(POOL_WINDOWS):
        for t in range(TOKENS):
            full[n, max(0, t + 1 - window):t + 1, t] = 1.0 / min(window, t + 1)
            full[n, t, t] -= 1.0
    both = np.concatenate([full[:, :P, :], full[:, P:, P:]], axis=2)
    return np.ascontiguousarray(both.transpose(1, 0, 2).astype(np.float32))


class Phase:

    def __init__(self, slab, up, tr, split, norm):
        self.slab, self.up, self.tr, self.split, self.norm = slab, up, tr, split, norm


def mid_fill(p, name, c):
    return p.tr + NORM_FILLS + TT * c + (MOD_FILLS * len(MODS.get(name, ())) if c else 0)


def plan():
    def fused(name, slabs, chunks):
        fills = NORM_FILLS + TT * chunks + MOD_FILLS * len(MODS.get(name, ()))
        return name, slabs * chunks, chunks, fills, TT * chunks, 1

    parts = [
        ("setup", 0, 0, 3, 0, 0),
        ("gate_in", 8, 4, NORM_FILLS, 0, 1),
        ("positions", 0, 0, GROUPS, 0, 0),
        ("gate_out", 4, 0, NORM_FILLS, NORM_FILLS, 0),
        fused("mlp0", 4, MLP_CHUNKS),
        ("qkv", 18, 9, NORM_FILLS + 6 * TT, 0, 1),
        ("attn", 0, 0, 3 * HEADS, 0, 0),
        ("attn_out", 2, 0, TT, TT, 0),
        fused("mlp1", 4, MLP_CHUNKS),
        ("final1", 0, 0, 0, 0, 1),
        fused("ffn0", 3, FFN_CHUNKS),
        ("pool", 1, 0, POOLS, 0, 1),
        fused("ffn1", 3, FFN_CHUNKS),
        fused("ffn2", 3, FFN_CHUNKS),
        ("conv_in", 12, 6, NORM_FILLS, 0, 1),
        ("conv_out", 4, 0, 2 * KT, 0, 0),
        fused("ffn3", 3, FFN_CHUNKS),
        ("final2", 0, 0, 0, 0, 1),
    ]
    at, c = {}, [0, 0, 0, 0, 0]
    for name, *n in parts:
        at[name] = Phase(*c)
        c = [a + b for a, b in zip(c, n)]
    at["end"] = Phase(*c)
    return at


def build(nc, x, mix_norm_g, mlp_norm_g, final_norm_g, a_w_in, a_ln_g, a_ln_b, a_w_s, a_b_s, a_w_out,
          b_w_qkv, b_w_out, rel_bias, w_up, w_down, c_2, ada_w_2, ada_b_2, norm_g_2, ffn_w_in_2,
          ffn_w_out_2, pool_w_2, pool_scale_2, conv_w_in_2, conv_w_2, conv_w_out_2, final_g_2,
          masks, means, bias_rows, out):
    at = plan()
    N_SLABS = at["end"].slab

    ctx = ExitStack()
    with ctx:
        def sb(name, shape, dt=F32):
            return ctx.enter_context(nc.sbuf_tensor(name, shape, dt))

        def sem(name):
            return ctx.enter_context(nc.semaphore(name))

        raw = sb("raw", [P, RING, SLAB])
        w_hi = sb("w_hi", [P, RING, SLAB], F32R)
        w_lo = sb("w_lo", [P, RING, SLAB], F32R)
        ada_raw = sb("ada_raw", [P, 2, SLAB])
        ada_acc = sb("ada_acc", [P, ADA_COLS])
        res = sb("res", [P, TT, D])
        xn = sb("xn", [P, TT, D])
        xT_hi = sb("xT_hi", [P, KT, TOKENS], F32R)
        xT_lo = sb("xT_lo", [P, KT, TOKENS], F32R)
        mid = sb("mid", [P, TT, UPN])
        pre = sb("pre", [P, TT, UPN])
        hT_hi = sb("hT_hi", [P, 4, TOKENS], F32R)
        hT_lo = sb("hT_lo", [P, 4, TOKENS], F32R)
        flip = sb("flip", [P, 2, P])
        ident = flip[:, 1, :]
        ones = sb("ones", [P, P])
        vecT = sb("vecT", [P, N_ROWS])
        adabT = sb("adabT", [P, 2, 72])
        cond = sb("cond", [P, KT])
        sumsq = sb("sumsq", [P, TT])
        msq = sb("msq", [P, TT])
        rstd = sb("rstd", [P, TT])
        neg_half = sb("neg_half", [P, 1])
        mod_sum = sb("mod_sum", [P, 2 * KT])
        mod = sb("mod", [P, 3, 2 * KT])
        gain = sb("gain", [P, 3, KT])
        den = sb("den", [P, 2 * HEADS])
        rden = sb("rden", [P, 2 * HEADS])
        mx = sb("mx", [P, 2 * HEADS])
        nmx = sb("nmx", [P, 2 * HEADS])
        stats = sb("stats", [P, TT, 2, 6])
        mv = sb("mv", [P, TT, 2])
        region = sb("region", [P, 10752])

        g_u = region[:, 0:2048].rearrange("p (t n) -> p t n", t=TT)
        g_v = region[:, 2048:4096].rearrange("p (t n) -> p t n", t=TT)
        ln_g = region[:, 4096:5120]
        ln_b = region[:, 5120:6144]
        ws_raw = region[:, 6144:7168].rearrange("p (g n) -> p g n", g=GROUPS)
        ws_T = region[:, 7168:8192].rearrange("p (g n) -> p g n", g=GROUPS)
        rows = region[0:N_ROWS, 8192:8320]
        rows_b = region[0:72, 8320:8576].rearrange("p (l n) -> p l n", l=2)
        rel = region[0:N_BUCKETS + 1, 8576:8600]
        mask_sb = region[0:N_BUCKETS + 1, 8600:8600 + NG * VLEN].rearrange("p (g n) -> p g n", g=NG)
        bias_v = region[0:HEADS, 8600:8600 + NG * VLEN]
        qkT = region[:, 0:6144].rearrange("p (f n) -> p f n", f=24)
        v_tok = region[:, 6144:9216].rearrange("p (t n) -> p t n", t=TT)
        bias_t = region[:, 9216:10752].rearrange("p (b g n) -> p b g n", b=2, g=NG)
        gate_B = region[:, 0:3072].rearrange("p (s n) -> p s n", s=3)
        gF = region[:, 4096:5120]
        pool_y = region[:, 4096:6144].rearrange("p (k n) -> p k n", k=KT)
        ps_B = region[:, 6144:7168]
        pool_w = region[:, 7168:7168 + POOLS * 3 * P].rearrange("p (w n) -> p w n", w=POOLS)
        b_tok = region[:, 4096:6144].rearrange("p (t n) -> p t n", t=TT)
        uT = region[:, 6144:6144 + KT * (TOKENS + 2)].rearrange("p (k n) -> p k n", k=KT)
        conv = region[:, 8208:8208 + KT * TOKENS].rearrange("p (k n) -> p k n", k=KT)
        o_tok = sb("o_tok", [P, TT, HEADS * HD])

        up_ps = ctx.enter_context(nc.psum_tensor("up_ps", [P, TT, UPN], F32))
        acc = ctx.enter_context(nc.psum_tensor("acc", [P, TT, D], F32))
        tr_ps = ctx.enter_context(nc.psum_tensor("tr_ps", [P, 2, 512], F32))

        raw_landed = [sem(f"raw_landed{i}") for i in range(RING)]
        ada_landed = [sem(f"ada_landed{i}") for i in range(2)]
        x_landed, small_landed = sem("x_landed"), sem("small_landed")
        ln_landed, mask_landed = sem("ln_landed"), sem("mask_landed")
        bias_stored = sem("bias_stored")
        bias_landed = [sem(f"bias_landed{i}") for i in range(2)]
        row_landed, gF_landed, ps_landed = sem("row_landed"), sem("gF_landed"), sem("ps_landed")
        ws_landed, o_ready = sem("ws_landed"), sem("o_ready")
        out_stored = sem("out_stored")
        hi_ready, lo_ready, slab_used = sem("hi_ready"), sem("lo_ready"), sem("slab_used")
        ada_step = sem("ada_step")
        consts_ready, ws_masked = sem("consts_ready"), sem("ws_masked")
        up0_ready, acc0_ready = sem("up0_ready"), sem("acc0_ready")
        tr_ready, tr_hi, tr_read = sem("tr_ready"), sem("tr_hi"), sem("tr_read")
        y_half, xT_ready = sem("y_half"), sem("xT_ready")
        res_ready, sumsq_ready, rstd_ready = ([sem(f"{n}{t}") for t in range(TT)]
                                              for n in ("res_ready", "sumsq_ready", "rstd_ready"))
        xn_ready = sem("xn_ready")
        msq_ready = sem("msq_ready")
        gelu_done, relu_done, mlp_mid = sem("gelu_done"), sem("relu_done"), sem("mlp_mid")
        var_ready, ln_rstd, vn_ready, mix_ready, gated = (sem("var_ready"), sem("ln_rstd"), sem("vn_ready"),
                                                          sem("mix_ready"), sem("gated"))
        cond_ready = sem("cond_ready")
        bias_ps_ready, bias_sb_ready = sem("bias_ps_ready"), sem("bias_sb_ready")
        qkv_copied = sem("qkv_copied")
        score_ready, logit_ready, max_ready, prob_ready = (sem("score_ready"), sem("logit_ready"), sem("max_ready"),
                                                           sem("prob_ready"))
        pv_ready = sem("pv_ready")
        silu_done, ffn_mid = sem("silu_done"), sem("ffn_mid")
        mod_ready = sem("mod_ready")
        gate_ps_ready, gate_ready = sem("gate_ps_ready"), sem("gate_ready")
        pool_landed, sums_ready, pool_lo = sem("pool_landed"), sem("sums_ready"), sem("pool_lo")
        conv_copied, u_ready, conv_hi, conv_lo = sem("conv_copied"), sem("u_ready"), sem("conv_hi"), sem("conv_lo")
        conv_step = sem("conv_step")
        dve_step = sem("dve_step")

        block = ctx.enter_context(nc.Block())

        NORM = {n: at[n].norm for n in ("gate_in", "mlp0", "qkv", "mlp1", "final1", "ffn0", "pool", "ffn1", "ffn2",
                                        "conv_in", "ffn3", "final2")}
        XN = {n: i for i, n in enumerate(n for n in NORM if n != "final1")}
        XT = {n: i for i, n in enumerate(n for n in XN if n not in ("pool", "final2"))}
        SUBS = ["ffn0", "pool", "ffn1", "ffn2", "conv_in", "ffn3"]

        up_view = lambda r: r.rearrange("p (k n) -> p k n", k=UPK)
        down_view = lambda r: r.rearrange("p (k n) -> p k n", k=DOWNK)
        ffn_view = lambda r: r.rearrange("p (k h n) -> p k h n", k=UPK, h=2)

        def up_src(w, s, col):
            return w[s * 512:(s + 1) * 512, bass.ds(col, UPN)].rearrange("(k p) n -> p k n", p=P)

        def load_bias(eng, h):
            skew = bass.AP(tensor=bias_rows.tensor, offset=h * NG * VLEN, ap=[[1, P], [VLEN, NG], [1, TOKENS]])
            eng.dma_start(bias_t[:, h % 2], skew).then_inc(bias_landed[h % 2], 16)

        @block.sync
        def _(sp):
            sp.dma_start(res[:, :, :], x.rearrange("b (t p) n -> p (b t) n", p=P)).then_inc(x_landed, 16)
            srcs = {"mix": mix_norm_g.rearrange("l (k p) -> (l k) p", p=P),
                    "mlp": mlp_norm_g.rearrange("l (k p) -> (l k) p", p=P),
                    "norm": norm_g_2.rearrange("l s (k p) -> (l s k) p", p=P),
                    "convw": conv_w_2.rearrange("j w (k p) -> (j w k) p", p=P),
                    "bs": a_b_s[0],
                    "c": c_2.rearrange("b (k p) -> (b k) p", p=P)}
            for name, (r0, n) in ROWS.items():
                sp.dma_start(rows[r0:r0 + n, :], srcs[name]).then_inc(small_landed, 16)
            sp.dma_start(rows_b, ada_b_2.rearrange("l (k p) -> k l p", p=P)).then_inc(small_landed, 16)
            sp.dma_start(ws_raw, a_w_s[0].rearrange("g t s -> t g s")).then_inc(ws_landed, 16)

            def load(g, src, view):
                n = g if isinstance(g, int) else None
                slot = (g if n is not None else g[0]) % RING
                if n is not None:
                    if n >= RING:
                        sp.wait_ge(hi_ready, n - RING + 1)
                        sp.wait_ge(lo_ready, n - RING + 1)
                else:
                    sp.wait_ge(hi_ready, g[1] + (g[0] - RING + 1))
                    sp.wait_ge(lo_ready, g[1] + (g[0] - RING + 1))
                dst = view(raw[:, slot, :])
                for h in range(2):
                    if len(src.shape) == 4:
                        part = (slice(None), slice(None), h)
                    else:
                        k = src.shape[1] // 2
                        part = (slice(None), slice(h * k, (h + 1) * k))
                    sp.dma_start(dst[part], src[part]).then_inc(raw_landed[slot], 16)

            def down_src(w, row):
                return w[bass.ds(row, DOWNK * P), :].rearrange("(k p) n -> p k n", p=P)

            def ffn_src(w, s, col):
                v = w[s * 512:(s + 1) * 512, :].rearrange("(k p) (h n) -> p k h n", p=P, h=2)
                return v[:, :, :, bass.ds(col, HALF)]

            g = at["gate_in"].slab
            for n, chunk in enumerate((2, 3, 0, 1)):
                for s in range(2):
                    load(g, up_src(a_w_in[0], s, chunk * UPN), up_view)
                    g += 1
                if n == 1:
                    sp.dma_start(ln_g, a_ln_g.to_broadcast([P, D])).then_inc(ln_landed, 16)
                    sp.dma_start(ln_b, a_ln_b.to_broadcast([P, D])).then_inc(ln_landed, 16)
                    sp.dma_start(rel[0:N_BUCKETS, :], rel_bias).then_inc(mask_landed, 16)
                    sp.dma_start(mask_sb, masks).then_inc(mask_landed, 16)
            for k in range(4):
                load(g, down_src(a_w_out[0], k * DOWNK * P), down_view)
                g += 1

            def mlp(name, layer):
                g0 = at[name].slab

                def up(g, j):
                    for s in range(2):
                        load(g(s), up_src(w_up[layer], s, j * UPN), up_view)

                def down(g, j):
                    for s in range(2):
                        load(g(s), down_src(w_down[layer], j * UPN + s * DOWNK * P), down_view)

                up(lambda s: g0 + s, 0)
                up(lambda s: g0 + 2 + s, 1)
                down(lambda s: g0 + 4 + s, 0)
                with sp.Fori(0, MLP_BODIES) as i:
                    for b in range(MLP_BODY):
                        j = i * MLP_BODY + (b + 2)
                        up(lambda s: (g0 + 6 + 4 * b + s, i * (4 * MLP_BODY)), j)
                        down(lambda s: (g0 + 8 + 4 * b + s, i * (4 * MLP_BODY)), j - 1)
                down(lambda s: g0 + 4 * MLP_CHUNKS - 2 + s, MLP_CHUNKS - 1)

            sp.wait_ge(bias_sb_ready, 1)
            sp.dma_start(bias_rows.rearrange("(h n) -> h n", h=HEADS), bias_v).then_inc(bias_stored, 16)
            mlp("mlp0", 0)

            g0 = at["qkv"].slab
            with sp.Fori(0, 3) as i:
                for b in range(3):
                    for s in range(2):
                        load((g0 + 2 * b + s, i * 6), up_src(b_w_qkv[0], s, (i * 3 + b) * UPN), up_view)
            sp.wait_ge(bias_stored, 16)
            g = at["attn_out"].slab
            load(g, down_src(b_w_out[0], 0), down_view)
            sp.wait_ge(xn_ready, 2 * XN["qkv"] + 2)
            for h in range(2):
                load_bias(sp, h)
            load(g + 1, down_src(b_w_out[0], DOWNK * P), down_view)

            mlp("mlp1", 1)

            sp.wait_ge(xn_ready, 2 * XN["mlp1"] + 2)
            sp.dma_start(gF, final_norm_g.rearrange("(a n) -> a n", a=1).to_broadcast([P, D])).then_inc(gF_landed, 16)

            def gate_rows(layer):
                if layer:
                    sp.wait_ge(res_ready[1], NORM["ffn2"])
                for s in range(3):
                    sp.dma_start(gate_B[:, s, :], ada_b_2[layer:layer + 1, (3 * s + 2) * D:(3 * s + 3) * D]
                                 .to_broadcast([P, D])).then_inc(row_landed, 16)

            def ffn(name, idx, rows_of=None):
                g0 = at[name].slab
                layer, which = divmod(idx, 2)
                w_in, w_out = ffn_w_in_2[layer, which], ffn_w_out_2[layer, which]
                for j in range(2):
                    for s in range(2):
                        load(g0 + 2 * j + s, ffn_src(w_in, s, j * HALF), ffn_view)
                if rows_of is not None:
                    gate_rows(rows_of)
                load(g0 + 4, down_src(w_out, 0), down_view)
                with sp.Fori(0, FFN_CHUNKS - 2) as i:
                    for s in range(2):
                        load((g0 + 5 + s, i * 3), ffn_src(w_in, s, (i + 2) * HALF), ffn_view)
                    load((g0 + 7, i * 3), down_src(w_out, (i + 1) * HALF), down_view)
                load(g0 + 3 * FFN_CHUNKS - 1, down_src(w_out, (FFN_CHUNKS - 1) * HALF), down_view)

            sp.dma_start(pool_w, means).then_inc(pool_landed, 16)
            sp.dma_start(ps_B, pool_scale_2.to_broadcast([P, D])).then_inc(ps_landed, 16)
            ffn("ffn0", 0, 0)
            load(at["pool"].slab, pool_w_2[0].rearrange("g (k p) n -> p (g k) n", p=P),
                 lambda r: r.rearrange("p (k n) -> p k n", k=KT))
            ffn("ffn1", 1)
            ffn("ffn2", 2, 1)
            g = at["conv_in"].slab
            for chunk in (2, 3, 4, 5, 0, 1):
                for s in range(2):
                    load(g, up_src(conv_w_in_2[0], s, chunk * UPN), up_view)
                    g += 1
            for k in range(4):
                load(g, down_src(conv_w_out_2[0], k * DOWNK * P), down_view)
                g += 1
            ffn("ffn3", 3)
            sp.dma_start(gF, final_g_2.rearrange("(a n) -> a n", a=1).to_broadcast([P, D])).then_inc(gF_landed, 16)
            for t in range(TT):
                sp.wait_ge(xn_ready, 2 * XN["final2"] + t + 1)
                sp.dma_start(out[0, t * P:(t + 1) * P, :], xn[:, t, :]).then_inc(out_stored, 16)
            sp.wait_ge(out_stored, 16 * TT)

        @block.gpsimd
        def _(pool):
            nc.gpsimd.memset(flip[:, :, :], 0.0).then_inc(consts_ready, 1)
            nc.gpsimd.memset(ones[:, :], 1.0).then_inc(consts_ready, 1)
            nc.gpsimd.memset(neg_half[:, :], -0.5).then_inc(consts_ready, 1)
            pool.wait_ge(consts_ready, 3)
            nc.gpsimd.memset(rel[N_BUCKETS:N_BUCKETS + 1, :], 1.0).then_inc(consts_ready, 1)
            pool.wait_ge(consts_ready, 4)
            nc.gpsimd.affine_select(out=ident, in_=ident, compare_op=ALU.not_equal, fill=1.0, base=0,
                                    pattern=[[-1, P]], channel_multiplier=1).then_inc(consts_ready, 1)
            nc.gpsimd.affine_select(out=flip[:, 0, :], in_=flip[:, 0, :], compare_op=ALU.not_equal, fill=1.0,
                                    base=1 - P, pattern=[[1, P]], channel_multiplier=1).then_inc(consts_ready, 1)
            pool.wait_ge(ws_landed, 16)
            nc.gpsimd.affine_select(out=ws_raw, in_=ws_raw, compare_op=ALU.is_ge, fill=0.0, base=0,
                                    pattern=[[0, GROUPS], [-1, P]], channel_multiplier=1).then_inc(ws_masked, 1)

            def inverse_root(src, dst, ready):
                nc.gpsimd.tensor_tensor(dst, src, neg_half[:, 0:1], ALU.pow).then_inc(ready, 1)

            scaled = [0]

            def root_of(src, scale, t, ready):
                nc.gpsimd.tensor_scalar(msq[:, t:t + 1], src, scale, EPS, ALU.mult, ALU.add).then_inc(msq_ready, 1)
                scaled[0] += 1
                pool.wait_ge(msq_ready, scaled[0])
                inverse_root(msq[:, t:t + 1], rstd[:, t:t + 1], ready)

            def norm(n, t):
                pool.wait_ge(sumsq_ready[t], n + 1)
                root_of(sumsq[:, t:t + 1], 1.0 / D, t, rstd_ready[t])

            for t in range(TT):
                norm(0, t)
            for t in range(TT):
                pool.wait_ge(var_ready, t + 1)
                root_of(mv[:, t, 1:2], 1.0, t, ln_rstd)
            for names in (("mlp0",), ("qkv",), ("mlp1",), ("final1", "ffn0"), ("pool",), ("ffn1",), ("ffn2",),
                          ("conv_in",), ("ffn3",), ("final2",)):
                for t in range(TT):
                    for name in names:
                        norm(NORM[name], t)

        @block.scalar
        def _(act):
            def split_hi(slot, n):
                if isinstance(n, int):
                    if n >= N_SLABS:
                        return
                    act.wait_ge(raw_landed[slot], 32 * (n // RING + 1))
                    if n >= RING:
                        act.wait_ge(slab_used, n - RING + 1)
                else:
                    first, i, per = n
                    act.wait_ge(raw_landed[slot], i * (32 * per // RING) + 32 * (first // RING + 1))
                    act.wait_ge(slab_used, i * per + (first - RING + 1))
                nc.scalar.activation(w_hi[:, slot, :], raw[:, slot, :], ACT.Copy).then_inc(hi_ready, 1)

            def ahead(g, i=None, per=0):
                n = g + RING
                split_hi(n % RING, n if i is None else (n, i, per))

            def plus(i, k, per=1):
                return k if i is None else i * per + k

            def hi_part(dst, tr, i=None, per=0):
                act.wait_ge(tr_ready, plus(i, tr + 1, per))
                src = tr_ps[:, tr % 2, 0:dst.shape[1] * P].rearrange("p (f n) -> p f n", n=P)
                nc.scalar.activation(dst, src, ACT.Copy).then_inc(tr_hi, 1)

            def square(n, t):
                if n:
                    act.wait_ge(res_ready[t], n)
                elif t == 0:
                    act.wait_ge(x_landed, 16)
                nc.scalar.activation(xn[:, t, :], res[:, t, :], ACT.Square,
                                     accum_out=sumsq[:, t:t + 1]).then_inc(sumsq_ready[t], 1)

            def norm_out(name, t, gain_of):
                for b in range(KT // FILL):
                    fill = at[name].tr + (KT // FILL) * t + b
                    act.wait_ge(tr_ready, fill + 1)
                    for q in range(FILL):
                        k = b * FILL + q
                        scale, bias = gain_of(k)
                        dst, src = xn[:, t, k * P:(k + 1) * P], tr_ps[:, fill % 2, q * P:(q + 1) * P]
                        if bias is None:
                            a = nc.scalar.activation(dst, src, ACT.Copy, scale=scale)
                        else:
                            a = nc.scalar.activation(dst, src, ACT.Identity, bias=bias, scale=scale)
                        if (t, b, q) == (0, 0, 1):
                            a.then_inc(y_half, 1)
                    a.then_inc(tr_read, 1)

            def enter(name, gain_of, before=(), after=(), sub=None):
                norms = [NORM[name]] if name != "ffn0" else [NORM["final1"], NORM["ffn0"]]
                for n in norms:
                    square(n, 0)
                for g in before:
                    ahead(g)
                if sub is not None:
                    act.wait_ge(mod_ready, sub + 1)
                if gain_of is not None:
                    norm_out(name, 0, gain_of)
                for n in norms:
                    square(n, 1)
                if gain_of is not None:
                    norm_out(name, 1, gain_of)
                for g in after:
                    ahead(g)

            def vec(name, k):
                r0 = ROWS[name][0]
                return vecT[:, r0 + k:r0 + k + 1], None

            def load_ada(u, s, i=None, per=0):
                col = plus(i, (u % ADA_UNITS) * UPN, per * UPN)
                if u:
                    act.wait_ge(ada_step, plus(i, 8 * u - 4 + 4 * s, 8 * per))
                act.dma_start(up_view(ada_raw[:, s, :]), up_src(ada_w_2[u // ADA_UNITS], s, col))\
                    .then_inc(ada_landed[s], 16)

            square(0, 0)
            square(0, 1)
            act.wait_ge(tr_read, 1)
            c0 = ROWS["c"][0]
            nc.scalar.activation(cond[:, :], vecT[:, c0:c0 + KT], ACT.Silu).then_inc(cond_ready, 1)
            split_hi(0, 0)
            for t in range(TT):
                norm_out("gate_in", t, lambda k: vec("mix", k))
                split_hi(1 + t, 1 + t)
            g = at["gate_in"].slab
            for c in range(4):
                ahead(g)
                dst = (g_v, g_u)[c // 2]
                for t in range(TT):
                    if t == 0:
                        act.wait_ge(up0_ready, c + 1)
                    else:
                        act.wait_ge(slab_used, g + 2)
                    nc.scalar.activation(dst[:, t, (c % 2) * UPN:(c % 2 + 1) * UPN], up_ps[:, t, :], ACT.Gelu)\
                        .then_inc(gelu_done, 1)
                ahead(g + 1)
                g += 2
            p = at["gate_out"]
            for n in range(NORM_FILLS):
                t, b = divmod(n, KT // FILL)
                hi_part(xT_hi[:, b * FILL:(b + 1) * FILL, t * P:(t + 1) * P], p.tr + n)
            for k in range(2):
                ahead(p.slab + k)

            def mlp(name):
                p = at[name]
                m0 = 0 if name == "mlp0" else MLP_CHUNKS
                unit0 = ADA_AT[name]

                def hidden(c, t, g, i=None, cper=0):
                    if t == 0:
                        act.wait_ge(up0_ready, plus(i, p.up + c + 1, cper))
                    else:
                        act.wait_ge(slab_used, plus(i, g + 2, 4 * cper))
                    nc.scalar.activation(pre[:, t, :], up_ps[:, t, :], ACT.Relu).then_inc(relu_done, 1)
                    act.wait_ge(relu_done, plus(i, 2 * (m0 + c) + t + 1, 2 * cper))
                    nc.scalar.activation(mid[:, t, :], pre[:, t, :], ACT.Square).then_inc(mlp_mid, 1)

                def transposed(c, i=None, cper=0):
                    for t in range(TT):
                        hi_part(hT_hi[:, :, t * P:(t + 1) * P], mid_fill(p, name, c) + t, i, 2 * cper)

                def step(c, g, i=None, cper=0):
                    per = 4 * cper
                    load_ada(unit0 + c, 0, i, cper)
                    ahead(g, i, per)
                    if c > 1:
                        load_ada(unit0 + c, 1, i, cper)
                    for t in range(TT):
                        hidden(c, t, g, i, cper)
                    if c == 1:
                        load_ada(unit0 + c, 1, i, cper)
                    ahead(g + 1, i, per)
                    ahead(g + 2, i, per)
                    transposed(c, i, cper)
                    ahead(g + 3, i, per)

                g = p.slab
                for s in range(2):
                    load_ada(unit0, s)
                hidden(0, 0, g)
                ahead(g)
                hidden(0, 1, g)
                ahead(g + 1)
                transposed(0)
                step(1, g + 2)
                with act.Fori(0, MLP_BODIES) as i:
                    for b in range(MLP_BODY):
                        step(2 + b, g + 6 + 4 * b, i, MLP_BODY)

            last = lambda name: at[name].slab - 1
            enter("mlp0", lambda k: vec("mlp", k), [last("mlp0") - 1], [last("mlp0")])
            mlp("mlp0")

            enter("qkv", lambda k: vec("mix", KT + k), [last("qkv") - 1], [last("qkv")])
            p = at["qkv"]
            stage = [mid, pre, xn]
            with act.Fori(0, 2) as i:
                for b in range(3):
                    g = p.slab + 2 * b
                    ahead(g, i, 6)
                    for t in range(TT):
                        if t == 0:
                            act.wait_ge(up0_ready, i * 3 + (p.up + b + 1))
                        else:
                            act.wait_ge(slab_used, i * 6 + (g + 2))
                        nc.scalar.activation(stage[b][:, t, 0:UPN], up_ps[:, t, :], ACT.Copy).then_inc(qkv_copied, 1)
                    ahead(g + 1, i, 6)
            for b in range(3):
                g = p.slab + 12 + 2 * b
                if b < 2:
                    load_ada(ADA_AT["qkv"] + b, 0)
                ahead(g)
                for t in range(TT):
                    if t == 0:
                        act.wait_ge(up0_ready, p.up + 6 + b + 1)
                    else:
                        act.wait_ge(slab_used, g + 2)
                    act.wait_ge(bias_stored, 16)
                    nc.scalar.activation(v_tok[:, t, b * UPN:(b + 1) * UPN], up_ps[:, t, :], ACT.Copy)\
                        .then_inc(qkv_copied, 1)
                if b < 2:
                    load_ada(ADA_AT["qkv"] + b, 1)
                    ahead(g + 1)

            p = at["attn"]

            def probs(u):
                t = u % 2
                act.wait_ge(max_ready, 2 * (u + 1))
                pt = xn[:, t, 0:NG * P * (t + 1)]
                nc.scalar.activation(pt, pt, ACT.Exp, bias=nmx[:, u:u + 1], accum_out=den[:, u:u + 1])\
                    .then_inc(prob_ready, 1)
                if t == 1 and u // 2 + 2 < HEADS:
                    load_bias(act, u // 2 + 2)

            def copy_probs(u):
                for a in range(1 + u % 2):
                    tr = p.tr + tr_of(u) + a
                    act.wait_ge(tr_ready, tr + 1)
                    if a == 0 and u >= 2:
                        act.wait_ge(pv_ready, u - 1)
                    nc.scalar.activation((mid, pre)[u % 2][:, :, :].rearrange("p t n -> p (t n)")[:, a * 384:(a + 1) * 384],
                                         tr_ps[:, tr % 2, 0:384], ACT.Copy).then_inc(tr_read, 1)

            for u in range(2 * HEADS):
                probs(u)
                if u == 1:
                    ahead(at["attn"].slab - 1)
                if u >= 1:
                    copy_probs(u - 1)
            copy_probs(2 * HEADS - 1)
            p = at["attn_out"]
            for t in range(TT):
                hi_part(hT_hi[:, :, t * P:(t + 1) * P], p.tr + t)
            enter("mlp1", lambda k: vec("mlp", KT + k), [last("mlp1") - 1], [last("mlp1")])
            mlp("mlp1")

            def affine(sub):
                s = sub % 3
                return lambda k: (gain[:, s, k:k + 1], mod[:, s, k:k + 1])

            def ffn(name):
                p = at[name]
                unit0 = ADA_AT.get(name)

                def gates(c, t, g, i=None):
                    if t == 0:
                        act.wait_ge(up0_ready, plus(i, p.up + c + 1))
                    else:
                        act.wait_ge(slab_used, plus(i, g + 2, 3))
                    nc.scalar.activation(pre[:, t, 0:HALF], up_ps[:, t, 0:HALF], ACT.Silu).then_inc(silu_done, 1)

                def transposed(c, i=None, f0=0):
                    for t in range(TT):
                        hi_part(hT_hi[:, f0:f0 + 2, t * P:(t + 1) * P], mid_fill(p, name, c) + t, i, 2)

                def begin(c, g, i=None):
                    unit = None if unit0 is None or c < 2 else unit0 + c - 2
                    if unit is not None:
                        load_ada(unit, 0, i, 1)
                    ahead(g, i, 3)
                    if unit is not None:
                        load_ada(unit, 1, i, 1)
                    for t in range(TT):
                        gates(c, t, g, i)
                    ahead(g + 1, i, 3)

                def step(c, g, i=None):
                    begin(c, g, i)
                    transposed(c, i)
                    ahead(g + 2, i, 3)

                g = p.slab
                gates(0, 0, g)
                ahead(g)
                gates(0, 1, g)
                ahead(g + 1)
                transposed(0)
                step(1, g + 2)
                with act.Fori(0, FFN_CHUNKS - 3) as i:
                    step(2, g + 5, i)
                begin(FFN_CHUNKS - 1, g + 3 * FFN_CHUNKS - 4)
                transposed(FFN_CHUNKS - 1, f0=2)

            enter("ffn0", affine(0), [last("ffn0") - 1], [last("ffn0")], 0)
            ffn("ffn0")
            enter("pool", None, [last("pool") - 1])
            for q in range(POOLS):
                fill = at["pool"].tr + q
                act.wait_ge(tr_ready, fill + 1)
                act.wait_ge(mod_ready, 2)
                for f in range(2):
                    k = 2 * q + f
                    a = nc.scalar.activation(pool_y[:, k, :], tr_ps[:, fill % 2, f * TOKENS:(f + 1) * TOKENS],
                                             ACT.Copy, scale=gain[:, 1, k:k + 1])
                a.then_inc(tr_read, 1)
            ahead(last("pool"))
            enter("ffn1", affine(2), (), [last("ffn1")], 2)
            ffn("ffn1")
            enter("ffn2", affine(3), [last("ffn2") - 1], [last("ffn2")], 3)
            ffn("ffn2")
            enter("conv_in", affine(4), [last("conv_in") - 1], [last("conv_in")], 4)
            p = at["conv_in"]
            g = p.slab
            for c in range(6):
                ahead(g)
                if c // 2 != 1:
                    dst = xn if c < 2 else b_tok
                    for t in range(TT):
                        if t == 0:
                            act.wait_ge(up0_ready, p.up + c + 1)
                        else:
                            act.wait_ge(slab_used, g + 2)
                        nc.scalar.activation(dst[:, t, (c % 2) * UPN:(c % 2 + 1) * UPN], up_ps[:, t, :], ACT.Copy)\
                            .then_inc(conv_copied, 1)
                if c == 4:
                    for k in range(KT):
                        act.wait_ge(tr_ready, at["conv_out"].tr + k + 1)
                        nc.scalar.activation(uT[:, k, CONV_W - 1:], tr_ps[:, (at["conv_out"].tr + k) % 2, 0:TOKENS],
                                             ACT.Copy).then_inc(tr_read, 1)
                if c < 5:
                    ahead(g + 1)
                g += 2
            for k in range(0, KT, 2):
                act.wait_ge(tr_read, at["conv_out"].tr + KT + k + 2)
                nc.scalar.activation(xT_hi[:, k:k + 2, :], conv[:, k:k + 2, :], ACT.Copy).then_inc(conv_hi, 1)
            for k in range(-1, 2):
                ahead(g + k)
            enter("ffn3", affine(5), [last("ffn3") - 1], [last("ffn3")], 5)
            ffn("ffn3")
            enter("final2", None)

        @block.vector
        def _(dve):
            steps = [0]

            def own(ins):
                ins.then_inc(dve_step, 1)
                steps[0] += 1
                dve.wait_ge(dve_step, steps[0])

            def plus(i, k, per=1):
                return k if i is None else i * per + k

            def split_lo(slot, n):
                if isinstance(n, int):
                    if n >= N_SLABS:
                        return
                    dve.wait_ge(hi_ready, n + 1)
                    if n >= RING:
                        dve.wait_ge(slab_used, n - RING + 1)
                else:
                    first, i, per = n
                    dve.wait_ge(hi_ready, i * per + (first + 1))
                    dve.wait_ge(slab_used, i * per + (first - RING + 1))
                nc.vector.tensor_tensor(w_lo[:, slot, :], raw[:, slot, :], w_hi[:, slot, :].bitcast(F32),
                                        ALU.subtract).then_inc(lo_ready, 1)

            def ahead(g, i=None, per=0):
                n = g + RING
                split_lo(n % RING, n if i is None else (n, i, per))

            def lo_part(hi, lo, tr, h, i=None, per=0):
                dve.wait_ge(tr_hi, plus(i, h + 1, per))
                src = tr_ps[:, tr % 2, 0:lo.shape[1] * P].rearrange("p (f n) -> p f n", n=P)
                nc.vector.tensor_tensor(lo, src, hi.bitcast(F32), ALU.subtract).then_inc(tr_read, 1)

            def scale_tokens(n, t):
                dve.wait_ge(rstd_ready[t], n + 1)
                nc.vector.tensor_scalar(xn[:, t, :], res[:, t, :], rstd[:, t:t + 1], None, ALU.mult)\
                    .then_inc(xn_ready, 1)

            def split_tiles(t, k0, k1):
                src = xn[:, t, k0 * P:k1 * P].rearrange("p (k n) -> p k n", n=P)
                hi, lo = xT_hi[:, k0:k1, t * P:(t + 1) * P], xT_lo[:, k0:k1, t * P:(t + 1) * P]
                own(nc.vector.tensor_copy(hi, src))
                nc.vector.tensor_tensor(lo, src, hi.bitcast(F32), ALU.subtract).then_inc(xT_ready, 1)

            def norm_split(name, t):
                for b in range(KT // FILL):
                    k0, k1 = b * FILL, (b + 1) * FILL
                    if (t, b) == (0, 0):
                        dve.wait_ge(y_half, XT[name] + 1)
                        split_tiles(t, 0, FILL // 2)
                        k0 = FILL // 2
                    dve.wait_ge(tr_read, at[name].tr + (KT // FILL) * t + b + 1)
                    split_tiles(t, k0, k1)

            def enter(name, products, before=(), after=(), last_norm=None):
                products(0)
                if last_norm is not None:
                    last_norm(0)
                scale_tokens(NORM[name], 0)
                products(1)
                if name in XT:
                    norm_split(name, 0)
                if last_norm is not None:
                    last_norm(1)
                scale_tokens(NORM[name], 1)
                for g in before:
                    ahead(g)
                if name in XT:
                    norm_split(name, 1)
                for g in after:
                    ahead(g)

            def ada(u, s, i=None, per=0):
                col = plus(i, (u % ADA_UNITS) * UPN, per * UPN)
                dst = ada_acc[:, bass.ds(col, UPN)]
                dve.wait_ge(ada_landed[s], plus(i, 16 * (u + 1), 16 * per))
                for q in range(UPK):
                    k = s * UPK + q
                    src = ada_raw[:, s, q * UPN:(q + 1) * UPN]
                    if k == 0:
                        a = nc.vector.tensor_scalar(dst, src, cond[:, k:k + 1], None, ALU.mult)
                    else:
                        dve.wait_ge(ada_step, plus(i, 8 * u + k, 8 * per))
                        a = nc.vector.scalar_tensor_tensor(out=dst, in0=src, scalar=cond[:, k:k + 1], in1=dst,
                                                           op0=ALU.mult, op1=ALU.add)
                    a.then_inc(ada_step, 1)

            def modulation(name, sub):
                layer, s = divmod(sub, 3)
                fill = mid_fill(at[name], name, 0) + TT + MOD_FILLS * MODS[name].index(sub)
                for q in range(MOD_FILLS):
                    dve.wait_ge(tr_ready, fill + q + 1)
                    nc.vector.tensor_reduce(mod_sum[:, q * FILL:(q + 1) * FILL],
                                            tr_ps[:, (fill + q) % 2, :].rearrange("p (f n) -> p f n", n=P),
                                            AX_X, ALU.add).then_inc(tr_read, 1)
                dve.wait_ge(tr_read, fill + MOD_FILLS)
                b = adabT[:, layer, s * 3 * KT:s * 3 * KT + 2 * KT]
                own(nc.vector.tensor_tensor(mod[:, s, :], mod_sum[:, :], b, ALU.add))
                r0 = ROWS["norm"][0] + KT * sub
                nc.vector.scalar_tensor_tensor(out=gain[:, s, :], in0=mod[:, s, KT:2 * KT], scalar=1.0,
                                               in1=vecT[:, r0:r0 + KT], op0=ALU.add, op1=ALU.mult)\
                    .then_inc(mod_ready, 1)
                dve.wait_ge(mod_ready, sub + 1)

            def residual(g, product, gate=None, sub=None):
                def products(t):
                    if sub is not None and t == 0:
                        dve.wait_ge(gate_ready, sub + 1)
                    if t == 0:
                        dve.wait_ge(acc0_ready, product + 1)
                    else:
                        dve.wait_ge(slab_used, g + 1)
                    src = acc[:, t, :]
                    if gate is not None:
                        own(nc.vector.scalar_tensor_tensor(out=xn[:, t, :], in0=src, scalar=gate,
                                                           in1=gate_B[:, sub % 3, :], op0=ALU.mult, op1=ALU.mult))
                        src = xn[:, t, :]
                    nc.vector.tensor_tensor(res[:, t, :], res[:, t, :], src, ALU.add).then_inc(res_ready[t], 1)
                return products

            last = lambda name: at[name].slab - 1

            for n, dst in ((0, vecT[:, :]), (1, adabT[:, 0, :]), (2, adabT[:, 1, :])):
                dve.wait_ge(tr_ready, n + 1)
                nc.vector.tensor_copy(dst, tr_ps[:, n % 2, 0:dst.shape[1]]).then_inc(tr_read, 1)
            dve.wait_ge(tr_read, 3)
            for t in range(TT):
                scale_tokens(0, t)
            split_lo(0, 0)
            for t in range(TT):
                norm_split("gate_in", t)
                split_lo(1 + t, 1 + t)
            g = at["gate_in"].slab
            for c in range(4):
                ahead(g)
                if c == 1:
                    p = at["positions"]
                    for q in range(GROUPS):
                        dve.wait_ge(tr_ready, p.tr + q + 1)
                        nc.vector.tensor_copy(ws_T[:, q, :], tr_ps[:, (p.tr + q) % 2, 0:P]).then_inc(tr_read, 1)
                    dve.wait_ge(bias_ps_ready, 1)
                    nc.vector.tensor_copy(bias_v[:, 0:D], acc[0:HEADS, 0, :])
                    nc.vector.tensor_copy(bias_v[:, D:NG * VLEN], acc[0:HEADS, 1, 0:NG * VLEN - D])\
                        .then_inc(bias_sb_ready, 1)
                ahead(g + 1)
                if c < 2:
                    for t in range(TT):
                        dve.wait_ge(gelu_done, 2 * c + t + 1)
                        a = nc.vector.bn_stats(out=stats[:, t, c, :], in_=g_v[:, t, c * UPN:(c + 1) * UPN])
                        own(a)
                if c == 1:
                    for t in range(TT):
                        a = nc.vector.bn_aggr(out=mv[:, t, :], in_=stats[:, t, :, :])
                        a.then_inc(var_ready, 1)
                if c == 2:
                    dve.wait_ge(ln_landed, 32)
                    for t in range(TT):
                        dve.wait_ge(ln_rstd, t + 1)
                        own(nc.vector.tensor_scalar(g_v[:, t, :], g_v[:, t, :], mv[:, t, 0:1], rstd[:, t:t + 1],
                                                    ALU.subtract, ALU.mult))
                        own(nc.vector.tensor_tensor(g_v[:, t, :], g_v[:, t, :], ln_g, ALU.mult))
                        nc.vector.tensor_tensor(g_v[:, t, :], g_v[:, t, :], ln_b, ALU.add).then_inc(vn_ready, 1)
                g += 2
            dve.wait_ge(gelu_done, 8)
            b0 = ROWS["bs"][0]
            for t in range(TT):
                dve.wait_ge(mix_ready, t + 1)
                for q in range(GROUPS):
                    cols = slice(q * P, (q + 1) * P)
                    a = nc.vector.scalar_tensor_tensor(out=xn[:, t, cols], in0=acc[:, t, cols],
                                                       scalar=vecT[:, b0 + q:b0 + q + 1], in1=g_u[:, t, cols],
                                                       op0=ALU.add, op1=ALU.mult)
                a.then_inc(gated, 1)
            p = at["gate_out"]
            for n in range(NORM_FILLS):
                t, b = divmod(n, KT // FILL)
                tiles = (slice(None), slice(b * FILL, (b + 1) * FILL), slice(t * P, (t + 1) * P))
                lo_part(xT_hi[tiles], xT_lo[tiles], p.tr + n, p.split + n)
            for k in range(2):
                ahead(p.slab + k)
            dve.wait_ge(cond_ready, 1)

            def mlp(name):
                p = at[name]
                unit0 = ADA_AT[name]
                h0 = p.split

                def transposed(c, i=None, cper=0):
                    for t in range(TT):
                        tiles = (slice(None), slice(None), slice(t * P, (t + 1) * P))
                        lo_part(hT_hi[tiles], hT_lo[tiles], mid_fill(p, name, c) + t, h0 + 2 * c + t, i, 2 * cper)

                g = p.slab
                ahead(g)
                ada(unit0, 0)
                ahead(g + 1)
                transposed(0)
                ada(unit0, 1)

                def step(c, g, i=None, per=0):
                    for s in range(2):
                        ahead(g + s, i, 4 * per)
                        if (c, s) == (1, 0):
                            for sub in MODS.get(name, ()):
                                modulation(name, sub)
                        ada(unit0 + c, s, i, per)
                    ahead(g + 2, i, 4 * per)
                    transposed(c, i, per)
                    ahead(g + 3, i, 4 * per)

                step(1, g + 2)
                with dve.Fori(0, MLP_BODIES) as i:
                    for b in range(MLP_BODY):
                        step(2 + b, g + 6 + 4 * b, i, MLP_BODY)

            enter("mlp0", residual(last("mlp0"), 0), [last("mlp0") - 1], [last("mlp0")])
            mlp("mlp0")

            enter("qkv", residual(last("qkv"), 1), [last("qkv") - 1], [last("qkv")])
            p = at["qkv"]
            tr0 = p.tr + NORM_FILLS
            with dve.Fori(0, 2) as i:
                for b in range(3):
                    g = p.slab + 2 * b
                    ahead(g, i, 6)
                    for c in ((), (0,), (1, 2))[b]:
                        for t in range(TT):
                            tr = tr0 + TT * c + t
                            dve.wait_ge(tr_ready, i * (3 * TT) + (tr + 1))
                            nc.vector.tensor_copy(qkT[:, bass.ds(i * 12 + 4 * c, 4), t * P:(t + 1) * P],
                                                  tr_ps[:, tr % 2, :].rearrange("p (f n) -> p f n", n=P))\
                                .then_inc(tr_read, 1)
                    ahead(g + 1, i, 6)
            for b in range(3):
                g = p.slab + 12 + 2 * b
                ahead(g)
                if b < 2:
                    ada(ADA_AT["qkv"] + b, 0)
                    ahead(g + 1)
                    ada(ADA_AT["qkv"] + b, 1)

            def logits(u):
                h, t = divmod(u, 2)
                nk = P * (t + 1)
                dve.wait_ge(score_ready, u + 1)
                if t == 0:
                    dve.wait_ge(bias_landed[h % 2], 16 * (h // 2 + 1))
                if u >= 2:
                    dve.wait_ge(tr_ready, at["attn"].tr + tr_of(u - 1))
                dst = xn[:, t, 0:NG * nk].rearrange("p (g n) -> p g n", g=NG)
                nc.vector.scalar_tensor_tensor(
                    out=dst, in0=acc[:, t, 0:NG * TOKENS].rearrange("p (g n) -> p g n", g=NG)[:, :, 0:nk],
                    scalar=HD ** -0.5, in1=bias_t[:, h % 2, :, TOKENS - nk:TOKENS], op0=ALU.mult,
                    op1=ALU.add).then_inc(logit_ready, 1)
                dve.wait_ge(logit_ready, u + 1)
                nc.vector.tensor_reduce(mx[:, u:u + 1], xn[:, t, 0:NG * nk], AX_X, ALU.max).then_inc(max_ready, 1)
                dve.wait_ge(max_ready, 2 * u + 1)
                nc.vector.tensor_scalar(nmx[:, u:u + 1], mx[:, u:u + 1], -1.0, None, ALU.mult).then_inc(max_ready, 1)

            def attended(u):
                h, t = divmod(u, 2)
                dve.wait_ge(prob_ready, u + 1)
                own(nc.vector.reciprocal(rden[:, u:u + 1], den[:, u:u + 1]))
                dve.wait_ge(pv_ready, u + 1)
                nc.vector.tensor_scalar(o_tok[:, t, h * HD:(h + 1) * HD], up_ps[:, t, h * HD:(h + 1) * HD],
                                        rden[:, u:u + 1], None, ALU.mult).then_inc(o_ready, 1)

            for u in range(2 * HEADS):
                logits(u)
                if u == 2:
                    ahead(at["attn"].slab - 1)
                if u >= 2:
                    attended(u - 2)
            attended(2 * HEADS - 2)
            attended(2 * HEADS - 1)
            p = at["attn_out"]
            for t in range(TT):
                tiles = (slice(None), slice(None), slice(t * P, (t + 1) * P))
                lo_part(hT_hi[tiles], hT_lo[tiles], p.tr + t, p.split + t)
            enter("mlp1", residual(last("mlp1"), 2), [last("mlp1") - 1], [last("mlp1")])
            mlp("mlp1")

            def final(name, dst, t, ready):
                dve.wait_ge(rstd_ready[t], NORM[name] + 1)
                nc.vector.scalar_tensor_tensor(out=dst[:, t, :], in0=res[:, t, :], scalar=rstd[:, t:t + 1],
                                               in1=gF, op0=ALU.mult, op1=ALU.mult).then_inc(ready, 1)

            def gate(sub):
                s = sub % 3
                half = GATE_HALF[sub]
                dve.wait_ge(gate_ps_ready, sub + 1)
                dve.wait_ge(row_landed, 48 * (sub // 3 + 1))
                a = nc.vector.tensor_tensor(gate_B[:, s, :], acc[:, half, :], gate_B[:, s, :], ALU.add)
                if SUBS[sub] == "pool":
                    own(a)
                    dve.wait_ge(ps_landed, 16)
                    a = nc.vector.tensor_tensor(gate_B[:, s, :], gate_B[:, s, :], ps_B, ALU.mult)
                a.then_inc(gate_ready, 1)

            def ffn(name, sub, carried=None):
                p = at[name]
                f0 = FFN_AT[name] * FFN_CHUNKS
                unit0 = ADA_AT.get(name)
                h0 = p.split

                def gated_mid(c, i=None, tiles=range(TT)):
                    for t in tiles:
                        dve.wait_ge(silu_done, plus(i, 2 * (f0 + c) + t + 1, 2))
                        nc.vector.tensor_tensor(mid[:, t, 0:HALF], pre[:, t, 0:HALF], up_ps[:, t, HALF:UPN],
                                                ALU.mult).then_inc(ffn_mid, 1)

                def transposed(c, i=None, f=0):
                    for t in range(TT):
                        tiles = (slice(None), slice(f, f + 2), slice(t * P, (t + 1) * P))
                        lo_part(hT_hi[tiles], hT_lo[tiles], mid_fill(p, name, c) + t, h0 + 2 * c + t, i, 2)

                def begin(c, g, i=None):
                    if c == 1:
                        for m in MODS.get(name, ())[:1]:
                            modulation(name, m)
                    ahead(g, i, 3)
                    if unit0 is not None and c >= 2:
                        ada(unit0 + c - 2, 0, i, 1)
                    gated_mid(c, i)
                    ahead(g + 1, i, 3)
                    if c == 1:
                        for m in MODS.get(name, ())[1:]:
                            modulation(name, m)

                def rest(c, i=None):
                    if unit0 is not None and c >= 2:
                        ada(unit0 + c - 2, 1, i, 1)

                def step(c, g, i=None):
                    begin(c, g, i)
                    transposed(c, i)
                    rest(c, i)
                    ahead(g + 2, i, 3)

                g = p.slab
                gated_mid(0, tiles=[0])
                ahead(g)
                gated_mid(0, tiles=[1])
                ahead(g + 1)
                transposed(0)
                for m in GATES[name]:
                    gate(m)
                if carried is not None:
                    carried()
                step(1, g + 2)
                with dve.Fori(0, FFN_CHUNKS - 3) as i:
                    step(2, g + 5, i)
                begin(FFN_CHUNKS - 1, g + 3 * FFN_CHUNKS - 4)
                transposed(FFN_CHUNKS - 1, f=2)
                return lambda: rest(FFN_CHUNKS - 1)

            def block_norm(t):
                dve.wait_ge(gF_landed, 16)
                final("final1", res, t, res_ready[t])

            enter("ffn0", residual(last("ffn0"), 3), [last("ffn0") - 1], [last("ffn0")], block_norm)
            rest = ffn("ffn0", 0)


            enter("pool", residual(last("pool"), 4, 0.5, 0), [last("pool") - 1])
            dve.wait_ge(sums_ready, 1)
            for q in range(POOLS):
                dve.wait_ge(tr_read, at["pool"].tr + q + 1)
                k = slice(2 * q, 2 * q + 2)
                for f in range(2):
                    n = 2 * q + f
                    y = pool_y[:, n, :]
                    a = nc.vector.scalar_tensor_tensor(out=y, in0=up_ps[:, q // 2, (q % 2) * TOKENS:(q % 2 + 1) * TOKENS],
                                                       scalar=mod[:, 1, n:n + 1], in1=y, op0=ALU.mult, op1=ALU.add)
                own(a)
                own(nc.vector.tensor_copy(xT_hi[:, k, :], pool_y[:, k, :]))
                nc.vector.tensor_tensor(xT_lo[:, k, :], pool_y[:, k, :], xT_hi[:, k, :].bitcast(F32), ALU.subtract)\
                    .then_inc(pool_lo, 1)
            ahead(last("pool"))
            enter("ffn1", residual(last("ffn1"), 5, 1.0, 1), (), [last("ffn1")])
            rest = ffn("ffn1", 2, rest)
            enter("ffn2", residual(last("ffn2"), 6, 0.5, 2), [last("ffn2") - 1], [last("ffn2")])
            ffn("ffn2", 3, rest)
            enter("conv_in", residual(last("conv_in"), 7, 0.5, 3), [last("conv_in") - 1], [last("conv_in")])
            p = at["conv_in"]
            own(nc.vector.memset(uT[:, :, 0:CONV_W - 1], 0.0))
            g = p.slab
            q = at["conv_out"]
            for c in range(6):
                ahead(g)
                if c // 2 == 1:
                    for t in range(TT):
                        cols = slice((c % 2) * UPN, (c % 2 + 1) * UPN)
                        dve.wait_ge(conv_copied, 4)
                        if t == 0:
                            dve.wait_ge(up0_ready, p.up + c + 1)
                        else:
                            dve.wait_ge(slab_used, g + 2)
                        nc.vector.tensor_tensor(xn[:, t, cols], xn[:, t, cols], up_ps[:, t, :], ALU.mult)\
                            .then_inc(u_ready, 1)
                if c == 4:
                    w0 = ROWS["convw"][0]
                    for j in reversed(range(CONV_W)):
                        for k in range(KT):
                            tap = vecT[:, w0 + KT * j + k:w0 + KT * j + k + 1]
                            if j == CONV_W - 1:
                                dve.wait_ge(tr_read, q.tr + k + 1)
                                a = nc.vector.tensor_scalar(conv[:, k, :], uT[:, k, j:j + TOKENS], tap, None, ALU.mult)
                            else:
                                dve.wait_ge(conv_step, KT * (CONV_W - 2 - j) + k + 1)
                                a = nc.vector.scalar_tensor_tensor(out=conv[:, k, :], in0=uT[:, k, j:j + TOKENS],
                                                                   scalar=tap, in1=conv[:, k, :], op0=ALU.mult,
                                                                   op1=ALU.add)
                            a.then_inc(conv_step, 1)
                if c < 5:
                    ahead(g + 1)
                g += 2
            dve.wait_ge(conv_step, CONV_W * KT)

            def conv_split(k):
                dve.wait_ge(conv_hi, k // 2 + 1)
                nc.vector.tensor_tensor(xT_lo[:, k:k + 2, :], conv[:, k:k + 2, :], xT_hi[:, k:k + 2, :].bitcast(F32),
                                        ALU.subtract).then_inc(conv_lo, 1)

            for k in range(KT):
                tr = q.tr + KT + k
                dve.wait_ge(tr_ready, tr + 1)
                nc.vector.tensor_tensor(conv[:, k, :], conv[:, k, :], tr_ps[:, tr % 2, 0:TOKENS], ALU.mult)\
                    .then_inc(tr_read, 1)
                if k % 2 and k > 1:
                    conv_split(k - 3)
            conv_split(KT - 2)
            for k in range(-1, 2):
                ahead(g + k)
            enter("ffn3", residual(last("ffn3"), 8, 1.0, 4), [last("ffn3") - 1], [last("ffn3")])
            ffn("ffn3", 5)
            dve.wait_ge(gF_landed, 32)
            products = residual(last("final2"), 9, 0.5, 5)
            for t in range(TT):
                products(t)
            for t in range(TT):
                final("final2", xn, t, xn_ready)

        @block.tensor
        def _(pe):
            def plus(i, k, per=1):
                return k if i is None else i * per + k

            def mm(dst, a, b, start=False, stop=False):
                return nc.tensor.matmul(dst, a, b, start=start, stop=stop, skip_group_check=True)

            def up_tile(g, s, t, half=None):
                slot = g % RING
                a = slice(t * P, (t + 1) * P)
                for q in range(UPK):
                    if half is not None and q == FILL // 2:
                        pe.wait_ge(xT_ready, half)
                    k = s * UPK + q
                    b = slice(q * UPN, (q + 1) * UPN)
                    mm(up_ps[:, t, :], xT_hi[:, k, a], w_hi[:, slot, b], start=(k == 0))
                    mm(up_ps[:, t, :], xT_hi[:, k, a], w_lo[:, slot, b])
                    last = mm(up_ps[:, t, :], xT_lo[:, k, a], w_hi[:, slot, b], stop=(k == KT - 1))
                return last

            def up_chunk(g, i=None, per=0, free=None, between=None):
                for s in range(2):
                    pe.wait_ge(lo_ready, plus(i, g + s + 1, per))
                    for t in range(TT):
                        if s == 0 and free is not None:
                            pe.wait_ge(free[0], plus(i, free[1] + t, free[2]))
                        last = up_tile(g + s, s, t)
                        if (s, t) == (1, 0):
                            last.then_inc(up0_ready, 1)
                        if between is not None:
                            between(s, t)
                    last.then_inc(slab_used, 1)

            def down_tile(g, t, hi, lo, k0, start, stop, qs=range(DOWNK)):
                slot = g % RING
                a = slice(t * P, (t + 1) * P)
                for q in qs:
                    for x_part, w_part in ((hi, w_hi), (hi, w_lo), (lo, w_hi)):
                        for c in range(2):
                            last = mm(acc[:, t, c * 512:(c + 1) * 512], x_part[:, k0 + q, a],
                                      w_part[:, slot, q * D + c * 512:q * D + (c + 1) * 512],
                                      start=start and q == 0 and x_part is hi and w_part is w_hi,
                                      stop=stop and q == DOWNK - 1 and x_part is lo)
                return last

            def down_slab(g, hi, lo, k0, start, i=None, per=0, ready=None):
                pe.wait_ge(lo_ready, plus(i, g + 1, per))
                for t in range(TT):
                    if ready is not None:
                        pe.wait_ge(tr_read, plus(i, ready[0] + (t + 1) * ready[1], ready[2]))
                    last = down_tile(g, t, hi, lo, k0, start, False)
                last.then_inc(slab_used, 1)

            def down_last(g, hi, lo, k0, start, ready=None):
                for t in range(TT):
                    if ready is not None:
                        pe.wait_ge(tr_read, ready[0] + (t + 1) * ready[1])
                    for s in range(2):
                        if t == 0:
                            pe.wait_ge(lo_ready, g + s + 1)
                        last = down_tile(g + s, t, hi, lo, k0 + 2 * s, start and s == 0, s == 1)
                        if t == 1:
                            last.then_inc(slab_used, 1)
                    if t == 0:
                        last.then_inc(acc0_ready, 1)

            def bank(tr, i=None, per=0):
                if tr >= 2:
                    pe.wait_ge(tr_read, plus(i, tr - 1, per))
                return tr_ps[:, tr % 2, :]

            def turn(src, t, f0, n, tr, i=None, per=0, order=ident):
                dst = bank(tr, i, per)
                for q in range(n):
                    tile = src[:, t, (f0 + q) * P:(f0 + q + 1) * P]
                    if order is ident:
                        last = nc.tensor.transpose(dst[:, q * P:(q + 1) * P], tile, ident)
                    else:
                        last = mm(dst[:, q * P:(q + 1) * P], tile, order, start=True, stop=True)
                last.then_inc(tr_ready, 1)

            def turn_tokens(src, f, tr, i=None, per=0, order=None):
                dst = bank(tr, i, per)
                for t in range(TT):
                    tile = src[:, t, f * P:(f + 1) * P]
                    if order is None:
                        last = nc.tensor.transpose(dst[:, t * P:(t + 1) * P], tile, ident)
                    else:
                        last = mm(dst[:, t * P:(t + 1) * P], tile, order, start=True, stop=True)
                last.then_inc(tr_ready, 1)

            def turn_norm(name, t):
                pe.wait_ge(xn_ready, 2 * XN[name] + t + 1)
                if t == 0:
                    pe.wait_ge(tr_read, at[name].tr)
                for b in range(KT // FILL):
                    turn(xn, t, b * FILL, FILL, at[name].tr + (KT // FILL) * t + b)

            def first_chunk(name):
                g = at[name].slab
                x0 = (NORM_FILLS + 1) * XT[name]
                turn_norm(name, 0)
                for t in range(TT):
                    for s in range(2):
                        if t == 0:
                            pe.wait_ge(lo_ready, g + s + 1)
                        first = (t, s) == (0, 0)
                        pe.wait_ge(xT_ready, x0 + 2 * t + s + (1 if first else 2))
                        last = up_tile(g + s, s, t, x0 + 2 if first else None)
                        if t == 1:
                            last.then_inc(slab_used, 1)
                        elif s == 0:
                            turn_norm(name, 1)
                        else:
                            last.then_inc(up0_ready, 1)

            pe.wait_ge(consts_ready, 6)
            pe.wait_ge(small_landed, 16 * (len(ROWS) + 1))
            for n, src in ((0, rows), (1, rows_b[:, 0, :]), (2, rows_b[:, 1, :])):
                if n >= 2:
                    pe.wait_ge(tr_read, n - 1)
                w = src.shape[0]
                nc.tensor.transpose(tr_ps[:, n % 2, 0:w], src, ident[0:w, 0:w]).then_inc(tr_ready, 1)
            g = at["gate_in"].slab
            first_chunk("gate_in")
            for c in range(1, 4):
                up_chunk(g + 2 * c, free=(gelu_done, 2 * (c - 1) + 1, 0))
                if c == 1:
                    p = at["positions"]
                    pe.wait_ge(ws_masked, 1)
                    pe.wait_ge(tr_read, p.tr)
                    for q in range(GROUPS):
                        nc.tensor.transpose(bank(p.tr + q)[:, 0:P], ws_raw[:, q, :], ident).then_inc(tr_ready, 1)
                    pe.wait_ge(mask_landed, 32)
                    for n in range(NG):
                        c0 = n * VLEN
                        while c0 < (n + 1) * VLEN:
                            c1 = min((n + 1) * VLEN, (c0 // 512 + 1) * 512)
                            last = mm(acc[0:HEADS, c0 // D, c0 % D:c0 % D + c1 - c0], rel[:, n * HEADS:(n + 1) * HEADS],
                                      mask_sb[:, n, c0 - n * VLEN:c1 - n * VLEN], start=True, stop=True)
                            c0 = c1
                    last.then_inc(bias_ps_ready, 1)
            pe.wait_ge(bias_sb_ready, 1)
            for t in range(TT):
                pe.wait_ge(vn_ready, t + 1)
                for q in range(GROUPS):
                    last = mm(acc[:, t, q * P:(q + 1) * P], ws_T[:, q, :], g_v[:, t, q * P:(q + 1) * P],
                              start=True, stop=True)
                last.then_inc(mix_ready, 1)
            p = at["gate_out"]
            for n in range(NORM_FILLS):
                t, b = divmod(n, KT // FILL)
                pe.wait_ge(gated, t + 1)
                turn(xn, t, b * FILL, FILL, p.tr + n)
            for k in range(2):
                down_slab(p.slab + k, xT_hi, xT_lo, 2 * k, k == 0, ready=(p.tr, 2, 0))
            down_last(p.slab + 2, xT_hi, xT_lo, 4, False, (p.tr, 2))

            def modulation(name, sub, half):
                fill = mid_fill(at[name], name, 0) + TT + MOD_FILLS * MODS[name].index(sub)
                pe.wait_ge(ada_step, 8 * ((sub // 3) * ADA_UNITS + 6 * (sub % 3) + 4))
                for q in range(half * MOD_FILLS // 2, (half + 1) * MOD_FILLS // 2):
                    dst = bank(fill + q)
                    for f in range(FILL):
                        n = (sub % 3) * 3 * KT + q * FILL + f
                        last = nc.tensor.transpose(dst[:, f * P:(f + 1) * P], ada_acc[:, n * P:(n + 1) * P], ident)
                    last.then_inc(tr_ready, 1)

            def mlp(name):
                p = at[name]
                m0 = 0 if name == "mlp0" else MLP_CHUNKS
                g = p.slab

                def turn_mid(c, i=None, cper=0):
                    for t in range(TT):
                        pe.wait_ge(mlp_mid, plus(i, 2 * (m0 + c) + t + 1, 2 * cper))
                        turn(mid, t, 0, 4, mid_fill(p, name, c) + t, i, 2 * cper)

                def step(c, start, i=None, cper=0, between=None):
                    gb = g + 4 * c - 2
                    up_chunk(gb, i, 4 * cper, (relu_done, 2 * (m0 + c - 1) + 1, 2 * cper), between)
                    for s in range(2):
                        down_slab(gb + 2 + s, hT_hi, hT_lo, 2 * s, start and s == 0, i, 4 * cper,
                                  (mid_fill(p, name, c - 1), 1, 2 * cper))
                    turn_mid(c, i, cper)

                first_chunk(name)

                def between(s, t):
                    if (s, t) == (0, 0):
                        turn_mid(0)
                    elif s == 1:
                        for sub in MODS.get(name, ()):
                            modulation(name, sub, t)

                step(1, True, between=between)
                with pe.Fori(0, MLP_BODIES) as i:
                    for b in range(MLP_BODY):
                        step(2 + b, False, i, MLP_BODY)
                down_last(g + 4 * MLP_CHUNKS - 2, hT_hi, hT_lo, 0, False, (mid_fill(p, name, MLP_CHUNKS - 1), 1))

            mlp("mlp0")

            p = at["qkv"]
            stage = [mid, pre, xn]
            tr0 = p.tr + NORM_FILLS

            def qk_turn(n, i):
                pe.wait_ge(qkv_copied, 2 * n + 2 + 6 * i)
                for t in range(TT):
                    turn(stage[n], t, 0, 4, tr0 + TT * (n + 3 * i) + t, order=flip[:, i, :])

            for i in range(2):
                for b in range(3):
                    c = 3 * i + b
                    if c == 0:
                        first_chunk("qkv")
                    else:
                        up_chunk(p.slab + 2 * c, free=(qkv_copied, 2 * (c - 1) + 1, 0))
                    if b:
                        qk_turn(b - 1, i)
                qk_turn(2, i)
            for b in range(3):
                up_chunk(p.slab + 12 + 2 * b, free=(qkv_copied, 2 * (6 + b - 1) + 1, 0))

            p = at["attn"]
            pe.wait_ge(tr_read, p.tr)
            pe.wait_ge(qkv_copied, 18)

            def scores(u):
                h, t = divmod(u, 2)
                rows_h = slice((h % 2) * HD, (h % 2 + 1) * HD)
                if u >= 2:
                    pe.wait_ge(logit_ready, u - 1)
                for n in range(NG):
                    last = mm(acc[:, t, n * TOKENS:n * TOKENS + P * (t + 1)],
                              qkT[rows_h, 4 * n + h // 2, t * P:(t + 1) * P],
                              qkT[rows_h, 12 + 4 * n + h // 2, 0:P * (t + 1)], start=True, stop=True)
                last.then_inc(score_ready, 1)

            def turn_probs(u):
                t = u % 2
                pe.wait_ge(prob_ready, u + 1)
                for a in range(1 + t):
                    tr = p.tr + tr_of(u) + a
                    pe.wait_ge(tr_read, tr - 1)
                    for q in range(3):
                        m = 3 * a + q
                        last = nc.tensor.transpose(tr_ps[:, tr % 2, q * P:(q + 1) * P],
                                                   xn[:, t, m * P:(m + 1) * P], ident)
                    last.then_inc(tr_ready, 1)

            def attend(u):
                h, t = divmod(u, 2)
                pe.wait_ge(tr_read, p.tr + tr_of(u + 1))
                if u >= 2:
                    pe.wait_ge(o_ready, u - 1)
                blocks = [(n, k) for n in range(NG) for k in range(t + 1)]
                src = (mid, pre)[u % 2][:, :, :].rearrange("p t n -> p (t n)")
                for m, (n, k) in enumerate(blocks):
                    last = mm(up_ps[:, t, h * HD:(h + 1) * HD], src[:, m * P:(m + 1) * P],
                              v_tok[:, k, n * UPN + h * HD:n * UPN + (h + 1) * HD],
                              start=(m == 0), stop=(m == len(blocks) - 1))
                last.then_inc(pv_ready, 1)

            scores(0)
            scores(1)
            turn_probs(0)
            for u in range(2 * HEADS):
                if u + 2 < 2 * HEADS:
                    scores(u + 2)
                if u + 1 < 2 * HEADS:
                    turn_probs(u + 1)
                attend(u)
            p = at["attn_out"]
            pe.wait_ge(o_ready, 2 * HEADS)
            for t in range(TT):
                turn(o_tok, t, 0, 4, p.tr + t, order=flip[:, 0, :])
            down_last(p.slab, hT_hi, hT_lo, 0, True, (p.tr, 1))

            mlp("mlp1")

            def gate(sub):
                s = sub % 3
                pe.wait_ge(ada_step, 8 * ((sub // 3) * ADA_UNITS + 6 * s + 6))
                for c in range(2):
                    n = (3 * s + 2) * D + c * 512
                    last = mm(acc[:, GATE_HALF[sub], c * 512:(c + 1) * 512], ones[:, :], ada_acc[:, n:n + 512],
                              start=True, stop=True)
                last.then_inc(gate_ps_ready, 1)

            def ffn(name, sub):
                p = at[name]
                f0 = FFN_AT[name] * FFN_CHUNKS
                g = p.slab
                mods = MODS.get(name, ())

                def turn_mid(c, i=None):
                    for t in range(TT):
                        pe.wait_ge(ffn_mid, plus(i, 2 * (f0 + c) + t + 1, 2))
                        turn(mid, t, 0, 2, mid_fill(p, name, c) + t, i, 2)

                def step(c, start, i=None, between=None):
                    gb = g + 3 * c - 1
                    up_chunk(gb, i, 3, (ffn_mid, 2 * (f0 + c - 1) + 1, 2), between)
                    if start:
                        pe.wait_ge(gate_ready, GATES[name][-1] + 1)
                        for m in mods[1:]:
                            modulation(name, m, 0)
                    down_slab(gb + 2, hT_hi, hT_lo, 0, start, i, 3, (mid_fill(p, name, c - 1), 1, 2))
                    if start:
                        for m in mods[1:]:
                            modulation(name, m, 1)
                    turn_mid(c, i)

                def between(s, t):
                    if (s, t) == (0, 0):
                        for m in GATES[name]:
                            gate(m)
                        turn_mid(0)
                    elif t != s:
                        for m in mods[:1]:
                            modulation(name, m, s)

                first_chunk(name)
                step(1, True, between=between)
                with pe.Fori(0, FFN_CHUNKS - 3) as i:
                    step(2, False, i)
                c = FFN_CHUNKS - 1
                gb = g + 3 * c - 1
                up_chunk(gb, free=(ffn_mid, 2 * (f0 + c - 1) + 1, 0))
                ready = mid_fill(p, name, c - 1)
                pe.wait_ge(lo_ready, gb + 3)
                pe.wait_ge(tr_read, ready + 2)
                down_tile(gb + 2, 0, hT_hi, hT_lo, 0, False, False)
                turn_mid(c)
                down_tile(gb + 2, 1, hT_hi, hT_lo, 0, False, False, [0])
                pe.wait_ge(lo_ready, gb + 4)
                pe.wait_ge(tr_read, ready + 3)
                down_tile(gb + 3, 0, hT_hi, hT_lo, 2, False, True).then_inc(acc0_ready, 1)
                down_tile(gb + 2, 1, hT_hi, hT_lo, 0, False, False, [1]).then_inc(slab_used, 1)
                pe.wait_ge(tr_read, ready + 4)
                down_tile(gb + 3, 1, hT_hi, hT_lo, 2, False, True).then_inc(slab_used, 1)

            ffn("ffn0", 0)
            p = at["pool"]
            pe.wait_ge(pool_landed, 16)
            for q in range(POOLS):
                dst = up_ps[:, q // 2, (q % 2) * TOKENS:(q % 2 + 1) * TOKENS]
                mm(dst[:, 0:P], ones[:, :], pool_w[:, q, 0:P], start=True, stop=True)
                mm(dst[:, P:TOKENS], ones[:, :], pool_w[:, q, P:TOKENS], start=True)
                last = mm(dst[:, P:TOKENS], ones[:, :], pool_w[:, q, TOKENS:], stop=True)
            last.then_inc(sums_ready, 1)
            pe.wait_ge(xn_ready, 2 * XN["pool"] + 2)
            for q in range(POOLS):
                dst = bank(p.tr + q)
                for f in range(2):
                    tiles = [xn[:, t, (2 * q + f) * P:(2 * q + f + 1) * P] for t in range(TT)]
                    c0 = f * TOKENS
                    mm(dst[:, c0:c0 + P], tiles[0], pool_w[:, q, 0:P], start=True, stop=True)
                    mm(dst[:, c0 + P:c0 + TOKENS], tiles[0], pool_w[:, q, P:TOKENS], start=True)
                    last = mm(dst[:, c0 + P:c0 + TOKENS], tiles[1], pool_w[:, q, TOKENS:], stop=True)
                last.then_inc(tr_ready, 1)
            pe.wait_ge(lo_ready, p.slab + 1)
            slot = p.slab % RING
            for t in range(TT):
                for q in range(POOLS):
                    pe.wait_ge(pool_lo, q + 1)
                    for kk in range(2):
                        k = 2 * q + kk
                        for n, (x_part, w_part) in enumerate(((xT_hi, w_hi), (xT_hi, w_lo), (xT_lo, w_hi))):
                            last = mm(acc[:, t, q * 256:(q + 1) * 256], x_part[:, k, t * P:(t + 1) * P],
                                      w_part[:, slot, k * 256:(k + 1) * 256], start=(kk == 0 and n == 0),
                                      stop=(kk == 1 and n == 2))
                if t == 0:
                    last.then_inc(acc0_ready, 1)
            last.then_inc(slab_used, 1)
            ffn("ffn1", 2)
            ffn("ffn2", 3)

            p = at["conv_in"]
            q = at["conv_out"]
            g = p.slab
            free = [None, (conv_copied, 1, 0), (conv_copied, 3, 0), (u_ready, 1, 0), (u_ready, 3, 0), (conv_copied, 5, 0)]
            for c in range(6):
                if c == 0:
                    first_chunk("conv_in")
                else:
                    up_chunk(g, free=free[c])
                g += 2
                if c == 4:
                    for k in range(KT):
                        turn_tokens(xn, k, q.tr + k)
            pe.wait_ge(conv_copied, 8)
            pe.wait_ge(tr_read, q.tr + KT)
            for k in range(KT):
                turn_tokens(b_tok, k, q.tr + KT + k)
            for k in range(2):
                pe.wait_ge(conv_lo, k + 1)
                down_slab(g + k, xT_hi, xT_lo, 2 * k, k == 0)
            pe.wait_ge(conv_lo, 4)
            down_last(g + 2, xT_hi, xT_lo, 4, False)
            ffn("ffn3", 5)


_INS = ["x", "mix_norm_g", "mlp_norm_g", "final_norm_g", "a_w_in", "a_ln_g", "a_ln_b", "a_w_s", "a_b_s", "a_w_out",
        "b_w_qkv", "b_w_out", "rel_bias", "w_up", "w_down", "c_2", "ada_w_2", "ada_b_2", "norm_g_2", "ffn_w_in_2",
        "ffn_w_out_2", "pool_w_2", "pool_scale_2", "conv_w_in_2", "conv_w_2", "conv_w_out_2", "final_g_2"]


def kernel(**inputs):
    import concourse.bacc as bacc
    from concourse.bass_utils import run_bass_kernel_spmd

    nc = bacc.Bacc("TRN2", target_bir_lowering=False, num_devices=1, dynamic_dma_scratch_size=64)
    arrays, args = {}, []
    for name in _INS:
        a = np.ascontiguousarray(inputs[name])
        arrays[f"in_{name}"] = a
        args.append(nc.dram_tensor(f"in_{name}", a.shape, mybir.dt.from_np(a.dtype), kind="ExternalInput").ap())
    masks = nc.inline_tensor(bucket_masks(), "bucket_masks").ap()
    bias_rows = nc.dram_tensor("bias_rows", (HEADS * NG * VLEN,), F32).ap()
    out = nc.dram_tensor("out", (1, TOKENS, D), F32, kind="ExternalOutput").ap()
    means = nc.inline_tensor(pool_weights(), "pool_weights").ap()
    build(nc, *args, masks, means, bias_rows, out)
    r = run_bass_kernel_spmd(nc, [arrays], core_ids=[0])
    return r.results[0]["out"]
```
